# Optimizing a Trainium2 kernel written in Bass

```python
import math
import jax
import jax.numpy as jnp
from jax import lax
import numpy as np
import jax, jax.numpy as jnp

D_MODEL = 1024
BATCH = 1
SEQ = 256
DEPTH = 2

CTX_LEN = 256
GRID_W = 64
NORM_EPS = 1e-6

HY_WIDTH = 1024
HY_SHORT = 3
HY_EMB = 33
HY_BANDS = (HY_EMB - 1) // 2
HY_HIDDEN = 64
HY_TARGET = 1e-2
HY_SHORT_DECAY_PCT = 0.3
HY_LONG_DECAY_PCT = 1.5

ATT_HEADS = 8
ATT_KV_HEADS = 2
HEAD_DIM = 128
ATT_WIDTH = ATT_HEADS * HEAD_DIM
Q_BLOCK = 128
ROPE_THETA = 10000.0

EVEN_MIX = HY_WIDTH + ATT_WIDTH
EVEN_SPLITS = (3 * HY_WIDTH, HY_WIDTH, ATT_WIDTH, ATT_KV_HEADS * HEAD_DIM, ATT_KV_HEADS * HEAD_DIM, ATT_WIDTH)
EVEN_IN = sum(EVEN_SPLITS)

ML_HEADS = 8
ML_QK = 128
ML_V = 256
ML_WIDTH = ML_HEADS * ML_V
ML_CHUNK = 64
ML_SHORT = 3
ODD_SPLITS = (ML_HEADS * ML_QK, ML_HEADS * ML_QK, ML_WIDTH, ML_WIDTH, ML_WIDTH, 4 * ML_HEADS)
ODD_IN = sum(ODD_SPLITS)

N_EVEN = (DEPTH + 1) // 2
N_ODD = DEPTH // 2


def _split(a, sizes):
    out, start = [], 0
    for s in sizes:
        out.append(a[..., start:start + s])
        start += s
    return out

def rms_norm(x, g):
    xf = x.astype(jnp.float32)
    y = xf * lax.rsqrt(jnp.mean(xf * xf, axis=-1, keepdims=True) + NORM_EPS)
    return (y * g.astype(jnp.float32)).astype(x.dtype)

def dw_conv(u, w, b):
    ch = u.shape[-1]
    k = w.shape[0]
    y = lax.conv_general_dilated(u, w[:, None, :].astype(u.dtype), window_strides=(1,),
                                 padding=[(k // 2, k // 2)], dimension_numbers=('NWC', 'WIO', 'NWC'),
                                 feature_group_count=ch)
    return y + b.astype(u.dtype)

def adaln(cond, w_mod, b_mod):
    m = jax.nn.silu(cond) @ w_mod + b_mod
    return _split(m, (D_MODEL, D_MODEL, D_MODEL))

def axial_rope(x, rows, cols):
    f32 = jnp.float32
    half = x.shape[-1] // 2
    nf = half // 2
    inv = ROPE_THETA ** (-jnp.arange(nf, dtype=f32) / nf)

    def rot(xa, pos):
        ang = pos.astype(f32)[:, None] * inv
        cos = jnp.cos(ang)[None, :, None, :]
        sin = jnp.sin(ang)[None, :, None, :]
        x1 = xa[..., :nf].astype(f32)
        x2 = xa[..., nf:].astype(f32)
        return jnp.concatenate([x1 * cos - x2 * sin, x1 * sin + x2 * cos], axis=-1)

    out = jnp.concatenate([rot(x[..., :half], rows), rot(x[..., half:], cols)], axis=-1)
    return out.astype(x.dtype)

def hyena_filter(n, w1, b1, freq, w2, b2, w3):
    f32 = jnp.float32
    t = jnp.linspace(0.0, 1.0, n, dtype=f32)[:, None]
    bands = jnp.linspace(1e-4, HY_BANDS - 1, HY_BANDS, dtype=f32)
    ang = (2.0 * math.pi / n) * jnp.arange(n, dtype=f32)[:, None] * bands
    z = jnp.concatenate([t, jnp.cos(ang), -jnp.sin(ang)], axis=-1)
    fr = freq.astype(f32)
    hdn = jnp.sin(fr * (z @ w1.astype(f32) + b1.astype(f32)))
    hdn = jnp.sin(fr * (hdn @ w2.astype(f32) + b2.astype(f32)))
    h = (hdn @ w3.astype(f32)).reshape(n, 2, HY_WIDTH)
    max_decay = math.log(HY_TARGET) / HY_SHORT_DECAY_PCT
    min_decay = math.log(HY_TARGET) / HY_LONG_DECAY_PCT
    deltas = jnp.linspace(min_decay, max_decay, HY_WIDTH, dtype=f32)
    h = h * jnp.exp(-t * jnp.abs(deltas))[:, None, :]
    two_sided = jnp.concatenate([h[:, 0], jnp.zeros((1, HY_WIDTH), f32), h[:0:-1, 1]], axis=0)
    return two_sided / jnp.sum(jnp.abs(two_sided), axis=0, keepdims=True)

def bidir_long_conv(u, filt):
    n = u.shape[1]
    uf = jnp.fft.rfft(u.astype(jnp.float32), n=2 * n, axis=1)
    ff = jnp.fft.rfft(filt, axis=0)
    return jnp.fft.irfft(uf * ff[None], n=2 * n, axis=1)[:, :n].astype(u.dtype)

def hyena_mixer(xv, conv_w, conv_b, f_w1, f_b1, f_freq, f_w2, f_b2, f_w3, hy_bias):
    n = xv.shape[1]
    x0, x1, v = _split(dw_conv(xv, conv_w, conv_b), (HY_WIDTH, HY_WIDTH, HY_WIDTH))
    filt = hyena_filter(n, f_w1, f_b1, f_freq, f_w2, f_b2, f_w3)
    g = v * x1
    return x0 * (bidir_long_conv(g, filt) + g * hy_bias.astype(g.dtype))

def block_attention(q, k, v):
    B, n, H, Dh = q.shape
    kvh = k.shape[2]
    grp = H // kvh
    nb = n // Q_BLOCK
    qb = jnp.moveaxis(q.reshape(B, nb, Q_BLOCK, kvh, grp, Dh), 1, 0)
    scale = Dh ** -0.5

    def attend(qblk):
        s = jnp.einsum('bqkgd,btkd->bkgqt', qblk, k, preferred_element_type=jnp.float32) * scale
        p = jax.nn.softmax(s, axis=-1).astype(v.dtype)
        return jnp.einsum('bkgqt,btkd->bqkgd', p, v)

    out = lax.map(attend, qb)
    return jnp.moveaxis(out, 0, 1).reshape(B, n, H * Dh)

def even_mixer(h_lat, h_ctx, rows, cols, need_ctx, w_in, conv_w, conv_b, f_w1, f_b1, f_freq,
               f_w2, f_b2, f_w3, hy_bias, q_norm, k_norm, w_out):
    def project(h):
        B, n = h.shape[:2]
        xv, g_hy, q, k, v, g_att = _split(h @ w_in, EVEN_SPLITS)
        q = rms_norm(q.reshape(B, n, ATT_HEADS, HEAD_DIM), q_norm)
        k = rms_norm(k.reshape(B, n, ATT_KV_HEADS, HEAD_DIM), k_norm)
        v = v.reshape(B, n, ATT_KV_HEADS, HEAD_DIM)
        return xv, g_hy, q, k, v, g_att

    def hyena(xv):
        return hyena_mixer(xv, conv_w, conv_b, f_w1, f_b1, f_freq, f_w2, f_b2, f_w3, hy_bias)

    def combine(hy, att, g_hy, g_att):
        return jnp.concatenate([hy * jax.nn.silu(g_hy), att * jax.nn.silu(g_att)], axis=-1) @ w_out

    xv_l, gh_l, q_l, k_l, v_l, ga_l = project(h_lat)
    xv_c, gh_c, q_c, k_c, v_c, ga_c = project(h_ctx)
    q_l = axial_rope(q_l, rows, cols)
    k_l = axial_rope(k_l, rows, cols)
    att_l = block_attention(q_l, jnp.concatenate([k_l, k_c], axis=1), jnp.concatenate([v_l, v_c], axis=1))
    y_lat = combine(hyena(xv_l), att_l, gh_l, ga_l)
    y_ctx = None
    if need_ctx:
        y_ctx = combine(hyena(xv_c), block_attention(q_c, k_c, v_c), gh_c, ga_c)
    return y_lat, y_ctx

def mlstm_chunkwise(q, k, v, i_pre, f_pre, state):
    f32 = jnp.float32
    B, H, n, _ = q.shape
    nc = n // ML_CHUNK

    def chunks(a):
        a = a.astype(f32)
        return jnp.moveaxis(a.reshape(B, H, nc, ML_CHUNK, *a.shape[3:]), 2, 0)

    lower = jnp.tril(jnp.ones((ML_CHUNK, ML_CHUNK), dtype=bool))

    def step(carry, inp):
        C, nvec, m = carry
        qc, kc, vc, ic, lfc = inp
        b = jnp.cumsum(lfc, axis=-1)
        d = jnp.where(lower, b[..., :, None] - b[..., None, :] + ic[..., None, :], -jnp.inf)
        inter = b + m[..., None]
        m_row = jnp.maximum(inter, jnp.max(d, axis=-1))
        s = jnp.einsum('bhtd,bhsd->bhts', qc, kc) * jnp.exp(d - m_row[..., None])
        w_prev = jnp.exp(inter - m_row)
        num = jnp.einsum('bhts,bhsv->bhtv', s, vc) + w_prev[..., None] * jnp.einsum('bhvd,bhtd->bhtv', C, qc)
        den = jnp.sum(s, axis=-1) + w_prev * jnp.einsum('bhd,bhtd->bht', nvec, qc)
        h = num / jnp.maximum(jnp.abs(den), jnp.exp(-m_row))[..., None]
        b_end = b[..., -1]
        g = b_end[..., None] - b + ic
        m_new = jnp.maximum(b_end + m, jnp.max(g, axis=-1))
        a = jnp.exp(g - m_new[..., None])
        a_prev = jnp.exp(b_end + m - m_new)
        C = a_prev[..., None, None] * C + jnp.einsum('bhsv,bhsd->bhvd', vc * a[..., None], kc)
        nvec = a_prev[..., None] * nvec + jnp.einsum('bhs,bhsd->bhd', a, kc)
        return (C, nvec, m_new), h

    xs = (chunks(q), chunks(k), chunks(v), chunks(i_pre), chunks(jax.nn.log_sigmoid(f_pre.astype(f32))))
    state, hs = lax.scan(step, state, xs)
    return state, jnp.moveaxis(hs, 0, 2).reshape(B, H, n, v.shape[-1])

def odd_mixer(h_lat, h_ctx, need_ctx, w_in, conv_w, conv_b, gate_b, head_norm, w_out):
    f32 = jnp.float32

    def project(h):
        B, n = h.shape[:2]
        q, k, v, o, z, gates = _split(h @ w_in, ODD_SPLITS)
        qk = jax.nn.silu(dw_conv(jnp.concatenate([q, k], axis=-1), conv_w, conv_b))
        q, k = _split(qk, (ML_HEADS * ML_QK, ML_HEADS * ML_QK))
        q = q.reshape(B, n, ML_HEADS, ML_QK).transpose(0, 2, 1, 3)
        k = k.reshape(B, n, ML_HEADS, ML_QK).transpose(0, 2, 1, 3) * (ML_QK ** -0.5)
        v = v.reshape(B, n, ML_HEADS, ML_V).transpose(0, 2, 1, 3)
        gates = (gates + gate_b).astype(f32).reshape(B, n, 4, ML_HEADS).transpose(2, 0, 3, 1)
        return q, k, v, o, z, gates

    def flip(a):
        return jnp.flip(a, axis=2)

    ql, kl, vl, ol, zl, gl = project(h_lat)
    qc, kc, vc, oc, zc, gc = project(h_ctx)
    B = h_lat.shape[0]
    zero = (jnp.zeros((B, ML_HEADS, ML_V, ML_QK), f32), jnp.zeros((B, ML_HEADS, ML_QK), f32),
            jnp.zeros((B, ML_HEADS), f32))
    st_f, hc_f = mlstm_chunkwise(qc, kc, vc, gc[0], gc[1], zero)
    _, hl_f = mlstm_chunkwise(ql, kl, vl, gl[0], gl[1], st_f)
    st_b, hc_b = mlstm_chunkwise(flip(qc), flip(kc), flip(vc), flip(gc[2]), flip(gc[3]), zero)
    _, hl_b = mlstm_chunkwise(flip(ql), flip(kl), flip(vl), flip(gl[2]), flip(gl[3]), st_b)

    def finish(h_f, h_b, o, z):
        Bn, _, n, _ = h_f.shape
        h = (h_f + h_b).transpose(0, 2, 1, 3).reshape(Bn, n, ML_WIDTH).astype(o.dtype) * jax.nn.sigmoid(o)
        h = rms_norm(h.reshape(Bn, n, ML_HEADS, ML_V), head_norm.reshape(ML_HEADS, ML_V)).reshape(Bn, n, ML_WIDTH)
        return (h * jax.nn.silu(z)) @ w_out

    y_lat = finish(hl_f, flip(hl_b), ol, zl)
    y_ctx = finish(hc_f, flip(hc_b), oc, zc) if need_ctx else None
    return y_lat, y_ctx

def first_inputs(seed: int = 0) -> dict:
    key = jax.random.key(seed)
    keys = jax.random.split(key, 32)
    f32 = jnp.float32

    def nrm(i, shape, scale):
        return jax.random.normal(keys[i], shape, f32) * scale

    D = D_MODEL
    forget_init = jnp.linspace(3.0, 6.0, ML_HEADS, dtype=f32)
    o_gate_b = jnp.concatenate([
        nrm(24, (N_ODD, ML_HEADS), 0.1),
        forget_init + nrm(25, (N_ODD, ML_HEADS), 0.1),
        nrm(26, (N_ODD, ML_HEADS), 0.1),
        forget_init + nrm(27, (N_ODD, ML_HEADS), 0.1)], axis=-1)
    return {
        'x': nrm(0, (BATCH, SEQ, D), 1.0),
        'c': nrm(1, (BATCH, D), 1.0),
        'ctx': nrm(2, (BATCH, CTX_LEN, D), 1.0),
        'c_ctx': nrm(3, (D,), 1.0),
        'w_mod': nrm(4, (DEPTH, D, 3 * D), D ** -0.5),
        'b_mod': nrm(5, (DEPTH, 3 * D), 0.02),
        'g_pre': 1.0 + nrm(6, (DEPTH, D), 0.02),
        'g_post': 1.0 + nrm(7, (DEPTH, D), 0.02),
        'e_w_in': nrm(8, (N_EVEN, D, EVEN_IN), D ** -0.5),
        'e_conv_w': nrm(9, (N_EVEN, HY_SHORT, 3 * HY_WIDTH), HY_SHORT ** -0.5),
        'e_conv_b': nrm(10, (N_EVEN, 3 * HY_WIDTH), 0.02),
        'e_filt_w1': nrm(11, (N_EVEN, HY_EMB, HY_HIDDEN), HY_EMB ** -0.5),
        'e_filt_b1': nrm(12, (N_EVEN, HY_HIDDEN), 0.1),
        'e_filt_freq': 1.0 + nrm(13, (N_EVEN, HY_HIDDEN), 0.02),
        'e_filt_w2': nrm(14, (N_EVEN, HY_HIDDEN, HY_HIDDEN), HY_HIDDEN ** -0.5),
        'e_filt_b2': nrm(15, (N_EVEN, HY_HIDDEN), 0.1),
        'e_filt_w3': nrm(16, (N_EVEN, HY_HIDDEN, 2 * HY_WIDTH), HY_HIDDEN ** -0.5),
        'e_hy_bias': nrm(17, (N_EVEN, HY_WIDTH), 0.1),
        'e_q_norm': 1.0 + nrm(18, (N_EVEN, HEAD_DIM), 0.02),
        'e_k_norm': 1.0 + nrm(19, (N_EVEN, HEAD_DIM), 0.02),
        'e_w_out': nrm(20, (N_EVEN, EVEN_MIX, D), EVEN_MIX ** -0.5),
        'o_w_in': nrm(21, (N_ODD, D, ODD_IN), D ** -0.5),
        'o_conv_w': nrm(22, (N_ODD, ML_SHORT, 2 * ML_HEADS * ML_QK), ML_SHORT ** -0.5),
        'o_conv_b': nrm(23, (N_ODD, 2 * ML_HEADS * ML_QK), 0.02),
        'o_gate_b': o_gate_b,
        'o_head_norm': 1.0 + nrm(28, (N_ODD, ML_WIDTH), 0.02),
        'o_w_out': nrm(29, (N_ODD, ML_WIDTH, D), ML_WIDTH ** -0.5),
    }

def first_block(x, c, ctx, c_ctx, w_mod, b_mod, g_pre, g_post, e_w_in, e_conv_w, e_conv_b, e_filt_w1,
              e_filt_b1, e_filt_freq, e_filt_w2, e_filt_b2, e_filt_w3, e_hy_bias, e_q_norm, e_k_norm,
              e_w_out, o_w_in, o_conv_w, o_conv_b, o_gate_b, o_head_norm, o_w_out):
    n_lat = x.shape[1]
    ROWS = n_lat // GRID_W
    rows = jnp.repeat(jnp.arange(ROWS, dtype=jnp.int32), GRID_W)
    cols = jnp.tile(jnp.arange(GRID_W, dtype=jnp.int32), ROWS)
    x_lat, x_ctx = x, ctx
    for layer in range(DEPTH):
        need_ctx = layer < DEPTH - 1
        sh_l, sc_l, ga_l = adaln(c, w_mod[layer], b_mod[layer])
        sh_c, sc_c, ga_c = adaln(c_ctx, w_mod[layer], b_mod[layer])
        h_lat = rms_norm(x_lat, g_pre[layer]) * (1 + sc_l[:, None]) + sh_l[:, None]
        h_ctx = rms_norm(x_ctx, g_pre[layer]) * (1 + sc_c) + sh_c
        j = layer // 2
        if layer % 2 == 0:
            y_lat, y_ctx = even_mixer(h_lat, h_ctx, rows, cols, need_ctx, e_w_in[j], e_conv_w[j], e_conv_b[j],
                                      e_filt_w1[j], e_filt_b1[j], e_filt_freq[j], e_filt_w2[j], e_filt_b2[j],
                                      e_filt_w3[j], e_hy_bias[j], e_q_norm[j], e_k_norm[j], e_w_out[j])
        else:
            y_lat, y_ctx = odd_mixer(h_lat, h_ctx, need_ctx, o_w_in[j], o_conv_w[j], o_conv_b[j], o_gate_b[j],
                                     o_head_norm[j], o_w_out[j])
        x_lat = x_lat + ga_l[:, None] * rms_norm(y_lat, g_post[layer])
        if need_ctx:
            x_ctx = x_ctx + ga_c * rms_norm(y_ctx, g_post[layer])
    return x_lat


MLA_HEADS = 8
MLA_Q_RANK = 256
MLA_KV_RANK = 128
MLA_NOPE = 64
MLA_ROPE = 32
MLA_V = 64
MOBA_HEADS = 8
MOBA_HEAD_DIM = 64
MOBA_BLOCK = 256
MOBA_TOPK = 3
MOBA_Q_CHUNK = 32
RET_HEADS = 4
RET_QK_DIM = 64
RET_V_DIM = 128
RET_CHUNK = 128
RET_THETA = 10000.0
ROPE_THETA_2 = 500000.0
PARTIAL_ROPE_DIV = 4
ATTN_Q_BLOCK = 128
D_FF = 4 * D_MODEL
GN_EPS = 1e-5
NEG_INF = -1e30

MOBA_W = MOBA_HEADS * MOBA_HEAD_DIM
RET_QK_W = RET_HEADS * RET_QK_DIM
RET_V_W = RET_HEADS * RET_V_DIM
MLA_OUT_W = MLA_HEADS * MLA_V
IN_SPLIT_SIZES = (MLA_Q_RANK, MLA_KV_RANK, MLA_ROPE,
                  MOBA_W, MOBA_W, MOBA_W,
                  RET_QK_W, RET_QK_W, RET_V_W, RET_V_W,
                  D_MODEL, D_MODEL, D_MODEL)
IN_COLS = sum(IN_SPLIT_SIZES)
IN_SPLIT_IDX = tuple(int(i) for i in np.cumsum(IN_SPLIT_SIZES)[:-1])


def rms_norm_2(x, g, eps=NORM_EPS):
    xf = x.astype(jnp.float32)
    y = xf * lax.rsqrt(jnp.mean(xf * xf, axis=-1, keepdims=True) + eps)
    return (y * g.astype(jnp.float32)).astype(x.dtype)

def rope_tables(seq, dim, theta):
    inv = 1.0 / (theta ** (jnp.arange(0, dim, 2, dtype=jnp.float32) / dim))
    ang = jnp.arange(seq, dtype=jnp.float32)[:, None] * inv[None, :]
    return jnp.cos(ang), jnp.sin(ang)

def apply_rope(x, cos, sin):
    half = x.shape[-1] // 2
    x1, x2 = x[..., :half], x[..., half:]
    c, s = cos.astype(x.dtype), sin.astype(x.dtype)
    return jnp.concatenate([x1 * c - x2 * s, x1 * s + x2 * c], axis=-1)

def causal_attention(q, k, v, scale):
    B, H, S, _ = q.shape
    kpos = jnp.arange(S)

    def block(i):
        start = i * ATTN_Q_BLOCK
        qb = lax.dynamic_slice_in_dim(q, start, ATTN_Q_BLOCK, axis=2)
        s = jnp.einsum('bhqd,bhkd->bhqk', qb, k).astype(jnp.float32) * scale
        qpos = start + jnp.arange(ATTN_Q_BLOCK)
        s = jnp.where(kpos[None, :] <= qpos[:, None], s, NEG_INF)
        p = jax.nn.softmax(s, axis=-1).astype(v.dtype)
        return jnp.einsum('bhqk,bhkd->bhqd', p, v)

    o = lax.map(block, jnp.arange(S // ATTN_Q_BLOCK))
    return o.transpose(1, 2, 0, 3, 4).reshape(B, H, S, v.shape[-1])

def mla_branch(cq, ckv, k_rope, q_norm_g, kv_norm_g, w_q_up, w_kv_up, cos, sin):
    B, S, _ = cq.shape
    cq = rms_norm_2(cq, q_norm_g)
    ckv = rms_norm_2(ckv, kv_norm_g)
    q = (cq @ w_q_up).reshape(B, S, MLA_HEADS, MLA_NOPE + MLA_ROPE).transpose(0, 2, 1, 3)
    q = jnp.concatenate([q[..., :MLA_NOPE], apply_rope(q[..., MLA_NOPE:], cos, sin)], axis=-1)
    kv = (ckv @ w_kv_up).reshape(B, S, MLA_HEADS, MLA_NOPE + MLA_V).transpose(0, 2, 1, 3)
    k_pe = apply_rope(k_rope, cos, sin)[:, None]
    k = jnp.concatenate([kv[..., :MLA_NOPE],
                         jnp.broadcast_to(k_pe, (B, MLA_HEADS, S, MLA_ROPE))], axis=-1)
    v = kv[..., MLA_NOPE:]
    o = causal_attention(q, k, v, (MLA_NOPE + MLA_ROPE) ** -0.5)
    return o.transpose(0, 2, 1, 3).reshape(B, S, MLA_OUT_W)

def moba_branch(q, k, v, cos, sin):
    B, S, _ = q.shape
    H, Dh, BS, QC = MOBA_HEADS, MOBA_HEAD_DIM, MOBA_BLOCK, MOBA_Q_CHUNK
    rd = Dh // PARTIAL_ROPE_DIV

    def heads(t):
        return t.reshape(B, S, H, Dh).transpose(0, 2, 1, 3)

    def partial_rope(t):
        return jnp.concatenate([apply_rope(t[..., :rd], cos, sin), t[..., rd:]], axis=-1)

    q, k, v = partial_rope(heads(q)), partial_rope(heads(k)), heads(v)
    nb = -(-S // BS)
    pad = nb * BS - S
    padw = ((0, 0), (0, 0), (0, pad), (0, 0))
    q, k, v = jnp.pad(q, padw), jnp.pad(k, padw), jnp.pad(v, padw)
    kb = k.reshape(B, H, nb, BS, Dh)
    vb = v.reshape(B, H, nb, BS, Dh)
    k_mean = jnp.mean(kb.astype(jnp.float32), axis=3)
    topk = min(MOBA_TOPK, nb)
    scale = Dh ** -0.5
    bi = jnp.arange(B)[:, None, None, None]
    hi = jnp.arange(H)[None, :, None, None]

    def chunk(c):
        start = c * QC
        blk = start // BS
        qc = lax.dynamic_slice_in_dim(q, start, QC, axis=2)
        gate = jnp.einsum('bhqd,bhnd->bhqn', qc.astype(jnp.float32), k_mean)
        gate = jnp.where(jnp.arange(nb) < blk, gate, NEG_INF)
        _, idx = lax.top_k(gate, topk)
        sel_valid = jnp.arange(topk) < blk
        k_sel = kb[bi, hi, idx]
        v_sel = vb[bi, hi, idx]
        s_sel = jnp.einsum('bhqd,bhqnkd->bhqnk', qc, k_sel).astype(jnp.float32) * scale
        s_sel = jnp.where(sel_valid[:, None], s_sel, NEG_INF).reshape(B, H, QC, topk * BS)
        k_own = lax.dynamic_index_in_dim(kb, blk, axis=2, keepdims=False)
        v_own = lax.dynamic_index_in_dim(vb, blk, axis=2, keepdims=False)
        s_own = jnp.einsum('bhqd,bhkd->bhqk', qc, k_own).astype(jnp.float32) * scale
        qpos = start + jnp.arange(QC)
        kpos = blk * BS + jnp.arange(BS)
        s_own = jnp.where(kpos[None, :] <= qpos[:, None], s_own, NEG_INF)
        p = jax.nn.softmax(jnp.concatenate([s_sel, s_own], axis=-1), axis=-1).astype(v.dtype)
        o_sel = jnp.einsum('bhqn,bhqnd->bhqd', p[..., :topk * BS],
                           v_sel.reshape(B, H, QC, topk * BS, Dh))
        o_own = jnp.einsum('bhqk,bhkd->bhqd', p[..., topk * BS:], v_own)
        return o_sel + o_own

    o = lax.map(chunk, jnp.arange(nb * BS // QC))
    o = o.transpose(1, 2, 0, 3, 4).reshape(B, H, nb * BS, Dh)[:, :, :S]
    return o.transpose(0, 2, 1, 3).reshape(B, S, MOBA_W)

def retention_branch(q, k, v, g, gn_w, gn_b, cos, sin):
    B, S, _ = q.shape
    H, Dk, Dv, C = RET_HEADS, RET_QK_DIM, RET_V_DIM, RET_CHUNK
    nc = S // C
    f32 = jnp.float32
    q = apply_rope(q.astype(f32).reshape(B, S, H, Dk).transpose(0, 2, 1, 3), cos, sin)
    k = apply_rope(k.astype(f32).reshape(B, S, H, Dk).transpose(0, 2, 1, 3), cos, sin) * (Dk ** -0.5)
    v = v.astype(f32).reshape(B, S, H, Dv).transpose(0, 2, 1, 3)
    log_gamma = jnp.log(1.0 - 2.0 ** (-5.0 - jnp.arange(H, dtype=f32)))
    pos = jnp.arange(C, dtype=f32)
    diff = pos[:, None] - pos[None, :]
    decay_in = jnp.where(diff >= 0, jnp.exp(log_gamma[:, None, None] * diff), 0.0)
    xi = jnp.exp(log_gamma[:, None] * (pos + 1.0))
    zeta = jnp.exp(log_gamma[:, None] * (C - 1.0 - pos))
    gamma_c = jnp.exp(log_gamma * C)[None, :, None, None]
    qc = q.reshape(B, H, nc, C, Dk)
    kc = k.reshape(B, H, nc, C, Dk)
    vc = v.reshape(B, H, nc, C, Dv)
    scores = jnp.einsum('bhnid,bhnjd->bhnij', qc, kc) * decay_in[:, None]
    inner = jnp.einsum('bhnij,bhnje->bhnie', scores, vc)
    kv_chunk = jnp.einsum('bhnjd,bhnje->bhnde', kc * zeta[:, None, :, None], vc)

    def step(R, kv):
        return gamma_c * R + kv, R

    _, R_prev = lax.scan(step, jnp.zeros((B, H, Dk, Dv), f32), kv_chunk.transpose(2, 0, 1, 3, 4))
    R_prev = R_prev.transpose(1, 2, 0, 3, 4)
    cross = jnp.einsum('bhnid,bhnde->bhnie', qc * xi[:, None, :, None], R_prev)
    o = (inner + cross).reshape(B, H, S, Dv)
    mu = jnp.mean(o, axis=-1, keepdims=True)
    var = jnp.mean(jnp.square(o - mu), axis=-1, keepdims=True)
    o = (o - mu) * lax.rsqrt(var + GN_EPS)
    o = o.transpose(0, 2, 1, 3).reshape(B, S, RET_V_W) * gn_w.astype(f32) + gn_b.astype(f32)
    return jax.nn.silu(g) * o.astype(g.dtype)

def hybrid_mixer(h, w_in, mla_q_norm, mla_kv_norm, mla_w_q_up, mla_w_kv_up, ret_gn_w, ret_gn_b,
                 w_branch_mla, w_branch_moba, w_branch_ret, w_out, ropes):
    (cos_mla, sin_mla), (cos_moba, sin_moba), (cos_ret, sin_ret) = ropes
    p = h @ w_in
    (cq, ckv, k_rope, mq, mk, mv, rq, rk, rv, rg, g_mla, g_moba, g_ret) = jnp.split(p, IN_SPLIT_IDX, axis=-1)
    o_mla = mla_branch(cq, ckv, k_rope, mla_q_norm, mla_kv_norm, mla_w_q_up, mla_w_kv_up, cos_mla, sin_mla)
    o_moba = moba_branch(mq, mk, mv, cos_moba, sin_moba)
    o_ret = retention_branch(rq, rk, rv, rg, ret_gn_w, ret_gn_b, cos_ret, sin_ret)
    merged = (jax.nn.sigmoid(g_mla) * (o_mla @ w_branch_mla)
              + jax.nn.sigmoid(g_moba) * (o_moba @ w_branch_moba)
              + jax.nn.sigmoid(g_ret) * (o_ret @ w_branch_ret))
    return merged @ w_out

def squared_relu_mlp(h, w_up, w_down):
    return jnp.square(jax.nn.relu(h @ w_up)) @ w_down

def second_inputs(seed: int = 0) -> dict:
    key = jax.random.key(seed)
    ks = jax.random.split(key, 18)

    def dense(k, shape):
        return jax.random.normal(k, shape, jnp.float32) * (shape[-2] ** -0.5)

    def gain(k, shape):
        return 1.0 + 0.02 * jax.random.normal(k, shape, jnp.float32)

    L = DEPTH
    return {
        "x": jax.random.normal(ks[0], (BATCH, SEQ, D_MODEL), jnp.float32),
        "attn_norm": gain(ks[1], (L, D_MODEL)),
        "w_in": dense(ks[2], (L, D_MODEL, IN_COLS)),
        "mla_q_norm": gain(ks[3], (L, MLA_Q_RANK)),
        "mla_kv_norm": gain(ks[4], (L, MLA_KV_RANK)),
        "mla_w_q_up": dense(ks[5], (L, MLA_Q_RANK, MLA_HEADS * (MLA_NOPE + MLA_ROPE))),
        "mla_w_kv_up": dense(ks[6], (L, MLA_KV_RANK, MLA_HEADS * (MLA_NOPE + MLA_V))),
        "ret_gn_w": gain(ks[7], (L, RET_V_W)),
        "ret_gn_b": 0.02 * jax.random.normal(ks[8], (L, RET_V_W), jnp.float32),
        "w_branch_mla": dense(ks[9], (L, MLA_OUT_W, D_MODEL)),
        "w_branch_moba": dense(ks[10], (L, MOBA_W, D_MODEL)),
        "w_branch_ret": dense(ks[11], (L, RET_V_W, D_MODEL)),
        "w_out": dense(ks[12], (L, D_MODEL, D_MODEL)),
        "mlp_norm": gain(ks[13], (L, D_MODEL)),
        "w_mlp_up": dense(ks[14], (L, D_MODEL, D_FF)),
        "w_mlp_down": dense(ks[15], (L, D_FF, D_MODEL)),
        "final_norm": gain(ks[16], (D_MODEL,)),
    }

def second_block(x, attn_norm, w_in, mla_q_norm, mla_kv_norm, mla_w_q_up, mla_w_kv_up, ret_gn_w, ret_gn_b,
              w_branch_mla, w_branch_moba, w_branch_ret, w_out, mlp_norm, w_mlp_up, w_mlp_down, final_norm):
    S = x.shape[1]
    ropes = (rope_tables(S, MLA_ROPE, ROPE_THETA_2),
             rope_tables(S, MOBA_HEAD_DIM // PARTIAL_ROPE_DIV, ROPE_THETA_2),
             rope_tables(S, RET_QK_DIM, RET_THETA))
    for l in range(DEPTH):
        h = rms_norm_2(x, attn_norm[l])
        x = x + hybrid_mixer(h, w_in[l], mla_q_norm[l], mla_kv_norm[l], mla_w_q_up[l], mla_w_kv_up[l],
                             ret_gn_w[l], ret_gn_b[l], w_branch_mla[l], w_branch_moba[l], w_branch_ret[l],
                             w_out[l], ropes)
        h = rms_norm_2(x, mlp_norm[l])
        x = x + squared_relu_mlp(h, w_mlp_up[l], w_mlp_down[l])
    return rms_norm_2(x, final_norm)


def setup_inputs(seed=0):
    out = dict(first_inputs(seed))
    for name, value in second_inputs(seed + 1).items():
        if name != "x":
            out[name + "_2"] = value
    return out


def reference(
    x, c, ctx, c_ctx, w_mod, b_mod, g_pre, g_post, e_w_in, e_conv_w, e_conv_b, e_filt_w1,
    e_filt_b1, e_filt_freq, e_filt_w2, e_filt_b2, e_filt_w3, e_hy_bias, e_q_norm, e_k_norm,
    e_w_out, o_w_in, o_conv_w, o_conv_b, o_gate_b, o_head_norm, o_w_out, attn_norm_2, w_in_2,
    mla_q_norm_2, mla_kv_norm_2, mla_w_q_up_2, mla_w_kv_up_2, ret_gn_w_2, ret_gn_b_2,
    w_branch_mla_2, w_branch_moba_2, w_branch_ret_2, w_out_2, mlp_norm_2, w_mlp_up_2,
    w_mlp_down_2, final_norm_2,
):
    x = first_block(
        x, c, ctx, c_ctx, w_mod, b_mod, g_pre, g_post, e_w_in, e_conv_w, e_conv_b, e_filt_w1,
        e_filt_b1, e_filt_freq, e_filt_w2, e_filt_b2, e_filt_w3, e_hy_bias, e_q_norm, e_k_norm,
        e_w_out, o_w_in, o_conv_w, o_conv_b, o_gate_b, o_head_norm, o_w_out,
    )
    return second_block(
        x, attn_norm_2, w_in_2, mla_q_norm_2, mla_kv_norm_2, mla_w_q_up_2, mla_w_kv_up_2,
        ret_gn_w_2, ret_gn_b_2, w_branch_mla_2, w_branch_moba_2, w_branch_ret_2, w_out_2,
        mlp_norm_2, w_mlp_up_2, w_mlp_down_2, final_norm_2,
    )


_drawn_inputs = setup_inputs


def setup_inputs(seed=0):
    import zlib

    import numpy as np

    out = dict(_drawn_inputs(seed))
    spreads = {}
    factors = {'g_post': 2.942,
     'e_conv_b': 4.243,
     'e_filt_freq': 6.403,
     'e_q_norm': 8.0,
     'e_k_norm': 8.0,
     'o_conv_b': 8.0,
     'o_head_norm': 3.843,
     'attn_norm_2': 3.288,
     'mla_q_norm_2': 8.0,
     'mla_kv_norm_2': 6.817,
     'ret_gn_w_2': 8.0,
     'ret_gn_b_2': 8.0,
     'final_norm_2': 7.47,
     'mlp_norm_2': 8.0}
    for name, (base, spread) in spreads.items():
        noise = np.random.default_rng([zlib.crc32(name.encode()), seed]).standard_normal(out[name].shape)
        drawn = base * np.exp(spread * noise) if base else spread * noise
        out[name] = jnp.asarray(drawn.astype(out[name].dtype))
    for name, factor in factors.items():
        out[name] = (out[name] * factor).astype(out[name].dtype)
    return out
```

```python
from contextlib import ExitStack, contextmanager
import math

import numpy as np
import concourse.bass as bass
from concourse import mybir

ALU = mybir.AluOpType
ACT = mybir.ActivationFunctionType
AX = mybir.AxisListType
F32 = mybir.dt.float32

P = 128
D = 1024
KC = D // P
SEQ = 256
NT = 2 * SEQ // P
LT = SEQ // P
DEPTH = 2
EPS = 1e-6
GN_EPS = 1e-5
NEG = -1e30

HY = 1024
EV_XV, EV_GHY, EV_Q, EV_KV, EV_GATT = 0, 3072, 4096, 5120, 5632
HEADS, KVH, DH = 8, 2, 128
ML_H, ML_QK, ML_V = 8, 128, 256
OD_K, OD_V, OD_O, OD_Z, OD_G = 1024, 2048, 4096, 6144, 8192

MLA_Q, MLA_KV, MLA_R, MLA_N = 256, 128, 32, 64
IN2_FIRST = MLA_Q + MLA_KV + MLA_R
RET_H, RET_QK, RET_V = 4, 64, 128
D_FF = 4096

SLOTS = 3
BANK = 512

COL_AT = {}
_n = 0
for _name, _w in (("c", 8), ("c_ctx", 8), ("b_sh0", 8), ("b_sc0", 8), ("b_sh1", 8), ("b_sc1", 8),
                  ("g_pre0", 8), ("g_pre1", 8), ("e_cw0", 24), ("e_cw1", 24), ("e_cw2", 24), ("e_cb", 24),
                  ("hy_bias", 8), ("o_cw0", 16), ("o_cw1", 16), ("o_cw2", 16), ("o_cb", 16),
                  ("an0", 8), ("an1", 8), ("mn0", 8), ("mn1", 8), ("qn0", 2), ("qn1", 2), ("kvn0", 1), ("kvn1", 1),
                  ("f_b1", 1), ("f_b2", 1), ("f_fr", 1), ("gb_i", 1), ("gb_f", 1)):
    COL_AT[_name] = _n
    _n += _w
NCOL = _n

ROW_AT = {}
_n = 0
for _name, _w in (("b_ga0", D), ("b_ga1", D), ("g_post0", D), ("g_post1", D), ("q_norm", DH), ("k_norm", DH),
                  ("head_norm", 2048), ("gn_w0", 512), ("gn_b0", 512), ("gn_w1", 512), ("gn_b1", 512),
                  ("final", D)):
    ROW_AT[_name] = (_n, _w)
    _n += _w
NROW = _n


def weight_stream(a):
    items, first = [], {}

    def cols(name, w, starts, width=BANK):
        first[name] = len(items)
        for s in starts:
            items.append([(w[:, s:s + width].rearrange("(k p) n -> p k n", p=P), 0, KC, width)])

    def rows(name, w):
        first[name] = len(items)
        n = w.shape[0] // 512
        for i in range(n):
            items.append([(w[i * 512:(i + 1) * 512, :].rearrange("(k p) n -> p k n", p=P), 0, 4, D)])

    for l in range(DEPTH):
        cols(f"mod{l}", a["w_mod"][l], range(0, 3 * D, BANK))
    w = a["e_w_in"][0]
    cols("e_qkv", w, (EV_Q, EV_Q + 512, EV_KV))
    cols("e_gatt", w, (EV_GATT, EV_GATT + 512))
    cols("e_x1", w, (1024, 1536))
    cols("e_v", w, (2048, 2560))
    cols("e_x0", w, (0, 512))
    cols("e_ghy", w, (EV_GHY, EV_GHY + 512))
    rows("e_out", a["e_w_out"][0])
    w = a["o_w_in"][0]
    cols("o_q", w, (0, 512))
    cols("o_k", w, (OD_K, OD_K + 512))
    cols("o_v", w, range(OD_V, OD_O, BANK))
    cols("o_o", w, range(OD_O, OD_Z, BANK))
    cols("o_z", w, range(OD_Z, OD_G, BANK))
    rows("o_out", a["o_w_out"][0])
    for l in range(DEPTH):
        w = a["w_in_2"][l]
        cols(f"in{l}a", w, (0,), IN2_FIRST)
        cols(f"in{l}", w, range(IN2_FIRST, IN2_FIRST + 12 * BANK, BANK))
        first[f"up{l}"] = len(items)
        items.append([
            (a["mla_w_q_up_2"][l].rearrange("(k p) n -> p k n", p=P), 0, 2, 768),
            (a["mla_w_kv_up_2"][l].rearrange("(k p) n -> p k n", p=P), 1536, 1, 1024)])
        rows(f"b_mla{l}", a["w_branch_mla_2"][l])
        rows(f"b_moba{l}", a["w_branch_moba_2"][l])
        rows(f"b_ret{l}", a["w_branch_ret_2"][l])
        rows(f"out{l}", a["w_out_2"][l])
        cols(f"mup{l}", a["w_mlp_up_2"][l], range(0, D_FF, BANK))
        rows(f"mdn{l}", a["w_mlp_down_2"][l])
    return items, first


class Chain:

    def __init__(self, sem):
        self.sem, self.n = sem, 0

    def __call__(self, eng, ins):
        self.n += 1
        ins.then_inc(self.sem, 1)
        eng.wait_ge(self.sem, self.n)


class Core:

    def __init__(self, nc, a, ctx):
        self.nc, self.a, self.ctx = nc, a, ctx
        self.items, self.first = weight_stream(a)
        sb = lambda name, shape: ctx.enter_context(nc.sbuf_tensor(name, shape, F32))
        self.x = sb("x_res", [P, NT, D])
        self.hT = sb("hT", [P, KC, 2 * SEQ])
        self.ring = sb("weights", [P, SLOTS, 4096])
        self.cols = sb("cols", [P, NCOL])
        self.ident = sb("ident", [P, P])
        self.ga = sb("ga", [P, 3, D])
        self.mod = sb("mod", [P, 2, 2, KC, 2])
        self.small = sb("small", [P, 256])
        self.ps = ctx.enter_context(nc.psum_tensor("psum", [P, 8, BANK], F32))
        keep = lambda name: ctx.enter_context(nc.semaphore(name))
        self.tables_in, self.tables_n = keep("tables_in"), 0
        self.stored = keep("result_stored")
        self.landed = [keep(f"weight_landed{s}") for s in range(SLOTS)]
        self.dve_chain = Chain(keep("dve_step"))
        self.act_chain = Chain(keep("act_step"))
        self.pool_chain = Chain(keep("pool_step"))
        self.landed_at, total = [], [0] * SLOTS
        for i, pieces in enumerate(self.items):
            total[i % SLOTS] += 16 * len(pieces)
            self.landed_at.append(total[i % SLOTS])
        self.issued = 0
        self.fresh, self.old = ([], ExitStack()), ([], ExitStack())

    def expect_tables(self, n):
        self.tables_n += 16 * n
        return self.tables_n

    def sem(self, name):
        s = self.fresh[1].enter_context(self.nc.semaphore(name))
        self.fresh[0].append(s)
        return s

    @contextmanager
    def phase(self):
        old, self.old = self.old, self.fresh
        self.fresh = ([], ExitStack())
        with self.nc.Block() as block:
            if old[0]:
                @block.gpsimd
                def _(pool):
                    for s in old[0]:
                        pool.sem_clear(s)
            yield block
        old[1].close()

    def col(self, name, i=0, n=1):
        at = COL_AT[name] + i
        return self.cols[:, at:at + n]

    def load_weight(self, eng, i):
        self.issued = i + 1
        for src, at, k, n in self.items[i]:
            dst = self.ring[:, i % SLOTS, at:at + k * n].rearrange("p (k n) -> p k n", k=k)
            eng.dma_start(dst, src).then_inc(self.landed[i % SLOTS], 16)

    def load_ahead(self, eng, lo, used, values):
        for i, value in enumerate(values):
            if lo + i + SLOTS < len(self.items):
                eng.wait_ge(used, value)
                self.load_weight(eng, lo + i + SLOTS)

    def weight(self, eng, i, piece=0):
        eng.wait_ge(self.landed[i % SLOTS], self.landed_at[i])
        _, at, k, n = self.items[i][piece]
        return self.ring[:, i % SLOTS, at:at + k * n].rearrange("p (k n) -> p k n", k=k)


def setup(core):
    nc, a = core.nc, core.a
    loaded = core.sem("setup_loaded")
    with core.phase() as block:
        @block.sync
        def _(sp):
            for i in range(SLOTS):
                core.load_weight(sp, i)

        @block.scalar
        def _(act):
            act.dma_start(core.cols[:], a["cols"]).then_inc(loaded, 16)
            act.dma_start(core.ident[:], a["ident"]).then_inc(loaded, 16)
            act.dma_start(core.x[:, 0:LT, :], a["x"][0].rearrange("(t p) d -> p t d", p=P)).then_inc(loaded, 16)
            act.dma_start(core.x[:, LT:NT, :], a["ctx"][0].rearrange("(t p) d -> p t d", p=P)).then_inc(loaded, 16)
            act.wait_ge(loaded, 64)


def row_bcast(a, name):
    at, n = ROW_AT[name]
    return a["rows"][at:at + n].partition_broadcast(P)


def adaln(core):
    nc, a, ps = core.nc, core.a, core.ps
    with ExitStack() as c:
        sb = lambda name, shape: c.enter_context(nc.sbuf_tensor(name, shape, F32))
        cond = sb("cond", [P, KC, 2])
        wide = sb("cond_wide", [P, 2, KC, P])
        brow = sb("mod_rows", [P, 4, D])
        rows_in = core.expect_tables(4)
        cond_ready, wide_ready = core.sem("cond_ready"), core.sem("cond_wide_ready")
        mod_done = core.sem("mod_done")
        lo = core.first["mod0"]
        gates = [(0, 0), (0, 1), (1, 0)]
        with core.phase() as block:
            @block.sync
            def _(sp):
                core.load_ahead(sp, lo, mod_done, range(1, 13))

            @block.gpsimd
            def _(pool):
                for i, name in enumerate(("b_ga0", "b_ga1", "g_post0", "g_post1")):
                    pool.dma_start(brow[:, i, :], row_bcast(a, name)).then_inc(core.tables_in, 16)

            @block.scalar
            def _(act):
                for s, name in enumerate(("c", "c_ctx")):
                    nc.scalar.activation(cond[:, :, s], core.col(name, 0, KC), ACT.Silu).then_inc(cond_ready, 1)

            @block.tensor
            def _(pe):
                pe.wait_ge(cond_ready, 2)
                pe.wait_ge(wide_ready, 2)
                for l in range(DEPTH):
                    for j in range(4):
                        w = core.weight(pe, lo + 6 * l + j)
                        for m in range(4):
                            o = ((l * 4 + j) * 4 + m) * 2
                            for k in range(KC):
                                mm = nc.tensor.matmul(ps[:, 0, o:o + 2], w[:, k, m * P:(m + 1) * P], cond[:, k, :],
                                                      start=(k == 0), stop=(k == KC - 1))
                        mm.then_inc(mod_done, 1)
                    for j in range(2):
                        w = core.weight(pe, lo + 6 * l + 4 + j)
                        for s in range(2 if l == 0 else 1):
                            for k in range(KC):
                                mm = nc.tensor.matmul(ps[:, 1 + (2 * l + s) * 2 + j, :], wide[:, s, k, :], w[:, k, :],
                                                      start=(k == 0), stop=(k == KC - 1))
                        mm.then_inc(mod_done, 1)

            @block.vector
            def _(dve):
                link = core.dve_chain
                dve.wait_ge(cond_ready, 2)
                for s in range(2):
                    nc.vector.tensor_copy(wide[:, s], cond[:, :, s:s + 1].broadcast_to([P, KC, P])).then_inc(wide_ready, 1)
                dve.wait_ge(mod_done, 10)
                for l in range(DEPTH):
                    m = ps[:, 0, l * 32:(l + 1) * 32].rearrange("p (h k s) -> p h k s", h=2, s=2)
                    for h, name in enumerate((f"b_sh{l}", f"b_sc{l}")):
                        for s in range(2):
                            link(dve, nc.vector.tensor_tensor(core.mod[:, l, h, :, s], m[:, h, :, s],
                                                              core.col(name, 0, KC), ALU.add))
                    for s in range(2):
                        link(dve, nc.vector.scalar_tensor_tensor(
                            out=core.mod[:, l, 1, :, s], in0=core.mod[:, l, 1, :, s], scalar=1.0,
                            in1=core.col(f"g_pre{l}", 0, KC), op0=ALU.add, op1=ALU.mult))
                dve.wait_ge(mod_done, 12)
                dve.wait_ge(core.tables_in, rows_in)
                for i, (l, s) in enumerate(gates):
                    for j in range(2):
                        o = core.ga[:, i, j * BANK:(j + 1) * BANK]
                        link(dve, nc.vector.tensor_tensor(o, ps[:, 1 + (2 * l + s) * 2 + j, :],
                                                          brow[:, l, j * BANK:(j + 1) * BANK], ALU.add))
                        link(dve, nc.vector.tensor_tensor(o, o, brow[:, 2 + l, j * BANK:(j + 1) * BANK], ALU.mult))


def normed(core, tag, tiles, scale, shift=None):
    nc, ps, x, hT = core.nc, core.ps, core.x, core.hT
    with ExitStack() as c:
        xn = c.enter_context(nc.sbuf_tensor(tag + "xn", [P, NT, D], F32))
        sq = c.enter_context(nc.sbuf_tensor(tag + "sq", [P, D], F32))
        st = c.enter_context(nc.sbuf_tensor(tag + "st", [P, 3, NT], F32))
        squares, meaned, rooted, scaled, turned, out_act, out_dve = (
            core.sem(tag + s) for s in ("squares", "meaned", "rooted", "scaled", "turned", "out_act", "out_dve"))
        T = len(tiles)
        with core.phase() as block:
            @block.scalar
            def _(act):
                for i, t in enumerate(tiles):
                    core.act_chain(act, nc.scalar.activation(sq[:], x[:, t, :], ACT.Square, accum_out=st[:, 0, i:i + 1]))
                nc.scalar.activation(sq[:, 0:1], x[:, 0, 0:1], ACT.Copy).then_inc(squares, 1)
                act.wait_ge(meaned, 1)
                nc.scalar.activation(st[:, 1, 0:T], st[:, 1, 0:T], ACT.Sqrt).then_inc(rooted, 1)
                for k in range(KC):
                    act.wait_ge(turned, k + 1)
                    nc.scalar.activation(hT[:, k, 0:SEQ], ps[:, k % 4, 0:SEQ], ACT.Identity, scale=scale(k, 0),
                                         bias=shift(k, 0) if shift else 0.0).then_inc(out_act, 1)

            @block.vector
            def _(dve):
                link = core.dve_chain
                dve.wait_ge(squares, 1)
                nc.vector.tensor_scalar(st[:, 1, 0:T], st[:, 0, 0:T], 1.0 / D, EPS, ALU.mult, ALU.add).then_inc(meaned, 1)
                dve.wait_ge(rooted, 1)
                link(dve, nc.vector.reciprocal(st[:, 2, 0:T], st[:, 1, 0:T]))
                for i, t in enumerate(tiles):
                    nc.vector.tensor_scalar(xn[:, i, :], x[:, t, :], st[:, 2, i:i + 1], None, ALU.mult).then_inc(scaled, 1)
                if T == NT:
                    for k in range(KC):
                        dve.wait_ge(turned, k + 1)
                        dve.wait_ge(out_act, k + 1)
                        nc.vector.tensor_scalar(hT[:, k, SEQ:2 * SEQ], ps[:, k % 4, SEQ:2 * SEQ], scale(k, 1),
                                                shift(k, 1), ALU.mult, ALU.add).then_inc(out_dve, 1)

            @block.tensor
            def _(pe):
                pe.wait_ge(scaled, T)
                for k in range(KC):
                    if k >= 4:
                        pe.wait_ge(out_dve if T == NT else out_act, k - 3)
                    for i in range(T):
                        mm = nc.tensor.transpose(ps[:, k % 4, i * P:(i + 1) * P], xn[:, i, k * P:(k + 1) * P], core.ident[:])
                    mm.then_inc(turned, 1)


def project(core, tag, groups, lo, route, act_out, dve_out, source=None):
    nc, ps = core.nc, core.ps
    hT = core.hT if source is None else source
    product, act_read, dve_read = core.sem(tag + "product"), core.sem(tag + "act_read"), core.sem(tag + "dve_read")
    flat = [(w, g) for w, gs in enumerate(groups) for g in gs]
    used_at = [sum(len(gs) for gs in groups[:w + 1]) for w in range(len(groups))]
    ways = [route(n) for n in range(len(flat))]
    acts = [sum("a" in w for w in ways[:n + 1]) for n in range(len(flat))]
    dves = [sum("d" in w for w in ways[:n + 1]) for n in range(len(flat))]
    with core.phase() as block:
        @block.sync
        def _(sp):
            core.load_ahead(sp, lo, product, used_at)

        @block.tensor
        def _(pe):
            for n, (wi, (kind, i, n0, n1)) in enumerate(flat):
                if n >= 8:
                    pe.wait_ge(dve_read if "d" in ways[n - 8] else act_read, (dves if "d" in ways[n - 8] else acts)[n - 8])
                w = core.weight(pe, lo + wi)
                for k in range(KC):
                    if kind == "tokens":
                        lhs, rhs = hT[:, k, i * P:(i + 1) * P], w[:, k, n0:n1]
                    else:
                        lhs, rhs = w[:, k, i * P:(i + 1) * P], hT[:, k, n0:n1]
                    mm = nc.tensor.matmul(ps[:, n % 8, 0:n1 - n0], lhs, rhs, start=(k == 0), stop=(k == KC - 1))
                mm.then_inc(product, 1)

        @block.scalar
        def _(act):
            for n, (wi, g) in enumerate(flat):
                if "a" in ways[n]:
                    act.wait_ge(product, n + 1)
                    act_out(act, n, wi, g, ps[:, n % 8, 0:g[3] - g[2]], lambda m: act.wait_ge(dve_read, dves[m])).then_inc(act_read, 1)

        @block.vector
        def _(dve):
            for n, (wi, g) in enumerate(flat):
                if "d" in ways[n]:
                    dve.wait_ge(product, n + 1)
                    if "a" in ways[n]:
                        dve.wait_ge(act_read, acts[n])
                    dve_out(dve, n, wi, g, ps[:, n % 8, 0:g[3] - g[2]]).then_inc(dve_read, 1)



def turn(core, tag, blocks, outs_per_bank=4):
    nc, ps = core.nc, core.ps
    turned, act_read, dve_read = core.sem(tag + "turned"), core.sem(tag + "act_read"), core.sem(tag + "dve_read")
    with core.phase() as block:
        @block.tensor
        def _(pe):
            for n, (ins, out, scale) in enumerate(blocks):
                if n >= 8:
                    pe.wait_ge(act_read if n % 2 == 0 else dve_read, (n - 8) // 2 + 1)
                at = 0
                for i in ins:
                    w, h = i.shape[0], i.shape[1]
                    mm = nc.tensor.transpose(ps[0:h, n % 8, at:at + w], i, core.ident[0:w, 0:w])
                    at += w
                mm.then_inc(turned, 1)

        @block.scalar
        def _(act):
            for n, (ins, out, scale) in enumerate(blocks):
                if n % 2 == 0:
                    act.wait_ge(turned, n + 1)
                    w = len(ins) * ins[0].shape[0]
                    nc.scalar.activation(out, ps[0:out.shape[0], n % 8, 0:w], ACT.Copy if scale is None else ACT.Identity,
                                         scale=1.0 if scale is None else scale).then_inc(act_read, 1)

        @block.vector
        def _(dve):
            for n, (ins, out, scale) in enumerate(blocks):
                if n % 2 == 1:
                    dve.wait_ge(turned, n + 1)
                    src = ps[0:out.shape[0], n % 8, 0:len(ins) * ins[0].shape[0]]
                    if scale is None:
                        nc.vector.tensor_copy(out, src).then_inc(dve_read, 1)
                    else:
                        nc.vector.tensor_scalar(out, src, scale, None, ALU.mult).then_inc(dve_read, 1)


def down(core, tag, lo, source, tiles, n_weights, finish_act=None, finish_dve=None, first_bank=0):
    nc, ps = core.nc, core.ps
    summed = core.sem(tag + "summed")
    done = core.sem(tag + "weight_done")
    with core.phase() as block:
        @block.sync
        def _(sp):
            core.load_ahead(sp, lo, done, range(1, n_weights + 1))

        @block.tensor
        def _(pe):
            for wi in range(n_weights):
                w = core.weight(pe, lo + wi)
                for i in range(tiles):
                    for j in range(2):
                        for k in range(4):
                            mm = nc.tensor.matmul(ps[:, first_bank + 2 * i + j, :],
                                                  source[:, wi * 4 + k, i * P:(i + 1) * P], w[:, k, j * BANK:(j + 1) * BANK],
                                                  start=(wi == 0 and k == 0), stop=(wi == n_weights - 1 and k == 3))
                mm.then_inc(done, 1)

        if finish_act:
            @block.scalar
            def _(act):
                act.wait_ge(done, n_weights)
                finish_act(act)

        if finish_dve:
            @block.vector
            def _(dve):
                dve.wait_ge(done, n_weights)
                finish_dve(dve)


def gated_residual(core, tag, tiles, gate_of):
    nc, ps, x = core.nc, core.ps, core.x
    with ExitStack() as c:
        sq = c.enter_context(nc.sbuf_tensor(tag + "sq", [P, BANK], F32))
        st = c.enter_context(nc.sbuf_tensor(tag + "st", [P, 4, 2 * NT], F32))
        t = c.enter_context(nc.sbuf_tensor(tag + "t", [P, NT * 2, BANK], F32))
        squares, meaned, rooted = core.sem(tag + "squares"), core.sem(tag + "meaned"), core.sem(tag + "rooted")
        n = 2 * tiles
        with core.phase() as block:
            @block.scalar
            def _(act):
                for b in range(n):
                    core.act_chain(act, nc.scalar.activation(sq[:], ps[:, b, :], ACT.Square, accum_out=st[:, 0, b:b + 1]))
                nc.scalar.activation(sq[:, 0:1], st[:, 0, 0:1], ACT.Copy).then_inc(squares, 1)
                act.wait_ge(meaned, 1)
                nc.scalar.activation(st[:, 2, 0:tiles], st[:, 2, 0:tiles], ACT.Sqrt).then_inc(rooted, 1)

            @block.vector
            def _(dve):
                link = core.dve_chain
                dve.wait_ge(squares, 1)
                pairs = st[:, 0, 0:n].rearrange("p (t j) -> p t j", j=2)
                link(dve, nc.vector.tensor_tensor(st[:, 1, 0:tiles], pairs[:, :, 0], pairs[:, :, 1], ALU.add))
                nc.vector.tensor_scalar(st[:, 2, 0:tiles], st[:, 1, 0:tiles], 1.0 / D, EPS, ALU.mult, ALU.add).then_inc(meaned, 1)
                dve.wait_ge(rooted, 1)
                link(dve, nc.vector.reciprocal(st[:, 3, 0:tiles], st[:, 2, 0:tiles]))
                for i in range(tiles):
                    for j in range(2):
                        last = nc.vector.scalar_tensor_tensor(out=t[:, 2 * i + j, :], in0=ps[:, 2 * i + j, :],
                                                              scalar=st[:, 3, i:i + 1],
                                                              in1=core.ga[:, gate_of[i], j * BANK:(j + 1) * BANK],
                                                              op0=ALU.mult, op1=ALU.mult)
                link(dve, last)
                for i in range(tiles):
                    last = nc.vector.tensor_tensor(x[:, i, :], x[:, i, :],
                                                   t[:, 2 * i:2 * i + 2, :].rearrange("p j n -> p (j n)"), ALU.add)
                link(dve, last)


def side_taps(core, dve, dst, src, w0, w2):
    nc = core.nc
    S = dst.shape[1] // SEQ
    d, u = (z.rearrange("p (s t) -> p s t", s=S) for z in (dst, src))
    core.dve_chain(dve, nc.vector.scalar_tensor_tensor(out=d[:, :, 1:], in0=u[:, :, :SEQ - 1], scalar=w0,
                                                       in1=d[:, :, 1:], op0=ALU.mult, op1=ALU.add))
    return nc.vector.scalar_tensor_tensor(out=d[:, :, :SEQ - 1], in0=u[:, :, 1:], scalar=w2,
                                          in1=d[:, :, :SEQ - 1], op0=ALU.mult, op1=ALU.add)


def softmax_attention(core, tag, jobs, scale):
    nc, ps = core.nc, core.ps
    with ExitStack() as c:
        sb = lambda name, shape: c.enter_context(nc.sbuf_tensor(tag + name, shape, F32))
        nkm = max(j["k"].shape[1] for j in jobs)
        masked = sb("masked", [P, 2, nkm])
        prob = sb("prob", [P, 2, nkm])
        probT = sb("probT", [P, 2, nkm])
        N = len(jobs)
        top, ntop, tot, rec = (sb(n, [P, N]) for n in ("top", "ntop", "tot", "rec"))
        scores, turned, values = core.sem(tag + "scores"), core.sem(tag + "turned"), core.sem(tag + "values")
        negmax, exped, prob_ready = core.sem(tag + "negmax"), core.sem(tag + "exped"), core.sem(tag + "prob_ready")
        probT_ready, out_done = core.sem(tag + "probT_ready"), core.sem(tag + "out_done")
        with core.phase() as block:
            @block.tensor
            def _(pe):
                for j in range(N + 2):
                    if j < N:
                        if j >= 2:
                            pe.wait_ge(exped, j - 1)
                        k = jobs[j]["k"]
                        nc.tensor.matmul(ps[:, j % 2, 0:k.shape[1]], jobs[j]["q"], k, start=True, stop=True).then_inc(scores, 1)
                    if 1 <= j <= N:
                        i = j - 1
                        pe.wait_ge(prob_ready, i + 1)
                        if i >= 2:
                            pe.wait_ge(probT_ready, i - 1)
                        for b in range(jobs[i]["k"].shape[1] // P):
                            mm = nc.tensor.transpose(ps[:, 2 + i % 2, b * P:(b + 1) * P], prob[:, i % 2, b * P:(b + 1) * P], core.ident[:])
                        mm.then_inc(turned, 1)
                    if j >= 2:
                        i = j - 2
                        pe.wait_ge(probT_ready, i + 1)
                        if i >= 2:
                            pe.wait_ge(out_done, i - 1)
                        vs = jobs[i]["v"]
                        for b, v in enumerate(vs):
                            pt = probT[:, i % 2, b * P:(b + 1) * P]
                            dv = v.shape[1]
                            if jobs[i]["feat"]:
                                o, lhs, rhs = ps[0:dv, 4 + i % 2, 0:P], v, pt
                            else:
                                o, lhs, rhs = ps[:, 4 + i % 2, 0:dv], pt, v
                            mm = nc.tensor.matmul(o, lhs, rhs, start=(b == 0), stop=(b == len(vs) - 1))
                        mm.then_inc(values, 1)

            @block.scalar
            def _(act):
                for j in range(N + 1):
                    if j < N:
                        act.wait_ge(negmax, j + 1)
                        if j >= 2:
                            act.wait_ge(turned, j - 1)
                        nk = jobs[j]["k"].shape[1]
                        src = masked[:, j % 2, 0:nk] if jobs[j]["mask"] is not None else ps[:, j % 2, 0:nk]
                        nc.scalar.activation(prob[:, j % 2, 0:nk], src, ACT.Exp, bias=ntop[:, j:j + 1], scale=scale,
                                             accum_out=tot[:, j:j + 1]).then_inc(exped, 1)
                    if j >= 1:
                        i = j - 1
                        act.wait_ge(turned, i + 1)
                        if i >= 2:
                            act.wait_ge(values, i - 1)
                        nk = jobs[i]["k"].shape[1]
                        nc.scalar.activation(probT[:, i % 2, 0:nk], ps[:, 2 + i % 2, 0:nk], ACT.Copy).then_inc(probT_ready, 1)

            @block.vector
            def _(dve):
                link = core.dve_chain
                for j in range(N + 3):
                    if j < N:
                        dve.wait_ge(scores, j + 1)
                        if j >= 2:
                            dve.wait_ge(exped, j - 1)
                        nk = jobs[j]["k"].shape[1]
                        if jobs[j]["mask"] is not None:
                            link(dve, nc.vector.tensor_tensor_reduce(masked[:, j % 2, 0:nk], ps[:, j % 2, 0:nk], jobs[j]["mask"],
                                                                     1.0, NEG, ALU.add, ALU.max, top[:, j:j + 1]))
                        else:
                            link(dve, nc.vector.tensor_reduce(top[:, j:j + 1], ps[:, j % 2, 0:nk], AX.X, ALU.max))
                        nc.vector.tensor_scalar(ntop[:, j:j + 1], top[:, j:j + 1], -scale, None, ALU.mult).then_inc(negmax, 1)
                    if j >= 1 and j - 1 < N:
                        i = j - 1
                        dve.wait_ge(exped, i + 1)
                        nk = jobs[i]["k"].shape[1]
                        link(dve, nc.vector.reciprocal(rec[:, i:i + 1], tot[:, i:i + 1]))
                        nc.vector.tensor_scalar(prob[:, i % 2, 0:nk], prob[:, i % 2, 0:nk], rec[:, i:i + 1], None, ALU.mult).then_inc(prob_ready, 1)
                    if j >= 3:
                        i = j - 3
                        dve.wait_ge(values, i + 1)
                        dv = jobs[i]["v"][0].shape[1]
                        if jobs[i]["feat"]:
                            nc.vector.tensor_tensor(jobs[i]["out"], ps[0:dv, 4 + i % 2, 0:P], jobs[i]["gate"], ALU.mult).then_inc(out_done, 1)
                        else:
                            nc.vector.tensor_copy(jobs[i]["out"], ps[:, 4 + i % 2, 0:dv]).then_inc(out_done, 1)


def rope(core, dve, x, tab, tmp, heads, width, halves=1):
    nc, link = core.nc, core.dve_chain
    w, h = halves * width, width // 2
    cos = tab[:, 0:w].unsqueeze(1).broadcast_to([P, heads, w])
    t1, t2 = tmp[:, 0, 0:heads * w].rearrange("p (a b) -> p a b", a=heads), tmp[:, 1, 0:heads * w].rearrange("p (a b) -> p a b", a=heads)
    nc.vector.tensor_tensor(t1, x, cos, ALU.mult)
    for a in range(halves):
        for first, second in ((0, h), (h, 0)):
            o = a * width
            s = tab[:, w + o + first:w + o + first + h].unsqueeze(1).broadcast_to([P, heads, h])
            last = nc.vector.tensor_tensor(t2[:, :, o + first:o + first + h], x[:, :, o + second:o + second + h], s, ALU.mult)
    link(dve, last)
    link(dve, nc.vector.tensor_tensor(x, t1, t2, ALU.add))


def even_layer(core):
    nc, a, ps = core.nc, core.a, core.ps
    mod = core.mod
    normed(core, "en_", range(NT), lambda k, s: mod[:, 0, 1, k, s:s + 1], lambda k, s: mod[:, 0, 0, k, s:s + 1])
    with ExitStack() as layer:
        mixT = layer.enter_context(nc.sbuf_tensor("mixT", [P, 16, 2 * SEQ], F32))
        even_attention(core, mixT)
        hyena(core, mixT)
        down(core, "eo_", core.first["e_out"], mixT, NT, 4)
    gated_residual(core, "er_", NT, [0, 0, 1, 1])


def even_attention(core, mixT):
    nc, a, ps = core.nc, core.a, core.ps
    first = core.first
    with ExitStack() as c:
        sb = lambda name, shape: c.enter_context(nc.sbuf_tensor(name, shape, F32))
        NH = HEADS + KVH
        v = sb("ea_v", [P, NT, KVH * DH])
        qkT = sb("ea_qkT", [P, NH, 2 * SEQ])
        with ExitStack() as c2:
            qk = c2.enter_context(nc.sbuf_tensor("ea_qk", [P, NT, NH * DH], F32))

            def take(copy):
                def out(eng, n, wi, g, src, dve_out=None):
                    t = g[1]
                    if wi < 2:
                        return copy(qk[:, t, wi * 512:(wi + 1) * 512], src)
                    return copy(qk[:, t, 1024:1280] if g[2] == 0 else v[:, t, :], src)
                return out
            groups = [[("tokens", t, 0, 512) for t in range(NT)]] * 2 + \
                     [[("tokens", t, h * 256, h * 256 + 256) for t in range(NT) for h in range(2)]]
            project(core, "eqkv_", groups, first["e_qkv"], lambda n: "ad"[n % 2],
                    take(lambda o, i: nc.scalar.activation(o, i, ACT.Copy)), take(nc.vector.tensor_copy))
            project(core, "ega_", [[("features", m, 0, 512) for m in range(4)]] * 2, first["e_gatt"], lambda n: "a",
                    lambda act, n, wi, g, src, w: nc.scalar.activation(mixT[:, 8 + n, :], src, ACT.Silu), None)

            tab = c2.enter_context(nc.sbuf_tensor("ea_rope", [P, LT, 256], F32))
            gains = c2.enter_context(nc.sbuf_tensor("ea_gains", [P, 2, DH], F32))
            tmp = c2.enter_context(nc.sbuf_tensor("ea_tmp", [P, 2, NH * DH], F32))
            st = c2.enter_context(nc.sbuf_tensor("ea_st", [P, 3, NT * NH], F32))
            tabs_in, meaned, rooted = core.expect_tables(3), core.sem("ea_meaned"), core.sem("ea_rooted")
            with core.phase() as block:
                @block.gpsimd
                def _(pool):
                    pool.dma_start(tab[:], a["rope_e"].rearrange("(t p) n -> p t n", p=P)).then_inc(core.tables_in, 16)
                    pool.dma_start(gains[:, 0, :], row_bcast(a, "q_norm")).then_inc(core.tables_in, 16)
                    pool.dma_start(gains[:, 1, :], row_bcast(a, "k_norm")).then_inc(core.tables_in, 16)

                @block.scalar
                def _(act):
                    act.wait_ge(meaned, 1)
                    nc.scalar.activation(st[:, 1, :], st[:, 1, :], ACT.Sqrt).then_inc(rooted, 1)

                @block.vector
                def _(dve):
                    link = core.dve_chain
                    for t in range(NT):
                        sq = tmp[:, t % 2, :]
                        link(dve, nc.vector.tensor_tensor(sq, qk[:, t, :], qk[:, t, :], ALU.mult))
                        link(dve, nc.vector.tensor_reduce(st[:, 0, t * NH:(t + 1) * NH], sq.rearrange("p (h d) -> p h d", h=NH),
                                                          AX.X, ALU.add))
                    nc.vector.tensor_scalar(st[:, 1, :], st[:, 0, :], 1.0 / DH, EPS, ALU.mult, ALU.add).then_inc(meaned, 1)
                    dve.wait_ge(rooted, 1)
                    link(dve, nc.vector.reciprocal(st[:, 2, :], st[:, 1, :]))
                    dve.wait_ge(core.tables_in, tabs_in)
                    for t in range(NT):
                        x = qk[:, t, :].rearrange("p (h d) -> p h d", h=NH)
                        r = st[:, 2, t * NH:(t + 1) * NH].unsqueeze(2).broadcast_to([P, NH, DH])
                        link(dve, nc.vector.tensor_tensor(x, x, r, ALU.mult))
                        nc.vector.tensor_tensor(x[:, 0:HEADS], x[:, 0:HEADS], gains[:, 0:1, :].broadcast_to([P, HEADS, DH]), ALU.mult)
                        link(dve, nc.vector.tensor_tensor(x[:, HEADS:], x[:, HEADS:], gains[:, 1:2, :].broadcast_to([P, KVH, DH]), ALU.mult))
                        if t < LT:
                            rope(core, dve, x, tab[:, t, :], tmp, NH, 64, 2)
            turn(core, "ea_t_", [([qk[:, t, h * DH:(h + 1) * DH] for t in range(NT)], qkT[:, h, :], None) for h in range(NH)])
        jobs = []
        for h in range(HEADS):
            g = h // (HEADS // KVH)
            for t in range(NT):
                k0 = 0 if t < LT else SEQ
                jobs.append(dict(q=qkT[:, h, t * P:(t + 1) * P], k=qkT[:, HEADS + g, k0:2 * SEQ], mask=None, feat=True,
                                 v=[v[:, b, g * DH:(g + 1) * DH] for b in range(k0 // P, NT)],
                                 out=mixT[:, 8 + h, t * P:(t + 1) * P], gate=mixT[:, 8 + h, t * P:(t + 1) * P]))
        softmax_attention(core, "ea_", jobs, DH ** -0.5)


def hyena(core, mixT):
    nc, a, ps = core.nc, core.a, core.ps
    first, col = core.first, core.col
    NTT = 4
    with ExitStack() as c:
        sb = lambda name, shape, c=c: c.enter_context(nc.sbuf_tensor(name, shape, F32))
        gT = sb("hy_gT", [P, KC, 2 * SEQ])
        x0T = sb("hy_x0T", [P, KC, 2 * SEQ])
        with ExitStack() as c2:
            tmp = c2.enter_context(nc.sbuf_tensor("hy_tmp", [P, 2, 2 * SEQ], F32))
            feats = [("features", m, 0, 512) for m in range(4)]

            def conv(tag, name, chan0, dst, after=None, own_tmp=False):
                def act_out(act, n, wi, g, src, dve_done):
                    if own_tmp and n >= 2:
                        dve_done(n - 2)
                    ch = chan0 + n
                    return nc.scalar.activation(dst(n), src, ACT.Identity, scale=col("e_cw1", ch), bias=col("e_cb", ch))

                def dve_out(dve, n, wi, g, src):
                    ch = chan0 + n
                    last = side_taps(core, dve, dst(n), src, col("e_cw0", ch), col("e_cw2", ch))
                    if after:
                        core.dve_chain(dve, last)
                        last = after(n)
                    return last
                project(core, tag, [feats] * 2, first[name], lambda n: "ad", act_out, dve_out)

            conv("hx1_", "e_x1", 8, lambda n: gT[:, n, :])
            conv("hv_", "e_v", 16, lambda n: tmp[:, n % 2, :],
                 lambda n: nc.vector.tensor_tensor(gT[:, n, :], gT[:, n, :], tmp[:, n % 2, :], ALU.mult), own_tmp=True)
            conv("hx0_", "e_x0", 0, lambda n: x0T[:, n, :])

            def silu_tmp(act, n, wi, g, src, dve_done):
                if n >= 2:
                    dve_done(n - 2)
                return nc.scalar.activation(tmp[:, n % 2, :], src, ACT.Silu)
            project(core, "hgh_", [feats] * 2, first["e_ghy"], lambda n: "ad", silu_tmp,
                    lambda dve, n, wi, g, src: nc.vector.tensor_tensor(x0T[:, n, :], x0T[:, n, :], tmp[:, n % 2, :], ALU.mult))

        F = sb("hy_F", [P, 5, HY])
        snorm = sb("hy_norm", [P, KC])
        dft = sb("hy_dft", [P, NTT, 2 * SEQ])
        tabs_in = core.expect_tables(7)
        gtok = core.hT[:].rearrange("p k t -> p (k t)").rearrange("p (t d) -> p t d", t=NT)
        with ExitStack() as c2:
            sb2 = lambda name, shape: c2.enter_context(nc.sbuf_tensor(name, shape, F32))
            filt = mixT[:, 0:KC, :].rearrange("p k t -> p (k t)").rearrange("p (t d) -> p t d", t=NTT)
            scratch = core.hT[:].rearrange("p k t -> p (k t)")
            zt = sb2("hy_zt", [33, SEQ])
            w1, w2 = sb2("hy_w1", [33, 64]), sb2("hy_w2", [64, 64])
            w3 = scratch[0:64, 0:2 * HY]
            decay = scratch[:, 2 * HY:4 * HY].rearrange("p (t d) -> p t d", t=2)
            ones = sb2("hy_ones", [P, NTT])
            hd = sb2("hy_hd", [64, 4, SEQ])
            dense, sined, arg_ready = core.sem("hy_dense"), core.sem("hy_sined"), core.sem("hy_arg_ready")
            filt_out = core.sem("hy_filt_out")
            TWO_PI_HI = float(np.float32(6.28125))
            TWO_PI_LO = float(2 * math.pi - 6.28125)
            MAGIC = 12582912.0
            with core.phase() as block:
                @block.gpsimd
                def _(pool):
                    for dst, src in ((zt[:], a["z_t"]), (w1[:], a["e_filt_w1"][0]), (w2[:], a["e_filt_w2"][0]),
                                     (w3, a["e_filt_w3"][0]), (decay, a["decay"].rearrange("(t p) n -> p t n", p=P)),
                                     (ones[:], a["tap_ones"]),
                                     (dft[:], a["dft"].rearrange("(t p) n -> p t n", p=P))):
                        pool.dma_start(dst, src).then_inc(core.tables_in, 16)

                @block.tensor
                def _(pe):
                    pe.wait_ge(core.tables_in, tabs_in)
                    nc.tensor.matmul(ps[0:64, 0, 0:SEQ], w1[:], zt[:], start=True, stop=True).then_inc(dense, 1)
                    pe.wait_ge(sined, 1)
                    nc.tensor.matmul(ps[0:64, 1, 0:SEQ], w2[:], hd[:, 3, :], start=True, stop=True).then_inc(dense, 1)
                    pe.wait_ge(sined, 2)
                    for n in range(8):
                        side, t, j = n // 4, n // 2 % 2, n % 2
                        if n >= 6:
                            pe.wait_ge(filt_out, n - 5)
                        nc.tensor.matmul(ps[:, 2 + n % 6, :], hd[:, 3, t * P:(t + 1) * P],
                                         w3[:, side * HY + j * BANK:side * HY + (j + 1) * BANK], start=True, stop=True).then_inc(dense, 1)

                @block.scalar
                def _(act):
                    for i in range(2):
                        act.wait_ge(arg_ready, i + 1)
                        nc.scalar.activation(hd[:, 3, :], hd[:, 2, :], ACT.Sin).then_inc(sined, 1)

                @block.vector
                def _(dve):
                    link = core.dve_chain
                    for i in range(2):
                        dve.wait_ge(dense, i + 1)
                        link(dve, nc.vector.tensor_scalar(hd[:, 0, :], ps[0:64, i, 0:SEQ], core.col(f"f_b{i + 1}")[0:64],
                                                          core.col("f_fr")[0:64], ALU.add, ALU.mult))
                        link(dve, nc.vector.tensor_scalar(hd[:, 1, :], hd[:, 0, :], float(1 / (2 * math.pi)), None, ALU.mult))
                        link(dve, nc.vector.tensor_scalar(hd[:, 1, :], hd[:, 1, :], MAGIC, None, ALU.add))
                        link(dve, nc.vector.tensor_scalar(hd[:, 1, :], hd[:, 1, :], MAGIC, None, ALU.subtract))
                        link(dve, nc.vector.scalar_tensor_tensor(out=hd[:, 0, :], in0=hd[:, 1, :], scalar=-TWO_PI_HI,
                                                                 in1=hd[:, 0, :], op0=ALU.mult, op1=ALU.add))
                        link(dve, nc.vector.scalar_tensor_tensor(out=hd[:, 0, :], in0=hd[:, 1, :], scalar=-TWO_PI_LO,
                                                                 in1=hd[:, 0, :], op0=ALU.mult, op1=ALU.add))
                        nc.vector.tensor_scalar(hd[:, 2, :], hd[:, 0, :], math.pi - 1e-6, -math.pi + 1e-6, ALU.min, ALU.max).then_inc(arg_ready, 1)
                    for n in range(8):
                        side, t, j = n // 4, n // 2 % 2, n % 2
                        dve.wait_ge(dense, n + 3)
                        nc.vector.tensor_tensor(filt[:, side * 2 + t, j * BANK:(j + 1) * BANK], ps[:, 2 + n % 6, :],
                                                decay[:, t, j * BANK:(j + 1) * BANK], ALU.mult).then_inc(filt_out, 1)
            absd, summed, F_done, F_out_dve = (core.sem(n) for n in ("hy_absd", "hy_summed", "hy_F_done", "hy_F_out_dve"))
            absf = c2.enter_context(nc.sbuf_tensor("hy_abs", [P, NTT, BANK], F32))
            with core.phase() as block:
                @block.scalar
                def _(act):
                    for j in range(2):
                        if j:
                            act.wait_ge(summed, 1)
                        for t in range(NTT):
                            core.act_chain(act, nc.scalar.activation(absf[:, t, :], filt[:, t, j * BANK:(j + 1) * BANK], ACT.Abs))
                        nc.scalar.activation(core.small[:, 1:2], core.ident[:, 0:1], ACT.Copy).then_inc(absd, 1)

                @block.tensor
                def _(pe):
                    for j in range(2):
                        pe.wait_ge(absd, j + 1)
                        for ch in range(4):
                            for t in range(NTT):
                                mm = nc.tensor.matmul(ps[:, 0, 4 * j + ch:4 * j + ch + 1], absf[:, t, ch * P:(ch + 1) * P],
                                                      ones[:, t:t + 1], start=(t == 0), stop=(t == NTT - 1))
                        mm.then_inc(summed, 1)
                    for n in range(8):
                        f, j = n // 2, n % 2
                        if n >= 7:
                            pe.wait_ge(F_out_dve, 1)
                        for t in range(NTT):
                            mm = nc.tensor.matmul(ps[:, 1 + n % 7, :], dft[:, t, f * P:(f + 1) * P],
                                                  filt[:, t, j * BANK:(j + 1) * BANK], start=(t == 0), stop=(t == NTT - 1))
                        mm.then_inc(F_done, 1)

                @block.vector
                def _(dve):
                    link = core.dve_chain
                    for n in range(8):
                        f, j = n // 2, n % 2
                        dve.wait_ge(F_done, n + 1)
                        nc.vector.tensor_copy(F[:, f, j * BANK:(j + 1) * BANK], ps[:, 1 + n % 7, :]).then_inc(F_out_dve, 1)
                    dve.wait_ge(F_out_dve, 8)
                    link(dve, nc.vector.tensor_copy(F[:, 4, :], F[:, 0, :]))
                    link(dve, nc.vector.tensor_copy(F[0:1, 4, :], F[0:1, 2, :]))
                    link(dve, nc.vector.memset(F[0:1, 2, :], 0.0))
                    dve.wait_ge(summed, 2)
                    link(dve, nc.vector.reciprocal(snorm[:], ps[:, 0, 0:KC]))
        turn(core, "hy_t_", [([gT[:, 4 * q + i, t * P:(t + 1) * P] for i in range(4)],
                              gtok[:, t, q * BANK:(q + 1) * BANK], None) for t in range(NT) for q in range(2)])
        Y = sb("hy_Y", [P, 4, BANK])
        T2 = sb("hy_T2", [P, 2, BANK])
        idft = sb("hy_idft", [P, NTT, SEQ])
        y1 = sb("hy_y1", [P, 2, SEQ])
        inv_in = core.expect_tables(1)
        spect, Y_ready, back, mixed = (core.sem(n) for n in ("hy_spect", "hy_Y_ready", "hy_back", "hy_mixed"))
        rounds = [(j, s) for j in range(2) for s in range(2)]
        with core.phase() as block:
            @block.gpsimd
            def _(pool):
                pool.dma_start(idft[:], a["idft"].rearrange("(t p) n -> p t n", p=P)).then_inc(core.tables_in, 16)

            @block.tensor
            def _(pe):
                pe.wait_ge(core.tables_in, inv_in)
                for r, (j, s) in enumerate(rounds):
                    if r:
                        pe.wait_ge(Y_ready, r)
                    for f in range(NTT):
                        for t in range(LT):
                            mm = nc.tensor.matmul(ps[:, f, :], dft[:, t, f * P:(f + 1) * P],
                                                  gtok[:, s * LT + t, j * BANK:(j + 1) * BANK], start=(t == 0), stop=(t == LT - 1))
                    mm.then_inc(spect, 1)
                    pe.wait_ge(Y_ready, r + 1)
                    for ch in range(4):
                        if r:
                            pe.wait_ge(mixed, 4 * (r - 1) + ch + 1)
                        for f in range(NTT):
                            mm = nc.tensor.matmul(ps[:, 4 + ch, 0:SEQ], Y[:, f, ch * P:(ch + 1) * P], idft[:, f, :],
                                                  start=(f == 0), stop=(f == NTT - 1))
                        mm.then_inc(back, 1)

            @block.vector
            def _(dve):
                link = core.dve_chain
                for r, (j, s) in enumerate(rounds):
                    dve.wait_ge(spect, r + 1)
                    if r:
                        dve.wait_ge(back, 4 * r)
                    cs = slice(j * BANK, (j + 1) * BANK)
                    for f in range(2):
                        nc.vector.tensor_tensor(Y[:, f, :], ps[:, f, :], F[:, f, cs], ALU.mult)
                        last = nc.vector.tensor_tensor(T2[:, f, :], ps[:, 2 + f, :], F[:, 2 + f, cs], ALU.mult)
                    link(dve, last)
                    link(dve, nc.vector.tensor_tensor(Y[:, 0:2, :], Y[:, 0:2, :], T2[:, 0:2, :], ALU.subtract))
                    for f in range(2):
                        nc.vector.tensor_tensor(Y[:, 2 + f, :], ps[:, f, :], F[:, 2 + f, cs], ALU.mult)
                        last = nc.vector.tensor_tensor(T2[:, f, :], ps[:, 2 + f, :], F[:, 4 if f == 0 else 1, cs], ALU.mult)
                    link(dve, last)
                    link(dve, nc.vector.tensor_tensor(Y[:, 2:4, :], Y[:, 2:4, :], T2[:, 0:2, :], ALU.add))
                    nc.vector.tensor_copy(core.small[:, 2:3], core.ident[:, 0:1]).then_inc(Y_ready, 1)
                    for ch in range(4):
                        k = 4 * j + ch
                        ss = slice(s * SEQ, (s + 1) * SEQ)
                        dve.wait_ge(back, 4 * r + ch + 1)
                        link(dve, nc.vector.tensor_scalar(y1[:, ch % 2, :], ps[:, 4 + ch, 0:SEQ], snorm[:, k:k + 1], None, ALU.mult))
                        link(dve, nc.vector.scalar_tensor_tensor(out=y1[:, ch % 2, :], in0=gT[:, k, ss], scalar=col("hy_bias", k),
                                                                 in1=y1[:, ch % 2, :], op0=ALU.mult, op1=ALU.add))
                        nc.vector.tensor_tensor(mixT[:, k, ss], y1[:, ch % 2, :], x0T[:, k, ss], ALU.mult).then_inc(mixed, 1)


def program(nc, a, out, n_phases, dump):
    with ExitStack() as ctx:
        core = Core(nc, a, ctx)
        setup(core)
        adaln(core)
        even_layer(core)
        if n_phases == "even":
            return finish_dump(core, out, core.x)
        odd_layer(core)
        if n_phases == "odd":
            return finish_dump(core, out, core.x)
        for l in range(DEPTH):
            block2(core, l)
            if n_phases == f"b{l}":
                return finish_dump(core, out, core.x)
        final(core, out)


def finish_dump(core, out, x):
    stored = core.stored
    with core.phase() as block:
        @block.sync
        def _(sp):
            sp.dma_start(out[0].rearrange("(t p) d -> p t d", p=P), x[:, 0:LT, :]).then_inc(stored, 16)
            sp.wait_ge(stored, 16)
            for s in range(SLOTS):
                last = max((v for i, v in enumerate(core.landed_at[:core.issued]) if i % SLOTS == s), default=0)
                sp.wait_ge(core.landed[s], last)


def mlstm_gates(core, aT, cumT, masks, select, g):
    nc, a, ps = core.nc, core.a, core.ps
    R = 40
    with ExitStack() as c:
        sb = lambda name, shape: c.enter_context(nc.sbuf_tensor("mg_" + name, shape, F32))
        wg = sb("w", [P, KC, 2, R])
        tot = sb("tot", [R, 2])
        loaded = core.expect_tables(4)
        products, logged, abs_ready, cum_ready, turned = (
            core.sem("mg_" + n) for n in ("products", "logged", "abs_ready", "cum_ready", "turned"))
        I, FG, LF, T, CUM, ONE = range(6)
        lat, ctx = slice(0, SEQ), slice(SEQ, 2 * SEQ)
        with core.phase() as block:
            @block.gpsimd
            def _(pool):
                pool.dma_start(wg[:], a["gate_w"].rearrange("p (k i r) -> p k i r", k=KC, i=2)).then_inc(core.tables_in, 16)
                pool.dma_start(select, a["select"]).then_inc(core.tables_in, 16)
                for d, name in enumerate(("causal", "anti")):
                    pool.dma_start(masks[:, d, :, 0:SEQ], a[name].rearrange("(t p) n -> p t n", p=P)).then_inc(core.tables_in, 16)
                core.pool_chain(pool, nc.gpsimd.memset(masks[:, :, :, SEQ:2 * SEQ], 0.0))
                pool.wait_ge(core.tables_in, loaded)

            @block.tensor
            def _(pe):
                pe.wait_ge(core.tables_in, loaded)
                for i in range(2):
                    for k in range(KC):
                        mm = nc.tensor.matmul(ps[0:R, i, :], wg[:, k, i, :], core.hT[:, k, :], start=(k == 0), stop=(k == KC - 1))
                    mm.then_inc(products, 1)
                pe.wait_ge(cum_ready, 1)
                for t in range(LT):
                    mm = nc.tensor.transpose(ps[:, 2, t * R:(t + 1) * R], g[:, CUM, t * P:(t + 1) * P], core.ident[0:R, 0:R])
                mm.then_inc(turned, 1)

            @block.scalar
            def _(act):
                act.wait_ge(abs_ready, 1)
                core.act_chain(act, nc.scalar.activation(g[:, T, :], g[:, T, :], ACT.Exp, scale=-1.0))
                nc.scalar.activation(g[:, T, :], g[:, T, :], ACT.Ln, bias=1.0).then_inc(logged, 1)

            @block.vector
            def _(dve):
                link = core.dve_chain
                link(dve, nc.vector.memset(g[:, ONE, :], 1.0))
                dve.wait_ge(products, 2)
                nc.vector.tensor_scalar(g[:, I, :], ps[0:R, 0, :], core.col("gb_i")[0:R], None, ALU.add)
                link(dve, nc.vector.tensor_scalar(g[:, FG, :], ps[0:R, 1, :], core.col("gb_f")[0:R], None, ALU.add))
                nc.vector.tensor_scalar(g[:, LF, :], g[:, FG, :], 0.0, None, ALU.min)
                nc.vector.scalar_tensor_tensor(out=g[:, T, :], in0=g[:, FG, :], scalar=-1.0, in1=g[:, FG, :],
                                               op0=ALU.mult, op1=ALU.max).then_inc(abs_ready, 1)
                dve.wait_ge(logged, 1)
                link(dve, nc.vector.tensor_tensor(g[:, LF, :], g[:, LF, :], g[:, T, :], ALU.subtract))
                nc.vector.tensor_tensor_scan(g[:, CUM, lat], g[:, ONE, lat], g[:, LF, lat], 0.0, ALU.mult, ALU.add)
                link(dve, nc.vector.tensor_tensor_scan(g[:, CUM, ctx], g[:, ONE, ctx], g[:, LF, ctx], 0.0, ALU.mult, ALU.add))
                end_lat, end_ctx = g[:, CUM, SEQ - 1:SEQ], g[:, CUM, 2 * SEQ - 1:2 * SEQ]
                nc.vector.tensor_copy(tot[:, 0:1], end_ctx)
                link(dve, nc.vector.tensor_tensor(tot[:, 1:2], end_ctx, end_lat, ALU.add))
                link(dve, nc.vector.tensor_scalar(g[0:8, CUM, lat], g[0:8, CUM, lat], tot[0:8, 0:1], None, ALU.add))
                B = slice(32, R)
                for n, part in ((1, lat), (0, ctx)):
                    link(dve, nc.vector.tensor_scalar(g[B, CUM, part], g[B, CUM, part], -1.0, tot[B, n:n + 1], ALU.mult, ALU.add))
                link(dve, nc.vector.tensor_tensor(g[B, CUM, :], g[B, CUM, :], g[B, LF, :], ALU.add))
                nc.vector.tensor_tensor(aT[:], g[:, I, :], g[:, CUM, :], ALU.subtract).then_inc(cum_ready, 1)
                dve.wait_ge(turned, 1)
                link(dve, nc.vector.tensor_copy(cumT[:], ps[:, 2, 0:LT * R].rearrange("p (t r) -> p t r", t=LT)))


def mlstm(core, qT, kT, v, o_gate, aT, cumT, masks, select, hs):
    nc, ps = core.nc, core.ps
    scale = ML_QK ** -0.5
    with ExitStack() as c:
        sb = lambda name, shape: c.enter_context(nc.sbuf_tensor("ml_" + name, shape, F32))
        Dm = sb("decay", [P, 2, 2, 2 * SEQ])
        WT = sb("WT", [P, 2, 2 * SEQ])
        jobs = [(h, t) for h in range(ML_H) for t in range(LT)]
        N = len(jobs)
        mu, nmu, flr, den, rec = (sb(n, [P, 2 * N]) for n in ("mu", "nmu", "flr", "den", "rec"))
        sems = {n: core.sem("ml_" + n) for n in ("scores", "spread", "negmax", "decayed", "floored", "mixed",
                                                 "turned", "WT_ready", "values", "out_done")}
        sc, spread, negmax, decayed, floored, mixed, turned, WT_ready, values, out_done = sems.values()
        with core.phase() as block:
            @block.tensor
            def _(pe):
                for j in range(N + 2):
                    if j < N:
                        h, t = jobs[j]
                        if j >= 2:
                            pe.wait_ge(mixed, j - 1)
                        nc.tensor.matmul(ps[:, j % 2, :], qT[:, h, t * P:(t + 1) * P], kT[:, h, :], start=True, stop=True).then_inc(sc, 1)
                        for d in range(2):
                            if j >= 1:
                                pe.wait_ge(negmax, 2 * (j - 1) + d + 1)
                            nc.tensor.matmul(ps[:, 2 + d, :], select[:, (8 * d + h) * P:(8 * d + h + 1) * P], aT[:],
                                             start=True, stop=True).then_inc(spread, 1)
                    if 1 <= j <= N:
                        i = j - 1
                        pe.wait_ge(mixed, i + 1)
                        if i >= 2:
                            pe.wait_ge(WT_ready, i - 1)
                        for b in range(4):
                            mm = nc.tensor.transpose(ps[:, 4 + i % 2, b * P:(b + 1) * P], Dm[:, i % 2, 0, b * P:(b + 1) * P], core.ident[:])
                        mm.then_inc(turned, 1)
                    if j >= 2:
                        i = j - 2
                        h, t = jobs[i]
                        pe.wait_ge(WT_ready, i + 1)
                        if i >= 2:
                            pe.wait_ge(out_done, i - 1)
                        for b in range(4):
                            mm = nc.tensor.matmul(ps[:, 6 + i % 2, 0:ML_V], WT[:, i % 2, b * P:(b + 1) * P],
                                                  v[:, b, h * ML_V:(h + 1) * ML_V], start=(b == 0), stop=(b == 3))
                        mm.then_inc(values, 1)

            @block.scalar
            def _(act):
                for j in range(N + 1):
                    if j < N:
                        h, t = jobs[j]
                        for d in range(2):
                            u = 2 * j + d
                            act.wait_ge(negmax, u + 1)
                            nc.scalar.activation(Dm[:, j % 2, d, :], Dm[:, j % 2, d, :], ACT.Exp, bias=nmu[:, u:u + 1]).then_inc(decayed, 1)
                            r = 32 * d + h
                            nc.scalar.activation(flr[:, u:u + 1], cumT[:, t, r:r + 1], ACT.Exp, bias=nmu[:, u:u + 1], scale=-1.0).then_inc(floored, 1)
                    if j >= 1:
                        i = j - 1
                        act.wait_ge(turned, i + 1)
                        if i >= 2:
                            act.wait_ge(values, i - 1)
                        nc.scalar.activation(WT[:, i % 2, :], ps[:, 4 + i % 2, :], ACT.Copy).then_inc(WT_ready, 1)

            @block.vector
            def _(dve):
                link = core.dve_chain
                for j in range(N + 3):
                    if j < N:
                        h, t = jobs[j]
                        if j >= 2:
                            dve.wait_ge(turned, j - 1)
                        for d in range(2):
                            u = 2 * j + d
                            dve.wait_ge(spread, u + 1)
                            link(dve, nc.vector.tensor_tensor_reduce(Dm[:, j % 2, d, :], ps[:, 2 + d, :], masks[:, d, t, :],
                                                                     1.0, 0.0, ALU.add, ALU.max, mu[:, u:u + 1]))
                            nc.vector.tensor_scalar(nmu[:, u:u + 1], mu[:, u:u + 1], -1.0, None, ALU.mult).then_inc(negmax, 1)
                    if 1 <= j <= N:
                        i = j - 1
                        dve.wait_ge(sc, i + 1)
                        for d in range(2):
                            u = 2 * i + d
                            dve.wait_ge(decayed, u + 1)
                            link(dve, nc.vector.tensor_tensor_reduce(Dm[:, i % 2, d, :], ps[:, i % 2, :], Dm[:, i % 2, d, :],
                                                                     scale, 0.0, ALU.mult, ALU.add, den[:, u:u + 1]))
                            dve.wait_ge(floored, u + 1)
                            nd = den[:, u:u + 1]
                            link(dve, nc.vector.scalar_tensor_tensor(out=rec[:, u:u + 1], in0=nd, scalar=-1.0, in1=nd, op0=ALU.mult, op1=ALU.max))
                            link(dve, nc.vector.tensor_tensor(nd, rec[:, u:u + 1], flr[:, u:u + 1], ALU.max))
                            link(dve, nc.vector.reciprocal(rec[:, u:u + 1], den[:, u:u + 1]))
                        u = 2 * i
                        link(dve, nc.vector.tensor_scalar(Dm[:, i % 2, 0, :], Dm[:, i % 2, 0, :], rec[:, u:u + 1], None, ALU.mult))
                        nc.vector.scalar_tensor_tensor(out=Dm[:, i % 2, 0, :], in0=Dm[:, i % 2, 1, :], scalar=rec[:, u + 1:u + 2],
                                                       in1=Dm[:, i % 2, 0, :], op0=ALU.mult, op1=ALU.add).then_inc(mixed, 1)
                    if j >= 3:
                        i = j - 3
                        h, t = jobs[i]
                        dve.wait_ge(values, i + 1)
                        cs = slice(h * ML_V, (h + 1) * ML_V)
                        nc.vector.tensor_tensor(hs[:, t, cs], ps[:, 6 + i % 2, 0:ML_V], o_gate[:, t, cs], ALU.mult).then_inc(out_done, 1)


def odd_layer(core):
    nc, a, ps = core.nc, core.a, core.ps
    mod, first, col = core.mod, core.first, core.col
    normed(core, "on_", range(NT), lambda k, s: mod[:, 1, 1, k, s:s + 1], lambda k, s: mod[:, 1, 0, k, s:s + 1])
    with ExitStack() as c:
        sb = lambda name, shape: c.enter_context(nc.sbuf_tensor(name, shape, F32))
        v = sb("od_v", [P, NT, ML_H * ML_V])
        o_gate = sb("od_o", [P, LT, ML_H * ML_V])
        z_gate = sb("od_z", [P, LT, ML_H * ML_V])
        with ExitStack() as c2:
            sb2 = lambda name, shape: c2.enter_context(nc.sbuf_tensor(name, shape, F32))
            qT = sb2("od_qT", [P, ML_H, SEQ])
            kT = sb2("od_kT", [P, ML_H, 2 * SEQ])

            def conv(tag, name, chan0, dst, tokens):
                def act_out(act, n, wi, g, src, dve_done):
                    ch = chan0 + n
                    return nc.scalar.activation(dst[:, n, :], src, ACT.Identity, scale=col("o_cw1", ch), bias=col("o_cb", ch))

                def dve_out(dve, n, wi, g, src):
                    ch = chan0 + n
                    return side_taps(core, dve, dst[:, n, :], src, col("o_cw0", ch), col("o_cw2", ch))
                project(core, tag, [[("features", m, 0, tokens) for m in range(4)]] * 2, first[name], lambda n: "ad", act_out, dve_out)

            conv("oq_", "o_q", 0, qT, SEQ)
            conv("ok_", "o_k", 8, kT, 2 * SEQ)

            def plain(dst):
                return (lambda act, n, wi, g, src, w: nc.scalar.activation(dst[:, g[1], wi * BANK:(wi + 1) * BANK], src, ACT.Copy),
                        lambda dve, n, wi, g, src: nc.vector.tensor_copy(dst[:, g[1], wi * BANK:(wi + 1) * BANK], src))

            def through(dst, func):
                return (lambda act, n, wi, g, src, w: nc.scalar.activation(dst[:, g[1], wi * BANK:(wi + 1) * BANK], src, func), None)
            project(core, "ov_", [[("tokens", t, 0, BANK) for t in range(NT)]] * 4, first["o_v"], lambda n: "ad"[n % 2], *plain(v))
            select = core.x[0:40, LT:NT, :].rearrange("p t d -> p (t d)")
            scratch = o_gate[0:40].rearrange("p t d -> p (t d)")[:, 0:12 * SEQ].rearrange("p (n t) -> p n t", n=6)
            aT = sb2("od_aT", [40, 2 * SEQ])
            cumT = sb2("od_cumT", [P, LT, 40])
            masks = sb2("od_masks", [P, 2, LT, 2 * SEQ])
            mlstm_gates(core, aT, cumT, masks, select, scratch)
            project(core, "oo_", [[("tokens", t, 0, BANK) for t in range(LT)]] * 4, first["o_o"], lambda n: "a", *through(o_gate, ACT.Sigmoid))
            project(core, "oz_", [[("tokens", t, 0, BANK) for t in range(LT)]] * 4, first["o_z"], lambda n: "a", *through(z_gate, ACT.Silu))
            with core.phase() as block:
                @block.scalar
                def _(act):
                    for h in range(0, ML_H, 4):
                        last = nc.scalar.activation(qT[:, h:h + 4, :], qT[:, h:h + 4, :], ACT.Silu)
                    core.act_chain(act, last)
                    for h in range(0, ML_H, 4):
                        last = nc.scalar.activation(kT[:, h:h + 4, :], kT[:, h:h + 4, :], ACT.Silu)
                    core.act_chain(act, last)
            hs = core.hT[:].rearrange("p k t -> p (k t)").rearrange("p (t d) -> p t d", t=LT)
            mlstm(core, qT, kT, v, o_gate, aT, cumT, masks, select, hs)
        flat_v = v[:].rearrange("p t d -> p (t d)")
        hsT = flat_v[:, 0:4096].rearrange("p (k t) -> p k t", k=16)
        sq = flat_v[:, 4096:6144]
        gain = flat_v[:, 6144:8192]
        st = sb("od_st", [P, 3, LT * ML_H])
        gain_in, meaned, rooted = core.expect_tables(1), core.sem("od_meaned"), core.sem("od_rooted")
        with core.phase() as block:
            @block.gpsimd
            def _(pool):
                pool.dma_start(gain, row_bcast(a, "head_norm")).then_inc(core.tables_in, 16)

            @block.scalar
            def _(act):
                act.wait_ge(meaned, 1)
                nc.scalar.activation(st[:, 1, :], st[:, 1, :], ACT.Sqrt).then_inc(rooted, 1)

            @block.vector
            def _(dve):
                link = core.dve_chain
                for t in range(LT):
                    link(dve, nc.vector.tensor_tensor(sq, hs[:, t, :], hs[:, t, :], ALU.mult))
                    link(dve, nc.vector.tensor_reduce(st[:, 0, t * ML_H:(t + 1) * ML_H], sq.rearrange("p (h d) -> p h d", h=ML_H), AX.X, ALU.add))
                nc.vector.tensor_scalar(st[:, 1, :], st[:, 0, :], 1.0 / ML_V, EPS, ALU.mult, ALU.add).then_inc(meaned, 1)
                dve.wait_ge(core.tables_in, gain_in)
                for t in range(LT):
                    link(dve, nc.vector.tensor_tensor(z_gate[:, t, :], z_gate[:, t, :], gain, ALU.mult))
                    link(dve, nc.vector.tensor_tensor(hs[:, t, :], hs[:, t, :], z_gate[:, t, :], ALU.mult))
                dve.wait_ge(rooted, 1)
                link(dve, nc.vector.reciprocal(st[:, 2, :], st[:, 1, :]))
                for t in range(LT):
                    x = hs[:, t, :].rearrange("p (h d) -> p h d", h=ML_H)
                    r = st[:, 2, t * ML_H:(t + 1) * ML_H].unsqueeze(2).broadcast_to([P, ML_H, ML_V])
                    link(dve, nc.vector.tensor_tensor(x, x, r, ALU.mult))
        turn(core, "od_t_", [([hs[:, t, k * P:(k + 1) * P] for k in (2 * q, 2 * q + 1) for t in range(LT)],
                              hsT[:, 2 * q:2 * q + 2, :].rearrange("p k t -> p (k t)"), None) for q in range(8)])
        down(core, "od_d_", first["o_out"], hsT, LT, 4)
    gated_residual(core, "or_", LT, [2, 2])


def retention(core, tag, rT, rv, decay, out):
    nc, ps = core.nc, core.ps
    with ExitStack() as c:
        sc = c.enter_context(nc.sbuf_tensor(tag + "sc", [P, 2, SEQ], F32))
        scT = c.enter_context(nc.sbuf_tensor(tag + "scT", [P, 2, SEQ], F32))
        scores, decayed, turned, back, values, out_done = (core.sem(tag + n) for n in ("scores", "decayed", "turned", "back", "values", "out_done"))
        jobs = [(h, t) for h in range(RET_H) for t in range(LT)]
        N = len(jobs)
        with core.phase() as block:
            @block.tensor
            def _(pe):
                for j in range(N + 2):
                    if j < N:
                        h, t = jobs[j]
                        nk = (t + 1) * P
                        if j >= 2:
                            pe.wait_ge(decayed, j - 1)
                        nc.tensor.matmul(ps[:, j % 2, 0:nk], rT[0:RET_QK, h, t * P:(t + 1) * P], rT[0:RET_QK, RET_H + h, 0:nk],
                                         start=True, stop=True).then_inc(scores, 1)
                    if 1 <= j <= N:
                        i = j - 1
                        pe.wait_ge(decayed, i + 1)
                        if i >= 2:
                            pe.wait_ge(back, i - 1)
                        for b in range(jobs[i][1] + 1):
                            mm = nc.tensor.transpose(ps[:, 2 + i % 2, b * P:(b + 1) * P], sc[:, i % 2, b * P:(b + 1) * P], core.ident[:])
                        mm.then_inc(turned, 1)
                    if j >= 2:
                        i = j - 2
                        h, t = jobs[i]
                        pe.wait_ge(back, i + 1)
                        if i >= 2:
                            pe.wait_ge(out_done, i - 1)
                        for b in range(t + 1):
                            mm = nc.tensor.matmul(ps[:, 4 + i % 2, 0:RET_V], scT[:, i % 2, b * P:(b + 1) * P],
                                                  rv[:, b, h * RET_V:(h + 1) * RET_V], start=(b == 0), stop=(b == t))
                        mm.then_inc(values, 1)

            @block.scalar
            def _(act):
                for i in range(N):
                    nk = (jobs[i][1] + 1) * P
                    act.wait_ge(turned, i + 1)
                    if i >= 2:
                        act.wait_ge(values, i - 1)
                    nc.scalar.activation(scT[:, i % 2, 0:nk], ps[:, 2 + i % 2, 0:nk], ACT.Copy).then_inc(back, 1)

            @block.vector
            def _(dve):
                for j in range(N + 2):
                    if j < N:
                        h, t = jobs[j]
                        nk = (t + 1) * P
                        dve.wait_ge(scores, j + 1)
                        if j >= 2:
                            dve.wait_ge(turned, j - 1)
                        nc.vector.tensor_tensor(sc[:, j % 2, 0:nk], ps[:, j % 2, 0:nk], decay[:, t, h * SEQ:h * SEQ + nk], ALU.mult).then_inc(decayed, 1)
                    if j >= 2:
                        h, t = jobs[j - 2]
                        dve.wait_ge(values, j - 1)
                        nc.vector.tensor_copy(out(t, h), ps[:, 4 + j % 2, 0:RET_V]).then_inc(out_done, 1)


def block2(core, l):
    nc, a, ps = core.nc, core.a, core.ps
    first, col, x = core.first, core.col, core.x
    T = f"b{l}_"
    normed(core, T + "n_", range(LT), lambda k, s: col(f"an{l}", k))
    with ExitStack() as c:
        sb = lambda name, shape, c=c: c.enter_context(nc.sbuf_tensor(T + name, shape, F32))
        gates = sb("gates", [P, LT, 3 * D])
        rg = sb("rg", [P, LT, 512])
        oa = sb("oa", [P, LT, 1536])
        with ExitStack() as c2:
            sb2 = lambda name, shape, c=c2: c.enter_context(nc.sbuf_tensor(T + name, shape, F32))
            lr = sb2("low", [P, LT, IN2_FIRST])
            moba = sb2("moba", [P, LT, 1536])
            rqk = sb2("rqk", [P, LT, 512])
            rv = sb2("rv", [P, LT, 512])
            ukv = sb2("ukv", [P, LT, 1024])
            mT = sb2("mT", [96, 2 * 8, SEQ])
            rT = sb2("rT", [64, 8, SEQ])
            toks = lambda w: [("tokens", t, 0, w) for t in range(LT)]

            def copies(dst_of):
                return (lambda act, n, wi, g, src, w: nc.scalar.activation(dst_of(wi, g[1]), src, ACT.Copy),
                        lambda dve, n, wi, g, src: nc.vector.tensor_copy(dst_of(wi, g[1]), src))

            def where(wi, t):
                if wi == 0:
                    return lr[:, t, :]
                if wi <= 3:
                    return moba[:, t, (wi - 1) * BANK:wi * BANK]
                return rqk[:, t, :] if wi == 4 else rv[:, t, :]
            project(core, T + "p_", [toks(IN2_FIRST)] + [toks(BANK)] * 5, first[f"in{l}a"], lambda n: "ad"[n % 2], *copies(where))
            project(core, T + "rg_", [toks(BANK)], first[f"in{l}"] + 5, lambda n: "a",
                    lambda act, n, wi, g, src, w: nc.scalar.activation(rg[:, g[1], :], src, ACT.Silu), None)
            project(core, T + "g_", [toks(BANK)] * 6, first[f"in{l}"] + 6, lambda n: "a",
                    lambda act, n, wi, g, src, w: nc.scalar.activation(gates[:, g[1], wi * BANK:(wi + 1) * BANK], src, ACT.Sigmoid), None)
            bT = core.hT[0:64].rearrange("p k t -> p (k t)").rearrange("p (h t) -> p h t", h=16)
            with ExitStack() as c3:
                sb3 = lambda name, shape: sb2(name, shape, c3)
                tabs = sb3("tabs", [P, LT, 224])
                tmp = sb3("ropetmp", [P, 2, 512])
                lowT = sb3("lowT", [P, 3, SEQ])
                uq = x[:, LT:NT, 0:768]
                kk = sb3("kk", [P, LT, 8, 96])
                st = sb3("st", [P, 3, 4])
                tabs_in = core.expect_tables(3)
                meaned, rooted = core.sem(T + "meaned"), core.sem(T + "rooted")
                o_moba, o_ret = 64, 96
                with core.phase() as block:
                    @block.gpsimd
                    def _(pool):
                        at = 0
                        for name, w in (("rope_mla", 64), ("rope_moba", 32), ("rope_ret", 128)):
                            pool.dma_start(tabs[:, :, at:at + w], a[name].rearrange("(t p) n -> p t n", p=P)).then_inc(core.tables_in, 16)
                            at += w

                    @block.scalar
                    def _(act):
                        act.wait_ge(meaned, 1)
                        nc.scalar.activation(st[:, 1, :], st[:, 1, :], ACT.Sqrt).then_inc(rooted, 1)

                    @block.vector
                    def _(dve):
                        link = core.dve_chain
                        parts = [(t, i, lo, w) for t in range(LT) for i, (lo, w) in enumerate(((0, MLA_Q), (MLA_Q, MLA_KV)))]
                        for t, i, lo, w in parts:
                            link(dve, nc.vector.tensor_tensor_reduce(tmp[:, 0, 0:w], lr[:, t, lo:lo + w], lr[:, t, lo:lo + w], 1.0 / w, EPS,
                                                                     ALU.mult, ALU.add, st[:, 1, 2 * t + i:2 * t + i + 1]))
                        nc.vector.tensor_copy(st[:, 0, 0:1], st[:, 1, 0:1]).then_inc(meaned, 1)
                        dve.wait_ge(core.tables_in, tabs_in)
                        for t in range(LT):
                            rope(core, dve, moba[:, t, 0:1024].rearrange("p (h d) -> p h d", h=16)[:, :, 0:16],
                                 tabs[:, t, o_moba:o_moba + 32], tmp, 16, 16)
                            rope(core, dve, rqk[:, t, :].rearrange("p (h d) -> p h d", h=8), tabs[:, t, o_ret:o_ret + 128], tmp, 8, 64)
                            rope(core, dve, lr[:, t, 384:416].unsqueeze(1), tabs[:, t, 0:64], tmp, 1, 32)
                        dve.wait_ge(rooted, 1)
                        link(dve, nc.vector.reciprocal(st[:, 2, :], st[:, 1, :]))
                        for t, i, lo, w in parts:
                            link(dve, nc.vector.tensor_scalar(lr[:, t, lo:lo + w], lr[:, t, lo:lo + w], st[:, 2, 2 * t + i:2 * t + i + 1], None, ALU.mult))
                turn(core, T + "lt_", [([lr[:, t, k * P:(k + 1) * P] for t in range(LT)], lowT[:, k, :],
                                        col(f"qn{l}", k) if k < 2 else col(f"kvn{l}")) for k in range(3)])
                up_done, up_act, up_dve = core.sem(T + "up_done"), core.sem(T + "up_act"), core.sem(T + "up_dve")
                wi = first[f"up{l}"]
                with core.phase() as block:
                    @block.sync
                    def _(sp):
                        core.load_ahead(sp, wi, up_done, [8])

                    @block.tensor
                    def _(pe):
                        wq, wkv = core.weight(pe, wi, 0), core.weight(pe, wi, 1)
                        for t in range(LT):
                            for j in range(2):
                                for k in range(2):
                                    mm = nc.tensor.matmul(ps[:, 2 * t + j, 0:384], lowT[:, k, t * P:(t + 1) * P],
                                                          wq[:, k, j * 384:(j + 1) * 384], start=(k == 0), stop=(k == 1))
                                mm.then_inc(up_done, 1)
                        for t in range(LT):
                            for j in range(2):
                                nc.tensor.matmul(ps[:, 4 + 2 * t + j, :], lowT[:, 2, t * P:(t + 1) * P],
                                                 wkv[:, 0, j * BANK:(j + 1) * BANK], start=True, stop=True).then_inc(up_done, 1)

                    @block.scalar
                    def _(act):
                        for t in range(LT):
                            for j in range(2):
                                act.wait_ge(up_done, 4 + 2 * t + j + 1)
                                last = nc.scalar.activation(ukv[:, t, j * BANK:(j + 1) * BANK], ps[:, 4 + 2 * t + j, :], ACT.Copy)
                            core.act_chain(act, last)
                            nc.scalar.activation(kk[:, t, :, 0:64], ukv[:, t, :].rearrange("p (h d) -> p h d", h=8)[:, :, 0:64], ACT.Copy).then_inc(up_act, 1)
                            core.act_chain(act, nc.scalar.activation(kk[:, t, :, 64:96], lr[:, t, 384:416].unsqueeze(1).broadcast_to([P, 8, 32]), ACT.Copy))

                    @block.vector
                    def _(dve):
                        for t in range(LT):
                            for j in range(2):
                                dve.wait_ge(up_done, 2 * t + j + 1)
                                last = nc.vector.tensor_copy(uq[:, t, j * 384:(j + 1) * 384], ps[:, 2 * t + j, 0:384])
                            core.dve_chain(dve, last)
                            rope(core, dve, uq[:, t, :].rearrange("p (h d) -> p h d", h=8)[:, :, 64:96], tabs[:, t, 0:64], tmp, 8, 32)
                flat = lambda z: z.rearrange("p h t -> p (h t)")
                blocks = []
                for h in range(0, 8, 2):
                    blocks.append(([uq[:, t, g * 96:(g + 1) * 96] for g in (h, h + 1) for t in range(LT)], flat(mT[:, h:h + 2, :]), None))
                    blocks.append(([kk[:, t, g, :] for g in (h, h + 1) for t in range(LT)], flat(mT[:, 8 + h:10 + h, :]), None))
                for h in range(0, 16, 2):
                    blocks.append(([moba[:, t, g * 64:(g + 1) * 64] for g in (h, h + 1) for t in range(LT)], flat(bT[:, h:h + 2, :]), None))
                for h in range(0, 8, 2):
                    blocks.append(([rqk[:, t, g * 64:(g + 1) * 64] for g in (h, h + 1) for t in range(LT)], flat(rT[:, h:h + 2, :]), None))
                turn(core, T + "t_", blocks)
            spare = x[:, LT:NT, :].rearrange("p t d -> p (t d)")
            causal = spare[:, 0:LT * SEQ].rearrange("p (t n) -> p t n", t=LT)
            gn = spare[:, 512:1536].rearrange("p (i n) -> p i n", i=2)
            decay = sb2("decay", [P, LT, RET_H * SEQ])
            tab_in = core.expect_tables(4)
            with core.phase() as block:
                @block.gpsimd
                def _(pool):
                    pool.dma_start(causal, a["causal"].rearrange("(t p) n -> p t n", p=P)).then_inc(core.tables_in, 16)
                    pool.dma_start(decay[:], a["ret_decay"].rearrange("(t p) n -> p t n", p=P)).then_inc(core.tables_in, 16)
                    pool.dma_start(gn[:, 0, :], row_bcast(a, f"gn_w{l}")).then_inc(core.tables_in, 16)
                    pool.dma_start(gn[:, 1, :], row_bcast(a, f"gn_b{l}")).then_inc(core.tables_in, 16)
                    pool.wait_ge(core.tables_in, tab_in)
            for name, qk, off, vsrc, scale in (("ma_", mT, 0, lambda b, h: ukv[:, b, h * 128 + 64:h * 128 + 128], 96 ** -0.5),
                                               ("mo_", bT, 512, lambda b, h: moba[:, b, 1024 + h * 64:1088 + h * 64], 64 ** -0.5)):
                jobs = [dict(q=qk[:, h, t * P:(t + 1) * P], k=qk[:, 8 + h, 0:(t + 1) * P], mask=causal[:, t, 0:(t + 1) * P],
                             feat=False, v=[vsrc(b, h) for b in range(t + 1)], out=oa[:, t, off + h * 64:off + (h + 1) * 64])
                        for h in range(8) for t in range(LT)]
                softmax_attention(core, T + name, jobs, scale)
            retention(core, T + "re_", rT, rv, decay, lambda t, h: oa[:, t, 1024 + h * P:1024 + (h + 1) * P])
            st = sb2("gst", [P, 4, LT * RET_H])
            sq = sb2("gsq", [P, 512])
            meaned, rooted = core.sem(T + "gn_meaned"), core.sem(T + "gn_rooted")
            with core.phase() as block:
                @block.scalar
                def _(act):
                    act.wait_ge(meaned, 1)
                    nc.scalar.activation(st[:, 2, :], st[:, 2, :], ACT.Sqrt).then_inc(rooted, 1)

                @block.vector
                def _(dve):
                    link = core.dve_chain
                    heads = lambda t: oa[:, t, 1024:1536].rearrange("p (h d) -> p h d", h=RET_H)
                    s4 = lambda n, t: st[:, n, t * RET_H:(t + 1) * RET_H]
                    wide = lambda z: z.unsqueeze(2).broadcast_to([P, RET_H, RET_V])
                    for t in range(LT):
                        link(dve, nc.vector.tensor_reduce(s4(0, t), heads(t), AX.X, ALU.add))
                        link(dve, nc.vector.tensor_scalar(s4(1, t), s4(0, t), 1.0 / RET_V, None, ALU.mult))
                        link(dve, nc.vector.tensor_tensor(heads(t), heads(t), wide(s4(1, t)), ALU.subtract))
                        link(dve, nc.vector.tensor_tensor(sq[:], oa[:, t, 1024:1536], oa[:, t, 1024:1536], ALU.mult))
                        link(dve, nc.vector.tensor_reduce(s4(0, t), sq[:].rearrange("p (h d) -> p h d", h=RET_H), AX.X, ALU.add))
                    nc.vector.tensor_scalar(st[:, 2, :], st[:, 0, :], 1.0 / RET_V, GN_EPS, ALU.mult, ALU.add).then_inc(meaned, 1)
                    dve.wait_ge(rooted, 1)
                    link(dve, nc.vector.reciprocal(st[:, 3, :], st[:, 2, :]))
                    for t in range(LT):
                        o = oa[:, t, 1024:1536]
                        link(dve, nc.vector.tensor_tensor(heads(t), heads(t), wide(s4(3, t)), ALU.mult))
                        link(dve, nc.vector.tensor_tensor(o, o, gn[:, 0, :], ALU.mult))
                        link(dve, nc.vector.tensor_tensor(o, o, gn[:, 1, :], ALU.add))
                        link(dve, nc.vector.tensor_tensor(o, o, rg[:, t, :], ALU.mult))
        oT = sb("oT", [P, 12, SEQ])
        merged = sb("merged", [P, LT, D])
        part = sb("part", [P, 2, BANK])
        turn(core, T + "ot_", [([oa[:, t, k * P:(k + 1) * P] for k in (2 * q, 2 * q + 1) for t in range(LT)],
                                oT[:, 2 * q:2 * q + 2, :].rearrange("p k t -> p (k t)"), None) for q in range(6)])
        b_done, b_read = core.sem(T + "branch_done"), core.sem(T + "branch_read")
        with core.phase() as block:
            @block.sync
            def _(sp):
                core.load_ahead(sp, first[f"b_mla{l}"], b_done, [4, 8, 12])

            @block.tensor
            def _(pe):
                for b in range(3):
                    w = core.weight(pe, first[f"b_mla{l}"] + b)
                    for t in range(LT):
                        for j in range(2):
                            n = 4 * b + 2 * t + j
                            if n >= 8:
                                pe.wait_ge(b_read, n - 7)
                            for k in range(4):
                                mm = nc.tensor.matmul(ps[:, n % 8, :], oT[:, 4 * b + k, t * P:(t + 1) * P],
                                                      w[:, k, j * BANK:(j + 1) * BANK], start=(k == 0), stop=(k == 3))
                            mm.then_inc(b_done, 1)

            @block.vector
            def _(dve):
                for n in range(12):
                    b, t, j = n // 4, n // 2 % 2, n % 2
                    dve.wait_ge(b_done, n + 1)
                    g = gates[:, t, b * D + j * BANK:b * D + (j + 1) * BANK]
                    m = merged[:, t, j * BANK:(j + 1) * BANK]
                    if b == 0:
                        nc.vector.tensor_tensor(m, ps[:, n % 8, :], g, ALU.mult).then_inc(b_read, 1)
                    else:
                        nc.vector.tensor_tensor(part[:, n % 2, :], ps[:, n % 8, :], g, ALU.mult).then_inc(b_read, 1)
                        dve.wait_ge(b_read, n + 1)
                        core.dve_chain(dve, nc.vector.tensor_tensor(m, m, part[:, n % 2, :], ALU.add))
        mTT = core.hT[:, :, 0:SEQ]
        turn(core, T + "mt_", [([merged[:, t, k * P:(k + 1) * P] for t in range(LT)], mTT[:, k, :], None) for k in range(KC)])
        down(core, T + "wo_", first[f"out{l}"], mTT, LT, 2)
    add_banks(core, T + "r1_")
    normed(core, T + "n2_", range(LT), lambda k, s: col(f"mn{l}", k))
    with ExitStack() as c:
        upT = c.enter_context(nc.sbuf_tensor(T + "upT", [P, D_FF // P, SEQ], F32))
        project(core, T + "mu_", [[("features", m, 0, SEQ) for m in range(4)]] * 8, first[f"mup{l}"], lambda n: "ad",
                lambda act, n, wi, g, src, w: nc.scalar.activation(upT[:, n, :], src, ACT.Relu),
                lambda dve, n, wi, g, src: nc.vector.tensor_tensor(upT[:, n, :], upT[:, n, :], upT[:, n, :], ALU.mult))
        down(core, T + "md_", first[f"mdn{l}"], upT, LT, 8)
    add_banks(core, T + "r2_")


def add_banks(core, tag):
    nc = core.nc
    with core.phase() as block:
        @block.vector
        def _(dve):
            for t in range(LT):
                for j in range(2):
                    xs = core.x[:, t, j * BANK:(j + 1) * BANK]
                    last = nc.vector.tensor_tensor(xs, xs, core.ps[:, 2 * t + j, :], ALU.add)
            core.dve_chain(dve, last)


def final(core, out):
    nc, a, x = core.nc, core.a, core.x
    with ExitStack() as c:
        sq = c.enter_context(nc.sbuf_tensor("f_sq", [P, D], F32))
        gain = c.enter_context(nc.sbuf_tensor("f_gain", [P, D], F32))
        st = c.enter_context(nc.sbuf_tensor("f_st", [P, 3, LT], F32))
        gain_in = core.expect_tables(1)
        meaned, rooted, ready = (core.sem("f_" + n) for n in ("meaned", "rooted", "ready"))
        stored = core.stored
        with core.phase() as block:
            @block.gpsimd
            def _(pool):
                pool.dma_start(gain[:], row_bcast(a, "final")).then_inc(core.tables_in, 16)

            @block.scalar
            def _(act):
                act.wait_ge(meaned, 1)
                nc.scalar.activation(st[:, 1, :], st[:, 1, :], ACT.Sqrt).then_inc(rooted, 1)

            @block.vector
            def _(dve):
                link = core.dve_chain
                for t in range(LT):
                    link(dve, nc.vector.tensor_tensor_reduce(sq[:], x[:, t, :], x[:, t, :], 1.0 / D, EPS, ALU.mult, ALU.add, st[:, 1, t:t + 1]))
                nc.vector.tensor_copy(st[:, 0, 0:1], st[:, 1, 0:1]).then_inc(meaned, 1)
                dve.wait_ge(rooted, 1)
                link(dve, nc.vector.reciprocal(st[:, 2, :], st[:, 1, :]))
                dve.wait_ge(core.tables_in, gain_in)
                for t in range(LT):
                    nc.vector.scalar_tensor_tensor(out=x[:, t, :], in0=x[:, t, :], scalar=st[:, 2, t:t + 1], in1=gain[:],
                                                   op0=ALU.mult, op1=ALU.mult).then_inc(ready, 1)

            @block.sync
            def _(sp):
                for t in range(LT):
                    sp.wait_ge(ready, t + 1)
                    sp.dma_start(out[0, t * P:(t + 1) * P, :], x[:, t, :]).then_inc(stored, 16)
                sp.wait_ge(stored, 16 * LT)


INS = ['x', 'c', 'ctx', 'c_ctx', 'w_mod', 'b_mod', 'g_pre', 'g_post', 'e_w_in', 'e_conv_w', 'e_conv_b', 'e_filt_w1',
       'e_filt_b1', 'e_filt_freq', 'e_filt_w2', 'e_filt_b2', 'e_filt_w3', 'e_hy_bias', 'e_q_norm', 'e_k_norm',
       'e_w_out', 'o_w_in', 'o_conv_w', 'o_conv_b', 'o_gate_b', 'o_head_norm', 'o_w_out', 'attn_norm_2', 'w_in_2',
       'mla_q_norm_2', 'mla_kv_norm_2', 'mla_w_q_up_2', 'mla_w_kv_up_2', 'ret_gn_w_2', 'ret_gn_b_2',
       'w_branch_mla_2', 'w_branch_moba_2', 'w_branch_ret_2', 'w_out_2', 'mlp_norm_2', 'w_mlp_up_2',
       'w_mlp_down_2', 'final_norm_2']
DIRECT = ['x', 'ctx', 'w_mod', 'e_w_in', 'e_filt_w1', 'e_filt_w2', 'e_filt_w3', 'e_w_out', 'o_w_in', 'o_w_out',
          'w_in_2', 'mla_w_q_up_2', 'mla_w_kv_up_2', 'w_branch_mla_2', 'w_branch_moba_2', 'w_branch_ret_2', 'w_out_2',
          'w_mlp_up_2', 'w_mlp_down_2']


def feature_columns(p):
    out = np.zeros((P, NCOL), np.float32)

    def put(name, v):
        v = np.asarray(v).reshape(-1, P)
        at = COL_AT[name]
        out[:, at:at + v.shape[0]] = v.T

    def put_short(name, v, at_partition=0):
        out[at_partition:at_partition + len(v), COL_AT[name]] = v

    put("c", p["c"])
    put("c_ctx", p["c_ctx"])
    for l in range(DEPTH):
        put(f"b_sh{l}", p["b_mod"][l, 0:D])
        put(f"b_sc{l}", p["b_mod"][l, D:2 * D])
        put(f"g_pre{l}", p["g_pre"][l])
        put(f"an{l}", p["attn_norm_2"][l])
        put(f"mn{l}", p["mlp_norm_2"][l])
        put(f"qn{l}", p["mla_q_norm_2"][l])
        put(f"kvn{l}", p["mla_kv_norm_2"][l])
    for i in range(3):
        put(f"e_cw{i}", p["e_conv_w"][0, i])
        put(f"o_cw{i}", p["o_conv_w"][0, i])
    put("e_cb", p["e_conv_b"][0])
    put("o_cb", p["o_conv_b"][0])
    put("hy_bias", p["e_hy_bias"][0])
    put_short("f_b1", p["e_filt_b1"][0])
    put_short("f_b2", p["e_filt_b2"][0])
    put_short("f_fr", p["e_filt_freq"][0])
    gb = p["o_gate_b"][0]
    put_short("gb_i", gb[0:8])
    put_short("gb_f", gb[8:16])
    put_short("gb_i", gb[16:24], 32)
    put_short("gb_f", gb[24:32], 32)
    return out


def spread_rows(p):
    parts = {"b_ga0": p["b_mod"][0, 2 * D:], "b_ga1": p["b_mod"][1, 2 * D:], "g_post0": p["g_post"][0],
             "g_post1": p["g_post"][1], "q_norm": p["e_q_norm"][0], "k_norm": p["e_k_norm"][0],
             "head_norm": p["o_head_norm"][0], "gn_w0": p["ret_gn_w_2"][0], "gn_b0": p["ret_gn_b_2"][0],
             "gn_w1": p["ret_gn_w_2"][1], "gn_b1": p["ret_gn_b_2"][1], "final": p["final_norm_2"]}
    return np.concatenate([np.asarray(parts[k]).reshape(-1) for k in ROW_AT]).astype(np.float32)


def tables():
    out = {"ident": np.eye(P)}
    n = SEQ
    t = np.arange(2 * n)[:, None]
    f = np.arange(n)[None, :]
    cos = np.cos(2 * np.pi * ((t * f) % (2 * n)) / (2 * n))
    sin = -np.sin(2 * np.pi * ((t * f) % (2 * n)) / (2 * n))
    sin[:, 0] = (-1.0) ** t[:, 0]
    full = np.concatenate([cos, sin], 1)
    back_taps = full[(2 * n - np.arange(n)) % (2 * n)].copy()
    back_taps[0] = 0.0
    out["dft"] = np.concatenate([full[:n], back_taps], 0)
    inv = full[:n].T * (2.0 / (2 * n))
    inv[0] *= 0.5
    inv[n] *= 0.5
    out["idft"] = inv
    out["tap_ones"] = np.concatenate([np.ones(n), [0.0], np.ones(n - 1)]).reshape(4, P).T
    bands = np.linspace(1e-4, 15, 16, dtype=np.float32)
    ang = np.float32(2.0 * math.pi / n) * np.arange(n, dtype=np.float32)[:, None] * bands
    tt = np.linspace(0.0, 1.0, n, dtype=np.float32)[:, None]
    out["z_t"] = np.concatenate([tt, np.cos(ang), -np.sin(ang)], 1).T
    deltas = np.linspace(math.log(1e-2) / 1.5, math.log(1e-2) / 0.3, HY, dtype=np.float32)
    out["decay"] = np.exp(-tt * np.abs(deltas))

    def rot(pos, dim, inv_freq, reps):
        a = pos.astype(np.float32)[:, None] * inv_freq.astype(np.float32)
        return (np.tile(np.concatenate([np.cos(a), np.cos(a)], 1), (1, reps)),
                np.tile(np.concatenate([-np.sin(a), np.sin(a)], 1), (1, reps)))

    nf = DH // 4
    inv_freq = 10000.0 ** (-np.arange(nf) / nf)
    pos = np.arange(SEQ)
    c0, s0 = rot(pos // 64, 64, inv_freq, 1)
    c1, s1 = rot(pos % 64, 64, inv_freq, 1)
    out["rope_e"] = np.concatenate([c0, c1, s0, s1], 1)
    for name, dim, theta, reps in (("rope_mla", 32, 500000.0, 1), ("rope_moba", 16, 500000.0, 1), ("rope_ret", 64, 10000.0, 1)):
        cc, ss = rot(pos, dim, 1.0 / theta ** (np.arange(0, dim, 2) / dim), reps)
        out[name] = np.concatenate([cc, ss], 1)
    q, k = np.arange(SEQ)[:, None], np.arange(SEQ)[None, :]
    out["causal"] = np.where(k <= q, 0.0, NEG)
    out["anti"] = np.where(k >= q, 0.0, NEG)
    lg = np.log(1.0 - 2.0 ** (-5.0 - np.arange(RET_H)))
    out["ret_decay"] = np.concatenate([np.where(k <= q, np.exp(g * np.maximum(q - k, 0)), 0.0) for g in lg], 1) * RET_QK ** -0.5
    sel = np.zeros((40, 16, P))
    for d in range(2):
        for h in range(8):
            sel[32 * d + h, 8 * d + h] = 1.0
    out["select"] = sel.reshape(40, 16 * P)
    return {k2: np.ascontiguousarray(v, np.float32) for k2, v in out.items()}


def make(nc, arrays_shapes, n_phases=None, dump=None):
    a = {}
    for name, shape in arrays_shapes.items():
        a[name] = nc.dram_tensor(f"in_{name}", shape, F32, kind="ExternalInput").ap()
    out = nc.dram_tensor("out_0", (1, SEQ, D), F32, kind="ExternalOutput").ap()
    program(nc, a, out, n_phases, dump)
    return out


def host_arrays(p):
    arrays = {name: np.ascontiguousarray(p[name]) for name in DIRECT}
    arrays["cols"] = feature_columns(p)
    arrays["rows"] = spread_rows(p)
    g = p["o_w_in"][0][:, OD_G:].reshape(KC, P, 2, 2, 8)
    gate_w = np.zeros((P, KC, 2, 40), np.float32)
    gate_w[:, :, :, 0:8] = g[:, :, 0].transpose(1, 0, 2, 3)
    gate_w[:, :, :, 32:40] = g[:, :, 1].transpose(1, 0, 2, 3)
    arrays["gate_w"] = gate_w.reshape(P, KC * 80)
    arrays.update(tables())
    return arrays


def kernel(**inputs):
    import concourse.bacc as bacc
    from concourse.bass_utils import run_bass_kernel_spmd as run

    p = {k: np.asarray(v) for k, v in inputs.items()}
    arrays = host_arrays(p)
    nc = bacc.Bacc("TRN2", target_bir_lowering=False, num_devices=1)
    make(nc, {k: v.shape for k, v in arrays.items()})
    r = run(nc, [{f"in_{k}": v for k, v in arrays.items()}], core_ids=[0])
    return r.results[0]["out_0"]
```

```python
from contextlib import ExitStack, contextmanager
import math

import numpy as np
import concourse.bass as bass
from concourse import mybir

ALU = mybir.AluOpType
ACT = mybir.ActivationFunctionType
AX = mybir.AxisListType
F32 = mybir.dt.float32
F32R = mybir.dt.float32r

P = 128
D = 1024
KC = D // P
SEQ = 256
NT = 2 * SEQ // P
LT = SEQ // P
DEPTH = 2
EPS = 1e-6
GN_EPS = 1e-5
NEG = -1e30

HY = 1024
EV_XV, EV_GHY, EV_Q, EV_KV, EV_GATT = 0, 3072, 4096, 5120, 5632
HEADS, KVH, DH = 8, 2, 128
ML_H, ML_QK, ML_V = 8, 128, 256
OD_K, OD_V, OD_O, OD_Z, OD_G = 1024, 2048, 4096, 6144, 8192

MLA_Q, MLA_KV, MLA_R, MLA_N = 256, 128, 32, 64
IN2_FIRST = MLA_Q + MLA_KV + MLA_R
RET_H, RET_QK, RET_V = 4, 64, 128
D_FF = 4096

SLOTS = 3
BANK = 512

COL_AT = {}
_n = 0
for _name, _w in (("c", 8), ("c_ctx", 8), ("b_sh0", 8), ("b_sc0", 8), ("b_sh1", 8), ("b_sc1", 8),
                  ("g_pre0", 8), ("g_pre1", 8), ("e_cw0", 24), ("e_cw1", 24), ("e_cw2", 24), ("e_cb", 24),
                  ("hy_bias", 8), ("o_cw0", 16), ("o_cw1", 16), ("o_cw2", 16), ("o_cb", 16),
                  ("an0", 8), ("an1", 8), ("mn0", 8), ("mn1", 8), ("qn0", 2), ("qn1", 2), ("kvn0", 1), ("kvn1", 1),
                  ("f_b1", 1), ("f_b2", 1), ("f_fr", 1), ("gb_i", 1), ("gb_f", 1)):
    COL_AT[_name] = _n
    _n += _w
NCOL = _n

ROW_AT = {}
_n = 0
for _name, _w in (("b_ga0", D), ("b_ga1", D), ("g_post0", D), ("g_post1", D), ("q_norm", DH), ("k_norm", DH),
                  ("head_norm", 2048), ("gn_w0", 512), ("gn_b0", 512), ("gn_w1", 512), ("gn_b1", 512),
                  ("final", D)):
    ROW_AT[_name] = (_n, _w)
    _n += _w
NROW = _n


def weight_stream(a):
    items, first = [], {}

    def cols(name, w, starts, width=BANK):
        first[name] = len(items)
        for s in starts:
            items.append([(w[:, s:s + width].rearrange("(k p) n -> p k n", p=P), 0, KC, width)])

    def rows(name, w):
        first[name] = len(items)
        n = w.shape[0] // 512
        for i in range(n):
            items.append([(w[i * 512:(i + 1) * 512, :].rearrange("(k p) n -> p k n", p=P), 0, 4, D)])

    for l in range(DEPTH):
        cols(f"mod{l}", a["w_mod"][l], range(0, 3 * D, BANK))
    w = a["e_w_in"][0]
    cols("e_qkv", w, (EV_Q, EV_Q + 512, EV_KV))
    cols("e_gatt", w, (EV_GATT, EV_GATT + 512))
    cols("e_x1", w, (1024, 1536))
    cols("e_v", w, (2048, 2560))
    cols("e_x0", w, (0, 512))
    cols("e_ghy", w, (EV_GHY, EV_GHY + 512))
    rows("e_out", a["e_w_out"][0])
    w = a["o_w_in"][0]
    cols("o_q", w, (0, 512))
    cols("o_k", w, (OD_K, OD_K + 512))
    cols("o_v", w, range(OD_V, OD_O, BANK))
    cols("o_o", w, range(OD_O, OD_Z, BANK))
    cols("o_z", w, range(OD_Z, OD_G, BANK))
    rows("o_out", a["o_w_out"][0])
    for l in range(DEPTH):
        w = a["w_in_2"][l]
        cols(f"in{l}a", w, (0,), IN2_FIRST)
        cols(f"in{l}", w, range(IN2_FIRST, IN2_FIRST + 12 * BANK, BANK))
        first[f"up{l}"] = len(items)
        items.append([
            (a["mla_w_q_up_2"][l].rearrange("(k p) n -> p k n", p=P), 0, 2, 768),
            (a["mla_w_kv_up_2"][l].rearrange("(k p) n -> p k n", p=P), 1536, 1, 1024)])
        rows(f"b_mla{l}", a["w_branch_mla_2"][l])
        rows(f"b_moba{l}", a["w_branch_moba_2"][l])
        rows(f"b_ret{l}", a["w_branch_ret_2"][l])
        rows(f"out{l}", a["w_out_2"][l])
        cols(f"mup{l}", a["w_mlp_up_2"][l], range(0, D_FF, BANK))
        rows(f"mdn{l}", a["w_mlp_down_2"][l])
    return items, first


class Chain:

    def __init__(self, sem):
        self.sem, self.n = sem, 0

    def __call__(self, eng, ins):
        self.n += 1
        ins.then_inc(self.sem, 1)
        eng.wait_ge(self.sem, self.n)


class Core:

    def __init__(self, nc, a, ctx):
        self.nc, self.a, self.ctx = nc, a, ctx
        self.items, self.first = weight_stream(a)
        sb = lambda name, shape: ctx.enter_context(nc.sbuf_tensor(name, shape, F32))
        self.x = sb("x_res", [P, NT, D])
        self.hT = sb("hT", [P, KC, 2 * SEQ])
        self.ring = sb("weights", [P, SLOTS, 4096])
        self.cols = sb("cols", [P, NCOL])
        self.ident = sb("ident", [P, P])
        self.ga = sb("ga", [P, 3, D])
        self.mod = sb("mod", [P, 2, 2, KC, 2])
        self.small = sb("small", [P, 256])
        self.ps = ctx.enter_context(nc.psum_tensor("psum", [P, 8, BANK], F32))
        keep = lambda name: ctx.enter_context(nc.semaphore(name))
        self.tables_in, self.tables_n = keep("tables_in"), 0
        self.stored = keep("result_stored")
        self.lead_ready, self.split_ready, self.n_split = keep("weight_lead_ready"), keep("weight_split_ready"), 0
        self.landed = [keep(f"weight_landed{s}") for s in range(SLOTS)]
        self.dve_chain = Chain(keep("dve_step"))
        self.act_chain = Chain(keep("act_step"))
        self.pool_chain = Chain(keep("pool_step"))
        self.landed_at, total = [], [0] * SLOTS
        for i, pieces in enumerate(self.items):
            total[i % SLOTS] += 16 * len(pieces)
            self.landed_at.append(total[i % SLOTS])
        self.issued = 0
        self.fresh, self.old = ([], ExitStack()), ([], ExitStack())

    def expect_tables(self, n):
        self.tables_n += 16 * n
        return self.tables_n

    def sem(self, name):
        s = self.fresh[1].enter_context(self.nc.semaphore(name))
        self.fresh[0].append(s)
        return s

    @contextmanager
    def phase(self):
        old, self.old = self.old, self.fresh
        self.fresh = ([], ExitStack())
        with self.nc.Block() as block:
            if old[0]:
                @block.gpsimd
                def _(pool):
                    for s in old[0]:
                        pool.sem_clear(s)
            yield block
        old[1].close()

    def col(self, name, i=0, n=1):
        at = COL_AT[name] + i
        return self.cols[:, at:at + n]

    def load_weight(self, eng, i):
        self.issued = i + 1
        for src, at, k, n in self.items[i]:
            dst = self.ring[:, i % SLOTS, at:at + k * n].rearrange("p (k n) -> p k n", k=k)
            eng.dma_start(dst, src).then_inc(self.landed[i % SLOTS], 16)

    def load_ahead(self, eng, lo, used, values):
        for i, value in enumerate(values):
            if lo + i + SLOTS < len(self.items):
                eng.wait_ge(used, value)
                self.load_weight(eng, lo + i + SLOTS)

    def weight(self, eng, i, piece=0):
        eng.wait_ge(self.landed[i % SLOTS], self.landed_at[i])
        _, at, k, n = self.items[i][piece]
        return self.ring[:, i % SLOTS, at:at + k * n].rearrange("p (k n) -> p k n", k=k)


class Split:

    def __init__(self, nc, c, name, shape):
        self.nc = nc
        self.lead = c.enter_context(nc.sbuf_tensor(name + "_lead", shape, F32R))
        self.rest = c.enter_context(nc.sbuf_tensor(name + "_rest", shape, F32R))

    def take_lead(self, eng, at, src):
        return eng.tensor_copy(self.lead[at], src)

    def take_rest(self, eng, at, src):
        return eng.tensor_tensor(self.rest[at], src, self.lead[at].bitcast(F32), ALU.subtract)

    def parts(self, at):
        return self.lead[at], self.rest[at]


def split_matmul(nc, out, lhs, rhs, start, stop):
    for i, (l, r) in enumerate(((lhs[0], rhs[0]), (lhs[0], rhs[1]), (lhs[1], rhs[0]))):
        mm = nc.tensor.matmul(out, l, r, start=start and i == 0, stop=stop and i == 2)
    return mm


class SplitWeights:

    def __init__(self, core, c, tag, first, n, buffers=2):
        self.core, self.B = core, buffers
        self.units = [(first + i, h) for i in range(n) for h in range(2)]
        self.base = core.n_split
        core.n_split += len(self.units)
        self.buf = Split(core.nc, c, tag + "w", [P, buffers, 2048])

    def size(self, u):
        _, _, k, n = self.core.items[self.units[u][0]][0]
        return k // 2, n

    def raw(self, u):
        i, h = self.units[u]
        k, n = self.size(u)
        return self.core.ring[:, i % SLOTS, h * k * n:(h + 1) * k * n]

    def at(self, u):
        k, n = self.size(u)
        return np.s_[:, u % self.B, 0:k * n]

    def take_lead(self, eng, u):
        if u < len(self.units):
            i = self.units[u][0]
            eng.wait_ge(self.core.landed[i % SLOTS], self.core.landed_at[i])
            self.core.nc.scalar.activation(self.buf.lead[self.at(u)], self.raw(u), ACT.Copy).then_inc(self.core.lead_ready, 1)

    def take_rest(self, eng, u):
        if u < len(self.units):
            eng.wait_ge(self.core.lead_ready, self.base + u + 1)
            self.buf.take_rest(eng, self.at(u), self.raw(u)).then_inc(self.core.split_ready, 1)

    def prime(self, dve):
        for u in range(self.B - 1):
            i = self.units[u][0]
            dve.wait_ge(self.core.landed[i % SLOTS], self.core.landed_at[i])
            self.buf.take_lead(dve, self.at(u), self.raw(u)).then_inc(self.core.lead_ready, 1)
            self.take_rest(dve, u)

    def parts(self, pe, u):
        pe.wait_ge(self.core.split_ready, self.base + u + 1)
        return [z.rearrange("p (k n) -> p k n", k=self.size(u)[0]) for z in self.buf.parts(self.at(u))]

    def load_ahead(self, sp, u0, n):
        for u in range(u0 + 1, u0 + n, 2):
            i = self.units[u][0]
            if i + SLOTS < len(self.core.items):
                sp.wait_ge(self.core.split_ready, self.base + u + 1)
                self.core.load_weight(sp, i + SLOTS)


def setup(core):
    nc, a = core.nc, core.a
    loaded = core.sem("setup_loaded")
    with core.phase() as block:
        @block.sync
        def _(sp):
            sp.dma_start(core.cols[:], a["cols"]).then_inc(loaded, 16)
            sp.dma_start(core.ident[:], a["ident"]).then_inc(loaded, 16)
            for i in range(SLOTS):
                core.load_weight(sp, i)
            sp.wait_ge(loaded, 32)


def row_bcast(a, name):
    at, n = ROW_AT[name]
    return a["rows"][at:at + n].partition_broadcast(P)


def adaln(core):
    nc, a, ps = core.nc, core.a, core.ps
    with ExitStack() as c:
        sb = lambda name, shape: c.enter_context(nc.sbuf_tensor(name, shape, F32))
        cond = sb("cond", [P, KC, 2])
        rows = sb("mod_rows", [2, DEPTH, 3 * D])
        pick = sb("row_pick", [2, 2, P])
        brow = sb("gate_rows", [P, 4, D])
        rows_in = core.expect_tables(5)
        cond_ready, mod_done, row_out = core.sem("cond_ready"), core.sem("mod_done"), core.sem("mod_row_out")
        turned, spread, x_in = (core.sem(n) for n in ("mod_turned", "gate_spread", "x_in"))
        lo = core.first["mod0"]
        gates = [(0, 0), (0, 1), (1, 0)]
        with core.phase() as block:
            @block.sync
            def _(sp):
                core.load_ahead(sp, lo, mod_done, range(1, 13))

            @block.gpsimd
            def _(pool):
                pool.dma_start(pick[:], a["pick"].rearrange("p (s n) -> p s n", s=2)).then_inc(core.tables_in, 16)
                for i, name in enumerate(("b_ga0", "b_ga1", "g_post0", "g_post1")):
                    pool.dma_start(brow[:, i, :], row_bcast(a, name)).then_inc(core.tables_in, 16)

            @block.scalar
            def _(act):
                for s, name in enumerate(("c", "c_ctx")):
                    nc.scalar.activation(cond[:, :, s], core.col(name, 0, KC), ACT.Silu).then_inc(cond_ready, 1)
                act.dma_start(core.x[:, 0:LT, :], a["x"][0].rearrange("(t p) d -> p t d", p=P)).then_inc(x_in, 16)
                act.dma_start(core.x[:, LT:NT, :], a["ctx"][0].rearrange("(t p) d -> p t d", p=P)).then_inc(x_in, 16)
                act.wait_ge(x_in, 32)

            @block.tensor
            def _(pe):
                pe.wait_ge(cond_ready, 2)
                for i in range(6 * DEPTH):
                    if i >= 2:
                        pe.wait_ge(row_out, i - 1)
                    w = core.weight(pe, lo + i)
                    for k in range(KC):
                        mm = nc.tensor.matmul(ps[0:2, i % 2, :], cond[:, k, :], w[:, k, :], start=(k == 0), stop=(k == KC - 1))
                    mm.then_inc(mod_done, 1)
                pe.wait_ge(row_out, 12)
                for l in range(DEPTH):
                    for k in range(2 * KC):
                        o = (l * 2 * KC + k) * 2
                        mm = nc.tensor.transpose(ps[:, 2, o:o + 2], rows[:, l, k * P:(k + 1) * P], core.ident[0:2, 0:2])
                mm.then_inc(turned, 1)
                pe.wait_ge(core.tables_in, rows_in)
                for n in range(6):
                    l, s = gates[n // 2]
                    b = 3 + n if n < 5 else 0
                    nc.tensor.matmul(ps[:, b, :], pick[:, s, :], rows[:, l, 2 * D + n % 2 * BANK:2 * D + (n % 2 + 1) * BANK],
                                     start=True, stop=True).then_inc(spread, 1)

            @block.vector
            def _(dve):
                link = core.dve_chain
                for i in range(6 * DEPTH):
                    dve.wait_ge(mod_done, i + 1)
                    nc.vector.tensor_copy(rows[:, i // 6, i % 6 * BANK:(i % 6 + 1) * BANK], ps[0:2, i % 2, :]).then_inc(row_out, 1)
                dve.wait_ge(turned, 1)
                for l in range(DEPTH):
                    m = ps[:, 2, l * 32:(l + 1) * 32].rearrange("p (h k s) -> p h k s", h=2, s=2)
                    for s in range(2):
                        nc.vector.tensor_tensor(core.mod[:, l, 0, :, s], m[:, 0, :, s], core.col(f"b_sh{l}", 0, KC), ALU.add)
                        link(dve, nc.vector.tensor_tensor(core.mod[:, l, 1, :, s], m[:, 1, :, s], core.col(f"b_sc{l}", 0, KC), ALU.add))
                        last = nc.vector.scalar_tensor_tensor(
                            out=core.mod[:, l, 1, :, s], in0=core.mod[:, l, 1, :, s], scalar=1.0,
                            in1=core.col(f"g_pre{l}", 0, KC), op0=ALU.add, op1=ALU.mult)
                link(dve, last)
                for n in range(6):
                    l, j = gates[n // 2][0], n % 2
                    dve.wait_ge(spread, n + 1)
                    o = core.ga[:, n // 2, j * BANK:(j + 1) * BANK]
                    link(dve, nc.vector.tensor_tensor(o, ps[:, 3 + n if n < 5 else 0, :], brow[:, l, j * BANK:(j + 1) * BANK], ALU.add))
                    last = nc.vector.tensor_tensor(o, o, brow[:, 2 + l, j * BANK:(j + 1) * BANK], ALU.mult)
                link(dve, last)


def normed(core, tag, tiles, scale, shift=None, into=None, weights=None):
    nc, ps, x, hT = core.nc, core.ps, core.x, core.hT
    with ExitStack() as c:
        T = len(tiles)
        xn = core.ga[:, 0:T, :] if T < NT else c.enter_context(nc.sbuf_tensor(tag + "xn", [P, T, D], F32))[:]
        sq = hT[:, 0:4, SEQ:] if T < NT else c.enter_context(nc.sbuf_tensor(tag + "sq", [P, 4, SEQ], F32))[:]
        st = c.enter_context(nc.sbuf_tensor(tag + "st", [P, 3, NT], F32))
        squares, meaned, rooted, scaled, turned, out_act, out_dve = (
            core.sem(tag + s) for s in ("squares", "meaned", "rooted", "scaled", "turned", "out_act", "out_dve"))
        T = len(tiles)
        with core.phase() as block:
            @block.scalar
            def _(act):
                for i, t in enumerate(tiles):
                    core.act_chain(act, nc.scalar.activation(sq, x[:, t, :].rearrange("p (a b) -> p a b", a=4), ACT.Square, accum_out=st[:, 0, i:i + 1]))
                nc.scalar.activation(sq[:, 0, 0:1], x[:, 0, 0:1], ACT.Copy).then_inc(squares, 1)
                act.wait_ge(meaned, 1)
                nc.scalar.activation(st[:, 1, 0:T], st[:, 1, 0:T], ACT.Sqrt).then_inc(rooted, 1)
                for k in range(KC):
                    act.wait_ge(turned, k + 1)
                    nc.scalar.activation(hT[:, k, 0:SEQ], ps[:, k % 4, 0:SEQ], ACT.Identity, scale=scale(k, 0),
                                         bias=shift(k, 0) if shift else 0.0).then_inc(out_act, 1)

            @block.vector
            def _(dve):
                link = core.dve_chain
                if weights:
                    weights.prime(dve)
                dve.wait_ge(squares, 1)
                nc.vector.tensor_scalar(st[:, 1, 0:T], st[:, 0, 0:T], 1.0 / D, EPS, ALU.mult, ALU.add).then_inc(meaned, 1)
                dve.wait_ge(rooted, 1)
                link(dve, nc.vector.reciprocal(st[:, 2, 0:T], st[:, 1, 0:T]))
                for i, t in enumerate(tiles):
                    nc.vector.tensor_scalar(xn[:, i, :], x[:, t, :], st[:, 2, i:i + 1], None, ALU.mult).then_inc(scaled, 1)
                if T == NT:
                    for k in range(KC):
                        dve.wait_ge(turned, k + 1)
                        dve.wait_ge(out_act, k + 1)
                        nc.vector.tensor_scalar(hT[:, k, SEQ:2 * SEQ], ps[:, k % 4, SEQ:2 * SEQ], scale(k, 1),
                                                shift(k, 1), ALU.mult, ALU.add).then_inc(out_dve, 1)
                if into:
                    for k in range(0, KC, 4):
                        at = np.s_[:, k:k + 4, 0:T * P]
                        dve.wait_ge(out_act, k + 4)
                        if T == NT:
                            dve.wait_ge(out_dve, k + 4)
                        link(dve, into.take_lead(dve, at, hT[at]))
                        last = into.take_rest(dve, at, hT[at])
                    link(dve, last)

            @block.tensor
            def _(pe):
                pe.wait_ge(scaled, T)
                for k in range(KC):
                    if k >= 4:
                        pe.wait_ge(out_dve if T == NT else out_act, k - 3)
                    for i in range(T):
                        mm = nc.tensor.transpose(ps[:, k % 4, i * P:(i + 1) * P], xn[:, i, k * P:(k + 1) * P], core.ident[:])
                    mm.then_inc(turned, 1)


def project(core, tag, groups, lo, route, act_out, dve_out, banks=range(8), before=None, after=None):
    nc, ps = core.nc, core.ps
    hT, B = core.hT, len(banks)
    product, act_read, dve_read = core.sem(tag + "product"), core.sem(tag + "act_read"), core.sem(tag + "dve_read")
    flat = [(w, g) for w, gs in enumerate(groups) for g in gs]
    used_at = [sum(len(gs) for gs in groups[:w + 1]) for w in range(len(groups))]
    ways = [route(n) for n in range(len(flat))]
    acts = [sum("a" in w for w in ways[:n + 1]) for n in range(len(flat))]
    dves = [sum("d" in w for w in ways[:n + 1]) for n in range(len(flat))]
    with core.phase() as block:
        if before:
            before(block)

        @block.sync
        def _(sp):
            core.load_ahead(sp, lo, product, used_at)

        @block.tensor
        def _(pe):
            for n, (wi, (kind, i, n0, n1)) in enumerate(flat):
                if n >= B:
                    pe.wait_ge(dve_read if "d" in ways[n - B] else act_read, (dves if "d" in ways[n - B] else acts)[n - B])
                w = core.weight(pe, lo + wi)
                for k in range(KC):
                    if kind == "tokens":
                        lhs, rhs = hT[:, k, i * P:(i + 1) * P], w[:, k, n0:n1]
                    else:
                        lhs, rhs = w[:, k, i * P:(i + 1) * P], hT[:, k, n0:n1]
                    mm = nc.tensor.matmul(ps[:, banks[n % B], 0:n1 - n0], lhs, rhs, start=(k == 0), stop=(k == KC - 1))
                mm.then_inc(product, 1)

        @block.scalar
        def _(act):
            for n, (wi, g) in enumerate(flat):
                if "a" in ways[n]:
                    act.wait_ge(product, n + 1)
                    act_out(act, n, wi, g, ps[:, banks[n % B], 0:g[3] - g[2]], lambda m: act.wait_ge(dve_read, dves[m])).then_inc(act_read, 1)

        @block.vector
        def _(dve):
            for n, (wi, g) in enumerate(flat):
                if "d" in ways[n]:
                    dve.wait_ge(product, n + 1)
                    if "a" in ways[n]:
                        dve.wait_ge(act_read, acts[n])
                    dve_out(dve, n, wi, g, ps[:, banks[n % B], 0:g[3] - g[2]]).then_inc(dve_read, 1)

        if after:
            after(block)


def project_split(core, tag, weights, u0, h, groups, route, act_out, dve_out, banks=range(8), before=None, after=None,
                  rest_on="vector"):
    nc, ps = core.nc, core.ps
    B = len(banks)
    product, act_read, dve_read = core.sem(tag + "product"), core.sem(tag + "act_read"), core.sem(tag + "dve_read")
    half_used = core.sem(tag + "half_used")
    W = len(groups)
    flat = [(w, g) for w, gs in enumerate(groups) for g in gs]
    start_at = [sum(len(gs) for gs in groups[:w]) for w in range(W + 1)]
    ways = [route(n) for n in range(len(flat))]
    acts = [sum("a" in w for w in ways[:n + 1]) for n in range(len(flat))]
    dves = [sum("d" in w for w in ways[:n + 1]) for n in range(len(flat))]

    def act_outs(act, w):
        for n in range(start_at[w], start_at[w + 1]):
            if "a" in ways[n]:
                act.wait_ge(product, n + 1)
                g = flat[n][1]
                act_out(act, n, w, g, ps[:, banks[n % B], 0:g[3] - g[2]], lambda m: act.wait_ge(dve_read, dves[m])).then_inc(act_read, 1)

    def dve_outs(dve, w):
        for n in range(start_at[w], start_at[w + 1]):
            if "d" in ways[n]:
                dve.wait_ge(product, n + 1)
                if "a" in ways[n]:
                    dve.wait_ge(act_read, acts[n])
                g = flat[n][1]
                dve_out(dve, n, w, g, ps[:, banks[n % B], 0:g[3] - g[2]]).then_inc(dve_read, 1)

    with core.phase() as block:
        if before:
            before(block)

        @block.sync
        def _(sp):
            weights.load_ahead(sp, u0, 2 * W)

        @block.tensor
        def _(pe):
            for u in range(2 * W):
                w = weights.parts(pe, u0 + u)
                for n in range(start_at[u // 2], start_at[u // 2 + 1]):
                    if n >= B and u % 2 == 0:
                        pe.wait_ge(dve_read if "d" in ways[n - B] else act_read, (dves if "d" in ways[n - B] else acts)[n - B])
                    kind, i, n0, n1 = flat[n][1]
                    for k in range(4):
                        kk = 4 * (u % 2) + k
                        if kind == "tokens":
                            lhs, rhs = h.parts(np.s_[:, kk, i * P:(i + 1) * P]), [z[:, k, n0:n1] for z in w]
                        else:
                            lhs, rhs = [z[:, k, i * P:(i + 1) * P] for z in w], h.parts(np.s_[:, kk, n0:n1])
                        mm = split_matmul(nc, ps[:, banks[n % B], 0:n1 - n0], lhs, rhs, kk == 0, kk == KC - 1)
                    if u % 2:
                        mm.then_inc(product, 1)
                if u % 2 == 0:
                    mm.then_inc(half_used, 1)

        @block.scalar
        def _(act):
            weights.take_lead(act, u0 + weights.B - 1)
            for u in range(2 * W):
                if u < 2 * W - 1:
                    if u % 2:
                        act.wait_ge(product, start_at[u // 2 + 1])
                    else:
                        act.wait_ge(half_used, u // 2 + 1)
                    weights.take_lead(act, u0 + weights.B + u)
                if u % 2:
                    act_outs(act, u // 2)

        if rest_on == "gpsimd":
            @block.gpsimd
            def _(pool):
                for u in range(-1, 2 * W - 1):
                    weights.take_rest(nc.gpsimd, u0 + weights.B + u)

        @block.vector
        def _(dve):
            for u in range(-1, 2 * W):
                if rest_on == "vector" and u < 2 * W - 1:
                    weights.take_rest(dve, u0 + weights.B + u)
                if u >= 0 and u % 2:
                    dve_outs(dve, u // 2)

        if after:
            after(block)



def turn(core, tag, blocks, outs_per_bank=4):
    nc, ps = core.nc, core.ps
    turned, act_read, dve_read = core.sem(tag + "turned"), core.sem(tag + "act_read"), core.sem(tag + "dve_read")
    with core.phase() as block:
        @block.tensor
        def _(pe):
            for n, (ins, out, scale) in enumerate(blocks):
                if n >= 8:
                    pe.wait_ge(act_read if n % 2 == 0 else dve_read, (n - 8) // 2 + 1)
                at = 0
                for i in ins:
                    w, h = i.shape[0], i.shape[1]
                    mm = nc.tensor.transpose(ps[0:h, n % 8, at:at + w], i, core.ident[0:w, 0:w])
                    at += w
                mm.then_inc(turned, 1)

        @block.scalar
        def _(act):
            for n, (ins, out, scale) in enumerate(blocks):
                if n % 2 == 0:
                    act.wait_ge(turned, n + 1)
                    w = len(ins) * ins[0].shape[0]
                    nc.scalar.activation(out, ps[0:out.shape[0], n % 8, 0:w], ACT.Copy if scale is None else ACT.Identity,
                                         scale=1.0 if scale is None else scale).then_inc(act_read, 1)

        @block.vector
        def _(dve):
            for n, (ins, out, scale) in enumerate(blocks):
                if n % 2 == 1:
                    dve.wait_ge(turned, n + 1)
                    src = ps[0:out.shape[0], n % 8, 0:len(ins) * ins[0].shape[0]]
                    if scale is None:
                        nc.vector.tensor_copy(out, src).then_inc(dve_read, 1)
                    else:
                        nc.vector.tensor_scalar(out, src, scale, None, ALU.mult).then_inc(dve_read, 1)


def turn_split(core, tag, blocks, into, weights=None):
    nc, ps = core.nc, core.ps
    turned, lead_out, rest_out = core.sem(tag + "turned"), core.sem(tag + "lead_out"), core.sem(tag + "rest_out")
    with core.phase() as block:
        @block.tensor
        def _(pe):
            for n, (ins, at) in enumerate(blocks):
                if n >= 8:
                    pe.wait_ge(rest_out, n - 7)
                for q, i in enumerate(ins):
                    mm = nc.tensor.transpose(ps[:, n % 8, q * P:(q + 1) * P], i, core.ident[:])
                mm.then_inc(turned, 1)

        @block.scalar
        def _(act):
            for n, (ins, at) in enumerate(blocks):
                act.wait_ge(turned, n + 1)
                dst = into.lead[at]
                nc.scalar.activation(dst, bank(ps, n, dst), ACT.Copy).then_inc(lead_out, 1)

        @block.vector
        def _(dve):
            if weights:
                weights.prime(dve)
            for n, (ins, at) in enumerate(blocks):
                dve.wait_ge(lead_out, n + 1)
                into.take_rest(dve, at, bank(ps, n, into.rest[at])).then_inc(rest_out, 1)


def bank(ps, n, like):
    k, t = like.shape[1], like.shape[2]
    return ps[:, n % 8, 0:k * t].rearrange("p (k t) -> p k t", k=k)


def down_split(core, tag, weights, u0, source, tiles, n_weights):
    nc, ps = core.nc, core.ps
    used = core.sem(tag + "half_used")
    N = 2 * n_weights
    with core.phase() as block:
        @block.sync
        def _(sp):
            weights.load_ahead(sp, u0, N)

        @block.tensor
        def _(pe):
            for u in range(N):
                w = weights.parts(pe, u0 + u)
                for i in range(tiles):
                    for j in range(2):
                        for k in range(2):
                            mm = split_matmul(nc, ps[:, 2 * i + j, :], source.parts(np.s_[:, 2 * u + k, i * P:(i + 1) * P]),
                                              [z[:, k, j * BANK:(j + 1) * BANK] for z in w],
                                              u == 0 and k == 0, u == N - 1 and k == 1)
                mm.then_inc(used, 1)

        @block.scalar
        def _(act):
            weights.take_lead(act, u0 + weights.B - 1)
            for u in range(N - 1):
                act.wait_ge(used, u + 1)
                weights.take_lead(act, u0 + weights.B + u)

        @block.vector
        def _(dve):
            for u in range(-1, N - 1):
                weights.take_rest(dve, u0 + weights.B + u)


def down(core, tag, lo, source, tiles, n_weights, finish_act=None, finish_dve=None, first_bank=0):
    nc, ps = core.nc, core.ps
    summed = core.sem(tag + "summed")
    done = core.sem(tag + "weight_done")
    with core.phase() as block:
        @block.sync
        def _(sp):
            core.load_ahead(sp, lo, done, range(1, n_weights + 1))

        @block.tensor
        def _(pe):
            for wi in range(n_weights):
                w = core.weight(pe, lo + wi)
                for i in range(tiles):
                    for j in range(2):
                        for k in range(4):
                            mm = nc.tensor.matmul(ps[:, first_bank + 2 * i + j, :],
                                                  source[:, wi * 4 + k, i * P:(i + 1) * P], w[:, k, j * BANK:(j + 1) * BANK],
                                                  start=(wi == 0 and k == 0), stop=(wi == n_weights - 1 and k == 3))
                mm.then_inc(done, 1)

        if finish_act:
            @block.scalar
            def _(act):
                act.wait_ge(done, n_weights)
                finish_act(act)

        if finish_dve:
            @block.vector
            def _(dve):
                dve.wait_ge(done, n_weights)
                finish_dve(dve)


def gated_residual(core, tag, tiles, gate_of):
    nc, ps, x = core.nc, core.ps, core.x
    with ExitStack() as c:
        sq = c.enter_context(nc.sbuf_tensor(tag + "sq", [P, BANK], F32))
        st = c.enter_context(nc.sbuf_tensor(tag + "st", [P, 4, 2 * NT], F32))
        t = c.enter_context(nc.sbuf_tensor(tag + "t", [P, NT * 2, BANK], F32))
        squares, meaned, rooted = core.sem(tag + "squares"), core.sem(tag + "meaned"), core.sem(tag + "rooted")
        n = 2 * tiles
        with core.phase() as block:
            @block.scalar
            def _(act):
                for b in range(n):
                    core.act_chain(act, nc.scalar.activation(sq[:], ps[:, b, :], ACT.Square, accum_out=st[:, 0, b:b + 1]))
                nc.scalar.activation(sq[:, 0:1], st[:, 0, 0:1], ACT.Copy).then_inc(squares, 1)
                act.wait_ge(meaned, 1)
                nc.scalar.activation(st[:, 2, 0:tiles], st[:, 2, 0:tiles], ACT.Sqrt).then_inc(rooted, 1)

            @block.vector
            def _(dve):
                link = core.dve_chain
                dve.wait_ge(squares, 1)
                pairs = st[:, 0, 0:n].rearrange("p (t j) -> p t j", j=2)
                link(dve, nc.vector.tensor_tensor(st[:, 1, 0:tiles], pairs[:, :, 0], pairs[:, :, 1], ALU.add))
                nc.vector.tensor_scalar(st[:, 2, 0:tiles], st[:, 1, 0:tiles], 1.0 / D, EPS, ALU.mult, ALU.add).then_inc(meaned, 1)
                dve.wait_ge(rooted, 1)
                link(dve, nc.vector.reciprocal(st[:, 3, 0:tiles], st[:, 2, 0:tiles]))
                for i in range(tiles):
                    for j in range(2):
                        last = nc.vector.scalar_tensor_tensor(out=t[:, 2 * i + j, :], in0=ps[:, 2 * i + j, :],
                                                              scalar=st[:, 3, i:i + 1],
                                                              in1=core.ga[:, gate_of[i], j * BANK:(j + 1) * BANK],
                                                              op0=ALU.mult, op1=ALU.mult)
                link(dve, last)
                for i in range(tiles):
                    last = nc.vector.tensor_tensor(x[:, i, :], x[:, i, :],
                                                   t[:, 2 * i:2 * i + 2, :].rearrange("p j n -> p (j n)"), ALU.add)
                link(dve, last)


def side_taps(core, dve, dst, src, w0, w2):
    nc = core.nc
    S = dst.shape[1] // SEQ
    d, u = (z.rearrange("p (s t) -> p s t", s=S) for z in (dst, src))
    core.dve_chain(dve, nc.vector.scalar_tensor_tensor(out=d[:, :, 1:], in0=u[:, :, :SEQ - 1], scalar=w0,
                                                       in1=d[:, :, 1:], op0=ALU.mult, op1=ALU.add))
    return nc.vector.scalar_tensor_tensor(out=d[:, :, :SEQ - 1], in0=u[:, :, 1:], scalar=w2,
                                          in1=d[:, :, :SEQ - 1], op0=ALU.mult, op1=ALU.add)


def softmax_attention(core, tag, jobs, scale):
    nc, ps = core.nc, core.ps
    with ExitStack() as c:
        sb = lambda name, shape: c.enter_context(nc.sbuf_tensor(tag + name, shape, F32))
        nkm = max(j["k"].shape[1] for j in jobs)
        masked = sb("masked", [P, 3, nkm]) if jobs[0]["mask"] is not None else None
        prob = sb("prob", [P, 3, nkm])
        probT = sb("probT", [P, 2, nkm])
        N = len(jobs)
        top, ntop, tot, rec = (sb(n, [P, N]) for n in ("top", "ntop", "tot", "rec"))
        scores, turned, values = core.sem(tag + "scores"), core.sem(tag + "turned"), core.sem(tag + "values")
        negmax, exped, prob_ready = core.sem(tag + "negmax"), core.sem(tag + "exped"), core.sem(tag + "prob_ready")
        probT_ready, out_done = core.sem(tag + "probT_ready"), core.sem(tag + "out_done")
        with core.phase() as block:
            @block.tensor
            def _(pe):
                for j in range(N + 4):
                    if j < N:
                        if j >= 3:
                            pe.wait_ge(exped, j - 2)
                        k = jobs[j]["k"]
                        nc.tensor.matmul(ps[:, j % 3, 0:k.shape[1]], jobs[j]["q"], k, start=True, stop=True).then_inc(scores, 1)
                    if 2 <= j < N + 2:
                        i = j - 2
                        pe.wait_ge(prob_ready, i + 1)
                        if i >= 2:
                            pe.wait_ge(probT_ready, i - 1)
                        for b in range(jobs[i]["k"].shape[1] // P):
                            mm = nc.tensor.transpose(ps[:, 3 + i % 2, b * P:(b + 1) * P], prob[:, i % 3, b * P:(b + 1) * P], core.ident[:])
                        mm.then_inc(turned, 1)
                    if j >= 4:
                        i = j - 4
                        pe.wait_ge(probT_ready, i + 1)
                        if i >= 2:
                            pe.wait_ge(out_done, i - 1)
                        vs = jobs[i]["v"]
                        for b, v in enumerate(vs):
                            pt = probT[:, i % 2, b * P:(b + 1) * P]
                            dv = v.shape[1]
                            if jobs[i]["feat"]:
                                o, lhs, rhs = ps[0:dv, 5 + i % 2, 0:P], v, pt
                            else:
                                o, lhs, rhs = ps[:, 5 + i % 2, 0:dv], pt, v
                            mm = nc.tensor.matmul(o, lhs, rhs, start=(b == 0), stop=(b == len(vs) - 1))
                        mm.then_inc(values, 1)

            @block.scalar
            def _(act):
                for j in range(N + 2):
                    if j < N:
                        act.wait_ge(negmax, j + 1)
                        if j >= 3:
                            act.wait_ge(turned, j - 2)
                        nk = jobs[j]["k"].shape[1]
                        src = masked[:, j % 3, 0:nk] if jobs[j]["mask"] is not None else ps[:, j % 3, 0:nk]
                        nc.scalar.activation(prob[:, j % 3, 0:nk], src, ACT.Exp, bias=ntop[:, j:j + 1], scale=scale,
                                             accum_out=tot[:, j:j + 1]).then_inc(exped, 1)
                    if j >= 2:
                        i = j - 2
                        act.wait_ge(turned, i + 1)
                        if i >= 2:
                            act.wait_ge(values, i - 1)
                        nk = jobs[i]["k"].shape[1]
                        nc.scalar.activation(probT[:, i % 2, 0:nk], ps[:, 3 + i % 2, 0:nk], ACT.Copy).then_inc(probT_ready, 1)

            @block.vector
            def _(dve):
                link = core.dve_chain
                for j in range(N + 4):
                    if j < N:
                        dve.wait_ge(scores, j + 1)
                        nk = jobs[j]["k"].shape[1]
                        if jobs[j]["mask"] is not None:
                            if j >= 3:
                                dve.wait_ge(exped, j - 2)
                            link(dve, nc.vector.tensor_tensor_reduce(masked[:, j % 3, 0:nk], ps[:, j % 3, 0:nk], jobs[j]["mask"],
                                                                     1.0, NEG, ALU.add, ALU.max, top[:, j:j + 1]))
                        else:
                            link(dve, nc.vector.tensor_reduce(top[:, j:j + 1], ps[:, j % 3, 0:nk], AX.X, ALU.max))
                        nc.vector.tensor_scalar(ntop[:, j:j + 1], top[:, j:j + 1], -scale, None, ALU.mult).then_inc(negmax, 1)
                    if 1 <= j <= N:
                        i = j - 1
                        dve.wait_ge(exped, i + 1)
                        nk = jobs[i]["k"].shape[1]
                        link(dve, nc.vector.reciprocal(rec[:, i:i + 1], tot[:, i:i + 1]))
                        nc.vector.tensor_scalar(prob[:, i % 3, 0:nk], prob[:, i % 3, 0:nk], rec[:, i:i + 1], None, ALU.mult).then_inc(prob_ready, 1)
                    if j >= 4:
                        i = j - 4
                        dve.wait_ge(values, i + 1)
                        dv = jobs[i]["v"][0].shape[1]
                        if jobs[i]["feat"]:
                            nc.vector.tensor_tensor(jobs[i]["out"], ps[0:dv, 5 + i % 2, 0:P], jobs[i]["gate"], ALU.mult).then_inc(out_done, 1)
                        else:
                            nc.vector.tensor_copy(jobs[i]["out"], ps[:, 5 + i % 2, 0:dv]).then_inc(out_done, 1)


def rope(core, dve, x, tab, tmp, heads, width, halves=1):
    nc, link = core.nc, core.dve_chain
    w, h = halves * width, width // 2
    cos = tab[:, 0:w].unsqueeze(1).broadcast_to([P, heads, w])
    t1, t2 = tmp[:, 0, 0:heads * w].rearrange("p (a b) -> p a b", a=heads), tmp[:, 1, 0:heads * w].rearrange("p (a b) -> p a b", a=heads)
    nc.vector.tensor_tensor(t1, x, cos, ALU.mult)
    for a in range(halves):
        for first, second in ((0, h), (h, 0)):
            o = a * width
            s = tab[:, w + o + first:w + o + first + h].unsqueeze(1).broadcast_to([P, heads, h])
            last = nc.vector.tensor_tensor(t2[:, :, o + first:o + first + h], x[:, :, o + second:o + second + h], s, ALU.mult)
    link(dve, last)
    link(dve, nc.vector.tensor_tensor(x, t1, t2, ALU.add))


def even_layer(core):
    nc, a, ps = core.nc, core.a, core.ps
    mod = core.mod
    normed(core, "en_", range(NT), lambda k, s: mod[:, 0, 1, k, s:s + 1], lambda k, s: mod[:, 0, 0, k, s:s + 1])
    with ExitStack() as layer:
        mixT = layer.enter_context(nc.sbuf_tensor("mixT", [P, 16, 2 * SEQ], F32))
        even_attention(core, mixT)
        hyena(core, mixT)
        down(core, "eo_", core.first["e_out"], mixT, NT, 4)
    gated_residual(core, "er_", NT, [0, 0, 1, 1])


def even_attention(core, mixT):
    nc, a, ps = core.nc, core.a, core.ps
    first = core.first
    with ExitStack() as c:
        sb = lambda name, shape: c.enter_context(nc.sbuf_tensor(name, shape, F32))
        NH = HEADS + KVH
        v = sb("ea_v", [P, NT, KVH * DH])
        qkT = sb("ea_qkT", [P, NH, 2 * SEQ])
        with ExitStack() as c2:
            qk = c2.enter_context(nc.sbuf_tensor("ea_qk", [P, NT, NH * DH], F32))

            def take(copy):
                def out(eng, n, wi, g, src, dve_out=None):
                    t = g[1]
                    if wi < 2:
                        return copy(qk[:, t, wi * 512:(wi + 1) * 512], src)
                    return copy(qk[:, t, 1024:1280] if g[2] == 0 else v[:, t, :], src)
                return out
            groups = [[("tokens", t, 0, 512) for t in range(NT)]] * 2 + \
                     [[("tokens", t, h * 256, h * 256 + 256) for t in range(NT) for h in range(2)]]
            project(core, "eqkv_", groups, first["e_qkv"], lambda n: "ad"[n % 2],
                    take(lambda o, i: nc.scalar.activation(o, i, ACT.Copy)), take(nc.vector.tensor_copy))
            tab = c2.enter_context(nc.sbuf_tensor("ea_rope", [P, LT, 256], F32))
            gains = c2.enter_context(nc.sbuf_tensor("ea_gains", [P, 2, DH], F32))
            tmp = c2.enter_context(nc.sbuf_tensor("ea_tmp", [P, 2, NH * DH], F32))
            st = c2.enter_context(nc.sbuf_tensor("ea_st", [P, 3, NT * NH], F32))
            tabs_in, meaned, rooted = core.expect_tables(3), core.sem("ea_meaned"), core.sem("ea_rooted")

            def norm_and_rotate(block):
                @block.gpsimd
                def _(pool):
                    pool.dma_start(tab[:], a["rope_e"].rearrange("(t p) n -> p t n", p=P)).then_inc(core.tables_in, 16)
                    pool.dma_start(gains[:, 0, :], row_bcast(a, "q_norm")).then_inc(core.tables_in, 16)
                    pool.dma_start(gains[:, 1, :], row_bcast(a, "k_norm")).then_inc(core.tables_in, 16)

                @block.scalar
                def _(act):
                    act.wait_ge(meaned, 1)
                    nc.scalar.activation(st[:, 1, :], st[:, 1, :], ACT.Sqrt).then_inc(rooted, 1)

                @block.vector
                def _(dve):
                    link = core.dve_chain
                    for t in range(NT):
                        sq = tmp[:, t % 2, :]
                        link(dve, nc.vector.tensor_tensor(sq, qk[:, t, :], qk[:, t, :], ALU.mult))
                        link(dve, nc.vector.tensor_reduce(st[:, 0, t * NH:(t + 1) * NH], sq.rearrange("p (h d) -> p h d", h=NH),
                                                          AX.X, ALU.add))
                    nc.vector.tensor_scalar(st[:, 1, :], st[:, 0, :], 1.0 / DH, EPS, ALU.mult, ALU.add).then_inc(meaned, 1)
                    dve.wait_ge(rooted, 1)
                    link(dve, nc.vector.reciprocal(st[:, 2, :], st[:, 1, :]))
                    dve.wait_ge(core.tables_in, tabs_in)
                    for t in range(NT):
                        x = qk[:, t, :].rearrange("p (h d) -> p h d", h=NH)
                        r = st[:, 2, t * NH:(t + 1) * NH].unsqueeze(2).broadcast_to([P, NH, DH])
                        link(dve, nc.vector.tensor_tensor(x, x, r, ALU.mult))
                        nc.vector.tensor_tensor(x[:, 0:HEADS], x[:, 0:HEADS], gains[:, 0:1, :].broadcast_to([P, HEADS, DH]), ALU.mult)
                        link(dve, nc.vector.tensor_tensor(x[:, HEADS:], x[:, HEADS:], gains[:, 1:2, :].broadcast_to([P, KVH, DH]), ALU.mult))
                        if t < LT:
                            rope(core, dve, x, tab[:, t, :], tmp, NH, 64, 2)

            project(core, "ega_", [[("features", m, 0, 512) for m in range(4)]] * 2, first["e_gatt"], lambda n: "a",
                    lambda act, n, wi, g, src, w: nc.scalar.activation(mixT[:, 8 + n, :], src, ACT.Silu), None,
                    before=norm_and_rotate)
            turn(core, "ea_t_", [([qk[:, t, h * DH:(h + 1) * DH] for t in range(NT)], qkT[:, h, :], None) for h in range(NH)])
        jobs = []
        for h in range(HEADS):
            g = h // (HEADS // KVH)
            for t in range(NT):
                k0 = 0 if t < LT else SEQ
                jobs.append(dict(q=qkT[:, h, t * P:(t + 1) * P], k=qkT[:, HEADS + g, k0:2 * SEQ], mask=None, feat=True,
                                 v=[v[:, b, g * DH:(g + 1) * DH] for b in range(k0 // P, NT)],
                                 out=mixT[:, 8 + h, t * P:(t + 1) * P], gate=mixT[:, 8 + h, t * P:(t + 1) * P]))
        softmax_attention(core, "ea_", jobs, DH ** -0.5)


def hyena(core, mixT):
    nc, a, ps = core.nc, core.a, core.ps
    first, col = core.first, core.col
    NTT = 4
    with ExitStack() as c:
        sb = lambda name, shape, c=c: c.enter_context(nc.sbuf_tensor(name, shape, F32))
        gT = sb("hy_gT", [P, KC, 2 * SEQ])
        x0T = sb("hy_x0T", [P, KC, 2 * SEQ])
        with ExitStack() as c2:
            tmp = c2.enter_context(nc.sbuf_tensor("hy_tmp", [P, 2, 2 * SEQ], F32))
            feats = [("features", m, 0, 512) for m in range(4)]

            def conv(tag, name, chan0, dst, after=None, own_tmp=False):
                def act_out(act, n, wi, g, src, dve_done):
                    if own_tmp and n >= 2:
                        dve_done(n - 2)
                    ch = chan0 + n
                    return nc.scalar.activation(dst(n), src, ACT.Identity, scale=col("e_cw1", ch), bias=col("e_cb", ch))

                def dve_out(dve, n, wi, g, src):
                    ch = chan0 + n
                    last = side_taps(core, dve, dst(n), src, col("e_cw0", ch), col("e_cw2", ch))
                    if after:
                        core.dve_chain(dve, last)
                        last = after(n)
                    return last
                project(core, tag, [feats] * 2, first[name], lambda n: "ad", act_out, dve_out)

            conv("hx1_", "e_x1", 8, lambda n: gT[:, n, :])
            conv("hv_", "e_v", 16, lambda n: tmp[:, n % 2, :],
                 lambda n: nc.vector.tensor_tensor(gT[:, n, :], gT[:, n, :], tmp[:, n % 2, :], ALU.mult), own_tmp=True)
            conv("hx0_", "e_x0", 0, lambda n: x0T[:, n, :])

            def silu_tmp(act, n, wi, g, src, dve_done):
                if n >= 2:
                    dve_done(n - 2)
                return nc.scalar.activation(tmp[:, n % 2, :], src, ACT.Silu)
            project(core, "hgh_", [feats] * 2, first["e_ghy"], lambda n: "ad", silu_tmp,
                    lambda dve, n, wi, g, src: nc.vector.tensor_tensor(x0T[:, n, :], x0T[:, n, :], tmp[:, n % 2, :], ALU.mult))

        F = sb("hy_F", [P, 5, HY])
        snorm = sb("hy_norm", [P, KC])
        dft = sb("hy_dft", [P, NTT, 2 * SEQ])
        tabs_in = core.expect_tables(7)
        gtok = core.hT[:].rearrange("p k t -> p (k t)").rearrange("p (t d) -> p t d", t=NT)
        with ExitStack() as c2:
            sb2 = lambda name, shape: c2.enter_context(nc.sbuf_tensor(name, shape, F32))
            filt = mixT[:, 0:KC, :].rearrange("p k t -> p (k t)").rearrange("p (t d) -> p t d", t=NTT)
            scratch = core.hT[:].rearrange("p k t -> p (k t)")
            zt = sb2("hy_zt", [33, SEQ])
            w1, w2 = sb2("hy_w1", [33, 64]), sb2("hy_w2", [64, 64])
            w3 = scratch[0:64, 0:2 * HY]
            decay = scratch[:, 2 * HY:4 * HY].rearrange("p (t d) -> p t d", t=2)
            ones = sb2("hy_ones", [P, NTT])
            hd = sb2("hy_hd", [64, 4, SEQ])
            dense, sined, arg_ready = core.sem("hy_dense"), core.sem("hy_sined"), core.sem("hy_arg_ready")
            filt_out = core.sem("hy_filt_out")
            TWO_PI_HI = float(np.float32(6.28125))
            TWO_PI_LO = float(2 * math.pi - 6.28125)
            MAGIC = 12582912.0
            with core.phase() as block:
                @block.gpsimd
                def _(pool):
                    for dst, src in ((zt[:], a["z_t"]), (w1[:], a["e_filt_w1"][0]), (w2[:], a["e_filt_w2"][0]),
                                     (w3, a["e_filt_w3"][0]), (decay, a["decay"].rearrange("(t p) n -> p t n", p=P)),
                                     (ones[:], a["tap_ones"]),
                                     (dft[:], a["dft"].rearrange("(t p) n -> p t n", p=P))):
                        pool.dma_start(dst, src).then_inc(core.tables_in, 16)

                @block.tensor
                def _(pe):
                    pe.wait_ge(core.tables_in, tabs_in)
                    nc.tensor.matmul(ps[0:64, 0, 0:SEQ], w1[:], zt[:], start=True, stop=True).then_inc(dense, 1)
                    pe.wait_ge(sined, 1)
                    nc.tensor.matmul(ps[0:64, 1, 0:SEQ], w2[:], hd[:, 3, :], start=True, stop=True).then_inc(dense, 1)
                    pe.wait_ge(sined, 2)
                    for n in range(8):
                        side, t, j = n // 4, n // 2 % 2, n % 2
                        if n >= 6:
                            pe.wait_ge(filt_out, n - 5)
                        nc.tensor.matmul(ps[:, 2 + n % 6, :], hd[:, 3, t * P:(t + 1) * P],
                                         w3[:, side * HY + j * BANK:side * HY + (j + 1) * BANK], start=True, stop=True).then_inc(dense, 1)

                @block.scalar
                def _(act):
                    for i in range(2):
                        act.wait_ge(arg_ready, i + 1)
                        nc.scalar.activation(hd[:, 3, :], hd[:, 2, :], ACT.Sin).then_inc(sined, 1)

                @block.vector
                def _(dve):
                    link = core.dve_chain
                    for i in range(2):
                        dve.wait_ge(dense, i + 1)
                        link(dve, nc.vector.tensor_scalar(hd[:, 0, :], ps[0:64, i, 0:SEQ], core.col(f"f_b{i + 1}")[0:64],
                                                          core.col("f_fr")[0:64], ALU.add, ALU.mult))
                        link(dve, nc.vector.tensor_scalar(hd[:, 1, :], hd[:, 0, :], float(1 / (2 * math.pi)), None, ALU.mult))
                        link(dve, nc.vector.tensor_scalar(hd[:, 1, :], hd[:, 1, :], MAGIC, None, ALU.add))
                        link(dve, nc.vector.tensor_scalar(hd[:, 1, :], hd[:, 1, :], MAGIC, None, ALU.subtract))
                        link(dve, nc.vector.scalar_tensor_tensor(out=hd[:, 0, :], in0=hd[:, 1, :], scalar=-TWO_PI_HI,
                                                                 in1=hd[:, 0, :], op0=ALU.mult, op1=ALU.add))
                        link(dve, nc.vector.scalar_tensor_tensor(out=hd[:, 0, :], in0=hd[:, 1, :], scalar=-TWO_PI_LO,
                                                                 in1=hd[:, 0, :], op0=ALU.mult, op1=ALU.add))
                        nc.vector.tensor_scalar(hd[:, 2, :], hd[:, 0, :], math.pi - 1e-6, -math.pi + 1e-6, ALU.min, ALU.max).then_inc(arg_ready, 1)
                    for n in range(8):
                        side, t, j = n // 4, n // 2 % 2, n % 2
                        dve.wait_ge(dense, n + 3)
                        nc.vector.tensor_tensor(filt[:, side * 2 + t, j * BANK:(j + 1) * BANK], ps[:, 2 + n % 6, :],
                                                decay[:, t, j * BANK:(j + 1) * BANK], ALU.mult).then_inc(filt_out, 1)
            absd, summed, F_done, F_out_dve = (core.sem(n) for n in ("hy_absd", "hy_summed", "hy_F_done", "hy_F_out_dve"))
            absf = c2.enter_context(nc.sbuf_tensor("hy_abs", [P, NTT, BANK], F32))
            with core.phase() as block:
                @block.scalar
                def _(act):
                    for j in range(2):
                        if j:
                            act.wait_ge(summed, 1)
                        for t in range(NTT):
                            core.act_chain(act, nc.scalar.activation(absf[:, t, :], filt[:, t, j * BANK:(j + 1) * BANK], ACT.Abs))
                        nc.scalar.activation(core.small[:, 1:2], core.ident[:, 0:1], ACT.Copy).then_inc(absd, 1)

                @block.tensor
                def _(pe):
                    for j in range(2):
                        pe.wait_ge(absd, j + 1)
                        for ch in range(4):
                            for t in range(NTT):
                                mm = nc.tensor.matmul(ps[:, 0, 4 * j + ch:4 * j + ch + 1], absf[:, t, ch * P:(ch + 1) * P],
                                                      ones[:, t:t + 1], start=(t == 0), stop=(t == NTT - 1))
                        mm.then_inc(summed, 1)
                    for n in range(8):
                        f, j = n // 2, n % 2
                        if n >= 7:
                            pe.wait_ge(F_out_dve, 1)
                        for t in range(NTT):
                            mm = nc.tensor.matmul(ps[:, 1 + n % 7, :], dft[:, t, f * P:(f + 1) * P],
                                                  filt[:, t, j * BANK:(j + 1) * BANK], start=(t == 0), stop=(t == NTT - 1))
                        mm.then_inc(F_done, 1)

                @block.vector
                def _(dve):
                    link = core.dve_chain
                    for n in range(8):
                        f, j = n // 2, n % 2
                        dve.wait_ge(F_done, n + 1)
                        nc.vector.tensor_copy(F[:, f, j * BANK:(j + 1) * BANK], ps[:, 1 + n % 7, :]).then_inc(F_out_dve, 1)
                    dve.wait_ge(F_out_dve, 8)
                    link(dve, nc.vector.tensor_copy(F[:, 4, :], F[:, 0, :]))
                    link(dve, nc.vector.tensor_copy(F[0:1, 4, :], F[0:1, 2, :]))
                    link(dve, nc.vector.memset(F[0:1, 2, :], 0.0))
                    dve.wait_ge(summed, 2)
                    link(dve, nc.vector.reciprocal(snorm[:], ps[:, 0, 0:KC]))
        turn(core, "hy_t_", [([gT[:, 4 * q + i, t * P:(t + 1) * P] for i in range(4)],
                              gtok[:, t, q * BANK:(q + 1) * BANK], None) for t in range(NT) for q in range(2)])
        Y = sb("hy_Y", [P, 2, 4, BANK])
        T2 = sb("hy_T2", [P, 2, BANK])
        idft = dft[:, 2:4, :].rearrange("p a b -> p (a b)").rearrange("p (t n) -> p t n", t=NTT)
        y1 = core.small
        inv_in = core.expect_tables(1)
        spect, Y_ready, back, mixed = (core.sem(n) for n in ("hy_spect", "hy_Y_ready", "hy_back", "hy_mixed"))
        rounds = [(j, s) for j in range(2) for s in range(2)]
        with core.phase() as block:
            @block.gpsimd
            def _(pool):
                pool.dma_start(idft, a["idft"].rearrange("(t p) n -> p t n", p=P)).then_inc(core.tables_in, 16)

            @block.tensor
            def _(pe):
                pe.wait_ge(core.tables_in, inv_in)
                for r in range(len(rounds) + 1):
                    if r < len(rounds):
                        j, s = rounds[r]
                        if r:
                            pe.wait_ge(Y_ready, r)
                        for f in range(NTT):
                            for t in range(LT):
                                mm = nc.tensor.matmul(ps[:, f, :], dft[:, t, f * P:(f + 1) * P],
                                                      gtok[:, s * LT + t, j * BANK:(j + 1) * BANK], start=(t == 0), stop=(t == LT - 1))
                        mm.then_inc(spect, 1)
                    if r:
                        pe.wait_ge(Y_ready, r)
                        for ch in range(4):
                            if r >= 2:
                                pe.wait_ge(mixed, 4 * (r - 2) + ch + 1)
                            for f in range(NTT):
                                mm = nc.tensor.matmul(ps[:, 4 + ch, 0:SEQ], Y[:, (r - 1) % 2, f, ch * P:(ch + 1) * P], idft[:, f, :],
                                                      start=(f == 0), stop=(f == NTT - 1))
                            mm.then_inc(back, 1)

            @block.vector
            def _(dve):
                link = core.dve_chain
                for r in range(len(rounds) + 1):
                    if r < len(rounds):
                        j, s = rounds[r]
                        dve.wait_ge(spect, r + 1)
                        if r >= 2:
                            dve.wait_ge(back, 4 * (r - 1))
                        cs, Yr = slice(j * BANK, (j + 1) * BANK), Y[:, r % 2]
                        for f in range(2):
                            nc.vector.tensor_tensor(Yr[:, f, :], ps[:, f, :], F[:, f, cs], ALU.mult)
                            last = nc.vector.tensor_tensor(T2[:, f, :], ps[:, 2 + f, :], F[:, 2 + f, cs], ALU.mult)
                        link(dve, last)
                        link(dve, nc.vector.tensor_tensor(Yr[:, 0:2, :], Yr[:, 0:2, :], T2[:, 0:2, :], ALU.subtract))
                        for f in range(2):
                            nc.vector.tensor_tensor(Yr[:, 2 + f, :], ps[:, f, :], F[:, 2 + f, cs], ALU.mult)
                            last = nc.vector.tensor_tensor(T2[:, f, :], ps[:, 2 + f, :], F[:, 4 if f == 0 else 1, cs], ALU.mult)
                        link(dve, last)
                        nc.vector.tensor_tensor(Yr[:, 2:4, :], Yr[:, 2:4, :], T2[:, 0:2, :], ALU.add).then_inc(Y_ready, 1)
                    if r:
                        j, s = rounds[r - 1]
                        for ch in range(4):
                            k, ss = 4 * j + ch, slice(s * SEQ, (s + 1) * SEQ)
                            dve.wait_ge(back, 4 * (r - 1) + ch + 1)
                            if r > 1 or ch:
                                dve.wait_ge(mixed, 4 * (r - 1) + ch)
                            link(dve, nc.vector.tensor_scalar(y1[:], ps[:, 4 + ch, 0:SEQ], snorm[:, k:k + 1], None, ALU.mult))
                            link(dve, nc.vector.scalar_tensor_tensor(out=y1[:], in0=gT[:, k, ss], scalar=col("hy_bias", k),
                                                                     in1=y1[:], op0=ALU.mult, op1=ALU.add))
                            nc.vector.tensor_tensor(mixT[:, k, ss], y1[:], x0T[:, k, ss], ALU.mult).then_inc(mixed, 1)


def program(nc, a, out, n_phases, dump):
    with ExitStack() as ctx:
        core = Core(nc, a, ctx)
        setup(core)
        adaln(core)
        even_layer(core)
        if n_phases == "even":
            return finish_dump(core, out, core.x)
        odd_layer(core)
        if n_phases == "odd":
            return finish_dump(core, out, core.x)
        for l in range(DEPTH):
            block2(core, l)
            if n_phases == f"b{l}":
                return finish_dump(core, out, core.x)
        final(core, out)


def finish_dump(core, out, x):
    stored = core.stored
    with core.phase() as block:
        @block.sync
        def _(sp):
            sp.dma_start(out[0].rearrange("(t p) d -> p t d", p=P), x[:, 0:LT, :]).then_inc(stored, 16)
            sp.wait_ge(stored, 16)
            for s in range(SLOTS):
                last = max((v for i, v in enumerate(core.landed_at[:core.issued]) if i % SLOTS == s), default=0)
                sp.wait_ge(core.landed[s], last)


def mlstm_gates(core, c, aT, cumT, masks, select, g):
    nc, a, ps = core.nc, core.a, core.ps
    R = 40
    sb = lambda name, shape: c.enter_context(nc.sbuf_tensor("mg_" + name, shape, F32))
    wg = sb("w", [P, KC, 2, R])
    tot = sb("tot", [R, 2])
    loaded = core.expect_tables(4)
    products, logged, abs_ready, cum_ready, turned = (
        core.sem("mg_" + n) for n in ("products", "logged", "abs_ready", "cum_ready", "turned"))
    I, FG, LF, T, CUM, ONE = range(6)
    lat, ctx = slice(0, SEQ), slice(SEQ, 2 * SEQ)
    def before(block):
        @block.gpsimd
        def _(pool):
            pool.dma_start(wg[:], a["gate_w"].rearrange("p (k i r) -> p k i r", k=KC, i=2)).then_inc(core.tables_in, 16)
            pool.dma_start(select, a["select"]).then_inc(core.tables_in, 16)
            for d, name in enumerate(("causal", "anti")):
                pool.dma_start(masks[:, LT * d:LT * (d + 1), :], a[name].rearrange("(t p) n -> p t n", p=P)).then_inc(core.tables_in, 16)
            core.pool_chain(pool, nc.gpsimd.memset(masks[:, 2 * LT, :], 0.0))
            pool.wait_ge(core.tables_in, loaded)

        @block.tensor
        def _(pe):
            pe.wait_ge(core.tables_in, loaded)
            for i in range(2):
                for k in range(KC):
                    mm = nc.tensor.matmul(ps[0:R, i, :], wg[:, k, i, :], core.hT[:, k, :], start=(k == 0), stop=(k == KC - 1))
                mm.then_inc(products, 1)

        @block.scalar
        def _(act):
            act.wait_ge(abs_ready, 1)
            core.act_chain(act, nc.scalar.activation(g[:, T, :], g[:, T, :], ACT.Exp, scale=-1.0))
            nc.scalar.activation(g[:, T, :], g[:, T, :], ACT.Ln, bias=1.0).then_inc(logged, 1)

        @block.vector
        def _(dve):
            link = core.dve_chain
            link(dve, nc.vector.memset(g[:, ONE, :], 1.0))
            dve.wait_ge(products, 2)
            nc.vector.tensor_scalar(g[:, I, :], ps[0:R, 0, :], core.col("gb_i")[0:R], None, ALU.add)
            link(dve, nc.vector.tensor_scalar(g[:, FG, :], ps[0:R, 1, :], core.col("gb_f")[0:R], None, ALU.add))
            nc.vector.tensor_scalar(g[:, LF, :], g[:, FG, :], 0.0, None, ALU.min)
            nc.vector.scalar_tensor_tensor(out=g[:, T, :], in0=g[:, FG, :], scalar=-1.0, in1=g[:, FG, :],
                                           op0=ALU.mult, op1=ALU.max).then_inc(abs_ready, 1)
            dve.wait_ge(logged, 1)
            link(dve, nc.vector.tensor_tensor(g[:, LF, :], g[:, LF, :], g[:, T, :], ALU.subtract))
            nc.vector.tensor_tensor_scan(g[:, CUM, lat], g[:, ONE, lat], g[:, LF, lat], 0.0, ALU.mult, ALU.add)
            link(dve, nc.vector.tensor_tensor_scan(g[:, CUM, ctx], g[:, ONE, ctx], g[:, LF, ctx], 0.0, ALU.mult, ALU.add))
            end_lat, end_ctx = g[:, CUM, SEQ - 1:SEQ], g[:, CUM, 2 * SEQ - 1:2 * SEQ]
            nc.vector.tensor_copy(tot[:, 0:1], end_ctx)
            link(dve, nc.vector.tensor_tensor(tot[:, 1:2], end_ctx, end_lat, ALU.add))
            link(dve, nc.vector.tensor_scalar(g[0:8, CUM, lat], g[0:8, CUM, lat], tot[0:8, 0:1], None, ALU.add))
            B = slice(32, R)
            for n, part in ((1, lat), (0, ctx)):
                link(dve, nc.vector.tensor_scalar(g[B, CUM, part], g[B, CUM, part], -1.0, tot[B, n:n + 1], ALU.mult, ALU.add))
            link(dve, nc.vector.tensor_tensor(g[B, CUM, :], g[B, CUM, :], g[B, LF, :], ALU.add))
            nc.vector.tensor_tensor(aT[:], g[:, I, :], g[:, CUM, :], ALU.subtract).then_inc(cum_ready, 1)

    def after(block):
        @block.tensor
        def _(pe):
            pe.wait_ge(cum_ready, 1)
            for t in range(LT):
                mm = nc.tensor.transpose(ps[:, 2, t * R:(t + 1) * R], g[:, CUM, t * P:(t + 1) * P], core.ident[0:R, 0:R])
            mm.then_inc(turned, 1)

        @block.vector
        def _(dve):
            link = core.dve_chain
            dve.wait_ge(turned, 1)
            link(dve, nc.vector.tensor_copy(cumT[:], ps[:, 2, 0:LT * R].rearrange("p (t r) -> p t r", t=LT)))

    return before, after


def mlstm(core, qT, kT, v, o_gate, aT, cumT, masks, select, hs):
    nc, ps = core.nc, core.ps
    scale = ML_QK ** -0.5
    with ExitStack() as c:
        sb = lambda name, shape: c.enter_context(nc.sbuf_tensor("ml_" + name, shape, F32))
        Dm = sb("decay", [P, 3, 2, 2 * SEQ])
        WT = sb("WT", [P, 2, 2 * SEQ])
        jobs = [(h, t) for h in range(ML_H) for t in range(LT)]
        N = len(jobs)
        mu, nmu, flr, den, rec = (sb(n, [P, 2 * N]) for n in ("mu", "nmu", "flr", "den", "rec"))
        sems = {n: core.sem("ml_" + n) for n in ("scores", "spread", "negmax", "decayed", "floored", "mixed",
                                                 "turned", "WT_ready", "values", "out_done")}
        sc, spread, negmax, decayed, floored, mixed, turned, WT_ready, values, out_done = sems.values()
        with core.phase() as block:
            @block.tensor
            def _(pe):
                for j in range(N + 3):
                    if j < N:
                        h, t = jobs[j]
                        if j >= 2:
                            pe.wait_ge(mixed, j - 1)
                        nc.tensor.matmul(ps[:, j % 2, :], qT[:, h, t * P:(t + 1) * P], kT[:, h, :], start=True, stop=True).then_inc(sc, 1)
                        for d in range(2):
                            if j >= 1:
                                pe.wait_ge(negmax, 2 * (j - 1) + d + 1)
                            nc.tensor.matmul(ps[:, 2 + d, :], select[:, (8 * d + h) * P:(8 * d + h + 1) * P], aT[:],
                                             start=True, stop=True).then_inc(spread, 1)
                    if 2 <= j < N + 2:
                        i = j - 2
                        pe.wait_ge(mixed, i + 1)
                        if i >= 2:
                            pe.wait_ge(WT_ready, i - 1)
                        for b in range(4):
                            mm = nc.tensor.transpose(ps[:, 4 + i % 2, b * P:(b + 1) * P], Dm[:, i % 3, 0, b * P:(b + 1) * P], core.ident[:])
                        mm.then_inc(turned, 1)
                    if j >= 3:
                        i = j - 3
                        h, t = jobs[i]
                        pe.wait_ge(WT_ready, i + 1)
                        if i >= 2:
                            pe.wait_ge(out_done, i - 1)
                        for b in range(4):
                            mm = nc.tensor.matmul(ps[:, 6 + i % 2, 0:ML_V], WT[:, i % 2, b * P:(b + 1) * P],
                                                  v[:, b, h * ML_V:(h + 1) * ML_V], start=(b == 0), stop=(b == 3))
                        mm.then_inc(values, 1)

            @block.scalar
            def _(act):
                for j in range(N + 2):
                    if j < N:
                        h, t = jobs[j]
                        for d in range(2):
                            u = 2 * j + d
                            act.wait_ge(negmax, u + 1)
                            nc.scalar.activation(Dm[:, j % 3, d, :], Dm[:, j % 3, d, :], ACT.Exp, bias=nmu[:, u:u + 1]).then_inc(decayed, 1)
                            r = 32 * d + h
                            nc.scalar.activation(flr[:, u:u + 1], cumT[:, t, r:r + 1], ACT.Exp, bias=nmu[:, u:u + 1], scale=-1.0).then_inc(floored, 1)
                    if j >= 2:
                        i = j - 2
                        act.wait_ge(turned, i + 1)
                        if i >= 2:
                            act.wait_ge(values, i - 1)
                        nc.scalar.activation(WT[:, i % 2, :], ps[:, 4 + i % 2, :], ACT.Copy).then_inc(WT_ready, 1)

            @block.vector
            def _(dve):
                link = core.dve_chain
                for j in range(N + 3):
                    if j < N:
                        h, t = jobs[j]
                        if j >= 3:
                            dve.wait_ge(turned, j - 2)
                        for d in range(2):
                            u = 2 * j + d
                            dve.wait_ge(spread, u + 1)
                            m = LT * d + t
                            halves = lambda z: z.rearrange("p (s n) -> p s n", s=2)
                            link(dve, nc.vector.tensor_tensor_reduce(halves(Dm[:, j % 3, d, :]), halves(ps[:, 2 + d, :]), masks[:, m:2 * LT + 1:2 * LT - m, :],
                                                                     1.0, 0.0, ALU.add, ALU.max, mu[:, u:u + 1]))
                            nc.vector.tensor_scalar(nmu[:, u:u + 1], mu[:, u:u + 1], -1.0, None, ALU.mult).then_inc(negmax, 1)
                    if 1 <= j <= N:
                        i = j - 1
                        dve.wait_ge(sc, i + 1)
                        for d in range(2):
                            u = 2 * i + d
                            dve.wait_ge(decayed, u + 1)
                            link(dve, nc.vector.tensor_tensor_reduce(Dm[:, i % 3, d, :], ps[:, i % 2, :], Dm[:, i % 3, d, :],
                                                                     scale, 0.0, ALU.mult, ALU.add, den[:, u:u + 1]))
                            dve.wait_ge(floored, u + 1)
                            nd = den[:, u:u + 1]
                            link(dve, nc.vector.scalar_tensor_tensor(out=rec[:, u:u + 1], in0=nd, scalar=-1.0, in1=nd, op0=ALU.mult, op1=ALU.max))
                            link(dve, nc.vector.tensor_tensor(nd, rec[:, u:u + 1], flr[:, u:u + 1], ALU.max))
                            link(dve, nc.vector.reciprocal(rec[:, u:u + 1], den[:, u:u + 1]))
                        u = 2 * i
                        link(dve, nc.vector.tensor_scalar(Dm[:, i % 3, 0, :], Dm[:, i % 3, 0, :], rec[:, u:u + 1], None, ALU.mult))
                        nc.vector.scalar_tensor_tensor(out=Dm[:, i % 3, 0, :], in0=Dm[:, i % 3, 1, :], scalar=rec[:, u + 1:u + 2],
                                                       in1=Dm[:, i % 3, 0, :], op0=ALU.mult, op1=ALU.add).then_inc(mixed, 1)
                    if j >= 3:
                        i = j - 3
                        h, t = jobs[i]
                        dve.wait_ge(values, i + 1)
                        cs = slice(h * ML_V, (h + 1) * ML_V)
                        nc.vector.tensor_tensor(hs[:, t, cs], ps[:, 6 + i % 2, 0:ML_V], o_gate[:, t, cs], ALU.mult).then_inc(out_done, 1)


def odd_layer(core):
    nc, a, ps = core.nc, core.a, core.ps
    mod, first, col = core.mod, core.first, core.col
    normed(core, "on_", range(NT), lambda k, s: mod[:, 1, 1, k, s:s + 1], lambda k, s: mod[:, 1, 0, k, s:s + 1])
    with ExitStack() as c:
        sb = lambda name, shape: c.enter_context(nc.sbuf_tensor(name, shape, F32))
        v = sb("od_v", [P, NT, ML_H * ML_V])
        o_gate = sb("od_o", [P, LT, ML_H * ML_V])
        z_gate = sb("od_z", [P, LT, ML_H * ML_V])
        with ExitStack() as c2:
            sb2 = lambda name, shape: c2.enter_context(nc.sbuf_tensor(name, shape, F32))
            qT = sb2("od_qT", [P, ML_H, SEQ])
            kT = sb2("od_kT", [P, ML_H, 2 * SEQ])

            def conv(tag, name, chan0, dst, tokens):
                def act_out(act, n, wi, g, src, dve_done):
                    ch = chan0 + n
                    return nc.scalar.activation(dst[:, n, :], src, ACT.Identity, scale=col("o_cw1", ch), bias=col("o_cb", ch))

                def dve_out(dve, n, wi, g, src):
                    ch = chan0 + n
                    return side_taps(core, dve, dst[:, n, :], src, col("o_cw0", ch), col("o_cw2", ch))
                project(core, tag, [[("features", m, 0, tokens) for m in range(4)]] * 2, first[name], lambda n: "ad", act_out, dve_out)

            conv("oq_", "o_q", 0, qT, SEQ)
            conv("ok_", "o_k", 8, kT, 2 * SEQ)

            def plain(dst):
                return (lambda act, n, wi, g, src, w: nc.scalar.activation(dst[:, g[1], wi * BANK:(wi + 1) * BANK], src, ACT.Copy),
                        lambda dve, n, wi, g, src: nc.vector.tensor_copy(dst[:, g[1], wi * BANK:(wi + 1) * BANK], src))

            def through(dst, func):
                return (lambda act, n, wi, g, src, w: nc.scalar.activation(dst[:, g[1], wi * BANK:(wi + 1) * BANK], src, func), None)
            select = core.x[0:40, LT:NT, :].rearrange("p t d -> p (t d)")
            scratch = o_gate[0:40].rearrange("p t d -> p (t d)")[:, 0:12 * SEQ].rearrange("p (n t) -> p n t", n=6)
            aT = sb2("od_aT", [40, 2 * SEQ])
            cumT = sb2("od_cumT", [P, LT, 40])
            masks = sb2("od_masks", [P, 2 * LT + 1, SEQ])
            with ExitStack() as c3:
                before, after = mlstm_gates(core, c3, aT, cumT, masks, select, scratch)

                project(core, "ov_", [[("tokens", t, 0, BANK) for t in range(NT)]] * 4, first["o_v"], lambda n: "a", *plain(v),
                        banks=range(3, 8), before=before, after=after)

            def silu_qk(block):
                @block.scalar
                def _(act):
                    for z in (qT, kT):
                        for h in range(0, ML_H, 4):
                            last = nc.scalar.activation(z[:, h:h + 4, :], z[:, h:h + 4, :], ACT.Silu)
                    core.act_chain(act, last)
            project(core, "oo_", [[("tokens", t, 0, BANK) for t in range(LT)]] * 4, first["o_o"], lambda n: "a",
                    *through(o_gate, ACT.Sigmoid), before=silu_qk)
            project(core, "oz_", [[("tokens", t, 0, BANK) for t in range(LT)]] * 4, first["o_z"], lambda n: "a", *through(z_gate, ACT.Silu))
            hs = core.hT[:].rearrange("p k t -> p (k t)").rearrange("p (t d) -> p t d", t=LT)
            mlstm(core, qT, kT, v, o_gate, aT, cumT, masks, select, hs)
        flat_v = v[:].rearrange("p t d -> p (t d)")
        hsT = flat_v[:, 0:4096].rearrange("p (k t) -> p k t", k=16)
        sq = flat_v[:, 4096:6144]
        gain = flat_v[:, 6144:8192]
        st = sb("od_st", [P, 3, LT * ML_H])
        gain_in, meaned, rooted = core.expect_tables(1), core.sem("od_meaned"), core.sem("od_rooted")
        with core.phase() as block:
            @block.gpsimd
            def _(pool):
                pool.dma_start(gain, row_bcast(a, "head_norm")).then_inc(core.tables_in, 16)

            @block.scalar
            def _(act):
                act.wait_ge(meaned, 1)
                nc.scalar.activation(st[:, 1, :], st[:, 1, :], ACT.Sqrt).then_inc(rooted, 1)

            @block.vector
            def _(dve):
                link = core.dve_chain
                for t in range(LT):
                    link(dve, nc.vector.tensor_tensor(sq, hs[:, t, :], hs[:, t, :], ALU.mult))
                    link(dve, nc.vector.tensor_reduce(st[:, 0, t * ML_H:(t + 1) * ML_H], sq.rearrange("p (h d) -> p h d", h=ML_H), AX.X, ALU.add))
                nc.vector.tensor_scalar(st[:, 1, :], st[:, 0, :], 1.0 / ML_V, EPS, ALU.mult, ALU.add).then_inc(meaned, 1)
                dve.wait_ge(core.tables_in, gain_in)
                for t in range(LT):
                    link(dve, nc.vector.tensor_tensor(z_gate[:, t, :], z_gate[:, t, :], gain, ALU.mult))
                    link(dve, nc.vector.tensor_tensor(hs[:, t, :], hs[:, t, :], z_gate[:, t, :], ALU.mult))
                dve.wait_ge(rooted, 1)
                link(dve, nc.vector.reciprocal(st[:, 2, :], st[:, 1, :]))
                for t in range(LT):
                    x = hs[:, t, :].rearrange("p (h d) -> p h d", h=ML_H)
                    r = st[:, 2, t * ML_H:(t + 1) * ML_H].unsqueeze(2).broadcast_to([P, ML_H, ML_V])
                    link(dve, nc.vector.tensor_tensor(x, x, r, ALU.mult))
        turn(core, "od_t_", [([hs[:, t, k * P:(k + 1) * P] for k in (2 * q, 2 * q + 1) for t in range(LT)],
                              hsT[:, 2 * q:2 * q + 2, :].rearrange("p k t -> p (k t)"), None) for q in range(8)])
        down(core, "od_d_", first["o_out"], hsT, LT, 4)
    gated_residual(core, "or_", LT, [2, 2])


def retention(core, tag, rT, rv, decay, out):
    nc, ps = core.nc, core.ps
    with ExitStack() as c:
        sc = c.enter_context(nc.sbuf_tensor(tag + "sc", [P, 2, SEQ], F32))
        scT = c.enter_context(nc.sbuf_tensor(tag + "scT", [P, 2, SEQ], F32))
        scores, decayed, turned, back, values, out_done = (core.sem(tag + n) for n in ("scores", "decayed", "turned", "back", "values", "out_done"))
        jobs = [(h, t) for h in range(RET_H) for t in range(LT)]
        N = len(jobs)
        with core.phase() as block:
            @block.tensor
            def _(pe):
                for j in range(N + 2):
                    if j < N:
                        h, t = jobs[j]
                        nk = (t + 1) * P
                        if j >= 2:
                            pe.wait_ge(decayed, j - 1)
                        nc.tensor.matmul(ps[:, j % 2, 0:nk], rT[0:RET_QK, h, t * P:(t + 1) * P], rT[0:RET_QK, RET_H + h, 0:nk],
                                         start=True, stop=True).then_inc(scores, 1)
                    if 1 <= j <= N:
                        i = j - 1
                        pe.wait_ge(decayed, i + 1)
                        if i >= 2:
                            pe.wait_ge(back, i - 1)
                        for b in range(jobs[i][1] + 1):
                            mm = nc.tensor.transpose(ps[:, 2 + i % 2, b * P:(b + 1) * P], sc[:, i % 2, b * P:(b + 1) * P], core.ident[:])
                        mm.then_inc(turned, 1)
                    if j >= 2:
                        i = j - 2
                        h, t = jobs[i]
                        pe.wait_ge(back, i + 1)
                        if i >= 2:
                            pe.wait_ge(out_done, i - 1)
                        for b in range(t + 1):
                            mm = nc.tensor.matmul(ps[:, 4 + i % 2, 0:RET_V], scT[:, i % 2, b * P:(b + 1) * P],
                                                  rv[:, b, h * RET_V:(h + 1) * RET_V], start=(b == 0), stop=(b == t))
                        mm.then_inc(values, 1)

            @block.scalar
            def _(act):
                for i in range(N):
                    nk = (jobs[i][1] + 1) * P
                    act.wait_ge(turned, i + 1)
                    if i >= 2:
                        act.wait_ge(values, i - 1)
                    nc.scalar.activation(scT[:, i % 2, 0:nk], ps[:, 2 + i % 2, 0:nk], ACT.Copy).then_inc(back, 1)

            @block.vector
            def _(dve):
                for j in range(N + 2):
                    if j < N:
                        h, t = jobs[j]
                        nk = (t + 1) * P
                        dve.wait_ge(scores, j + 1)
                        if j >= 2:
                            dve.wait_ge(turned, j - 1)
                        nc.vector.tensor_tensor(sc[:, j % 2, 0:nk], ps[:, j % 2, 0:nk], decay[:, t, h * SEQ:h * SEQ + nk], ALU.mult).then_inc(decayed, 1)
                    if j >= 2:
                        h, t = jobs[j - 2]
                        dve.wait_ge(values, j - 1)
                        nc.vector.tensor_copy(out(t, h), ps[:, 4 + j % 2, 0:RET_V]).then_inc(out_done, 1)


def block2(core, l):
    nc, a, ps = core.nc, core.a, core.ps
    first, col, x = core.first, core.col, core.x
    T = f"b{l}_"
    with ExitStack() as c:
        sb = lambda name, shape, c=c: c.enter_context(nc.sbuf_tensor(T + name, shape, F32))
        gates = sb("gates", [P, LT, 3 * D])
        rg = sb("rg", [P, LT, 512])
        oa = sb("oa", [P, LT, 1536])
        with ExitStack() as c2:
            sb2 = lambda name, shape, c=c2: c.enter_context(nc.sbuf_tensor(T + name, shape, F32))
            lr = sb2("low", [P, LT, IN2_FIRST])
            moba = sb2("moba", [P, LT, 1536])
            rqk = sb2("rqk", [P, LT, 512])
            rv = sb2("rv", [P, LT, 512])
            tabs = x[:, LT:NT, 768:992]
            tmp = core.hT[:, 0:2, :]
            st = sb2("st", [P, 3, 4])
            c_in = ExitStack()
            h = Split(nc, c_in, T + "h", [P, KC, SEQ])
            weights = SplitWeights(core, c_in, T + "i", first[f"in{l}a"], 13)
            normed(core, T + "n_", range(LT), lambda k, s: col(f"an{l}", k), into=h, weights=weights)
            toks = lambda w: [("tokens", t, 0, w) for t in range(LT)]

            def copies(dst_of):
                return (lambda act, n, wi, g, src, w: nc.scalar.activation(dst_of(wi, g[1]), src, ACT.Copy),
                        lambda dve, n, wi, g, src: nc.vector.tensor_copy(dst_of(wi, g[1]), src))

            def where(wi, t):
                if wi == 0:
                    return lr[:, t, :]
                if wi <= 3:
                    return moba[:, t, (wi - 1) * BANK:wi * BANK]
                return rqk[:, t, :] if wi == 4 else rv[:, t, :]
            project_split(core, T + "p_", weights, 0, h, [toks(IN2_FIRST)] + [toks(BANK)] * 5, lambda n: "ad"[n % 2], *copies(where))
            project_split(core, T + "rg_", weights, 12, h, [toks(BANK)], lambda n: "a",
                    lambda act, n, wi, g, src, w: nc.scalar.activation(rg[:, g[1], :], src, ACT.Silu), None)
            with ExitStack() as c3:
                sb3 = lambda name, shape: sb2(name, shape, c3)
                uq = x[:, LT:NT, 0:768]
                tabs_in = core.expect_tables(3)
                meaned, rooted = core.sem(T + "meaned"), core.sem(T + "rooted")
                o_moba, o_ret = 64, 96

                def norm_and_rotate(block):
                    @block.gpsimd
                    def _(pool):
                        at = 0
                        for name, w in (("rope_mla", 64), ("rope_moba", 32), ("rope_ret", 128)):
                            pool.dma_start(tabs[:, :, at:at + w], a[name].rearrange("(t p) n -> p t n", p=P)).then_inc(core.tables_in, 16)
                            at += w

                    @block.scalar
                    def _(act):
                        act.wait_ge(meaned, 1)
                        nc.scalar.activation(st[:, 1, :], st[:, 1, :], ACT.Sqrt).then_inc(rooted, 1)

                    @block.vector
                    def _(dve):
                        link = core.dve_chain
                        parts = [(t, i, lo, w) for t in range(LT) for i, (lo, w) in enumerate(((0, MLA_Q), (MLA_Q, MLA_KV)))]
                        for t, i, lo, w in parts:
                            link(dve, nc.vector.tensor_tensor_reduce(tmp[:, 0, 0:w], lr[:, t, lo:lo + w], lr[:, t, lo:lo + w], 1.0 / w, EPS,
                                                                     ALU.mult, ALU.add, st[:, 1, 2 * t + i:2 * t + i + 1]))
                        nc.vector.tensor_copy(st[:, 0, 0:1], st[:, 1, 0:1]).then_inc(meaned, 1)
                        dve.wait_ge(core.tables_in, tabs_in)
                        for t in range(LT):
                            rope(core, dve, moba[:, t, 0:1024].rearrange("p (h d) -> p h d", h=16)[:, :, 0:16],
                                 tabs[:, t, o_moba:o_moba + 32], tmp, 16, 16)
                            rope(core, dve, rqk[:, t, :].rearrange("p (h d) -> p h d", h=8), tabs[:, t, o_ret:o_ret + 128], tmp, 8, 64)
                            rope(core, dve, lr[:, t, 384:416].unsqueeze(1), tabs[:, t, 0:64], tmp, 1, 32)
                        dve.wait_ge(rooted, 1)
                        link(dve, nc.vector.reciprocal(st[:, 2, :], st[:, 1, :]))
                        for t, i, lo, w in parts:
                            link(dve, nc.vector.tensor_scalar(lr[:, t, lo:lo + w], lr[:, t, lo:lo + w], st[:, 2, 2 * t + i:2 * t + i + 1], None, ALU.mult))
                project_split(core, T + "g_", weights, 14, h, [toks(BANK)] * 6, lambda n: "a",
                        lambda act, n, wi, g, src, w: nc.scalar.activation(gates[:, g[1], wi * BANK:(wi + 1) * BANK], src, ACT.Sigmoid), None,
                        before=norm_and_rotate, rest_on="gpsimd")
                c_in.close()
                ukv = sb2("ukv", [P, LT, 1024])
                mT = sb2("mT", [96, 2 * 8, SEQ])
                rT = sb2("rT", [64, 8, SEQ])
                lowT = sb3("lowT", [P, 3, SEQ])
                kk = sb3("kk", [P, LT, 8, 96])
                bT = core.hT[0:64].rearrange("p k t -> p (k t)").rearrange("p (h t) -> p h t", h=16)
                turn(core, T + "lt_", [([lr[:, t, k * P:(k + 1) * P] for t in range(LT)], lowT[:, k, :],
                                        col(f"qn{l}", k) if k < 2 else col(f"kvn{l}")) for k in range(3)])
                up_done, up_act, up_dve = core.sem(T + "up_done"), core.sem(T + "up_act"), core.sem(T + "up_dve")
                wi = first[f"up{l}"]
                with core.phase() as block:
                    @block.sync
                    def _(sp):
                        core.load_ahead(sp, wi, up_done, [8])

                    @block.tensor
                    def _(pe):
                        wq, wkv = core.weight(pe, wi, 0), core.weight(pe, wi, 1)
                        for t in range(LT):
                            for j in range(2):
                                for k in range(2):
                                    mm = nc.tensor.matmul(ps[:, 2 * t + j, 0:384], lowT[:, k, t * P:(t + 1) * P],
                                                          wq[:, k, j * 384:(j + 1) * 384], start=(k == 0), stop=(k == 1))
                                mm.then_inc(up_done, 1)
                        for t in range(LT):
                            for j in range(2):
                                nc.tensor.matmul(ps[:, 4 + 2 * t + j, :], lowT[:, 2, t * P:(t + 1) * P],
                                                 wkv[:, 0, j * BANK:(j + 1) * BANK], start=True, stop=True).then_inc(up_done, 1)

                    @block.scalar
                    def _(act):
                        for t in range(LT):
                            for j in range(2):
                                act.wait_ge(up_done, 4 + 2 * t + j + 1)
                                last = nc.scalar.activation(ukv[:, t, j * BANK:(j + 1) * BANK], ps[:, 4 + 2 * t + j, :], ACT.Copy)
                            core.act_chain(act, last)
                            nc.scalar.activation(kk[:, t, :, 0:64], ukv[:, t, :].rearrange("p (h d) -> p h d", h=8)[:, :, 0:64], ACT.Copy).then_inc(up_act, 1)
                            core.act_chain(act, nc.scalar.activation(kk[:, t, :, 64:96], lr[:, t, 384:416].unsqueeze(1).broadcast_to([P, 8, 32]), ACT.Copy))

                    @block.vector
                    def _(dve):
                        for t in range(LT):
                            for j in range(2):
                                dve.wait_ge(up_done, 2 * t + j + 1)
                                last = nc.vector.tensor_copy(uq[:, t, j * 384:(j + 1) * 384], ps[:, 2 * t + j, 0:384])
                            core.dve_chain(dve, last)
                            rope(core, dve, uq[:, t, :].rearrange("p (h d) -> p h d", h=8)[:, :, 64:96], tabs[:, t, 0:64], tmp, 8, 32)
                flat = lambda z: z.rearrange("p h t -> p (h t)")
                blocks = []
                for h in range(0, 8, 2):
                    blocks.append(([uq[:, t, g * 96:(g + 1) * 96] for g in (h, h + 1) for t in range(LT)], flat(mT[:, h:h + 2, :]), None))
                    blocks.append(([kk[:, t, g, :] for g in (h, h + 1) for t in range(LT)], flat(mT[:, 8 + h:10 + h, :]), None))
                for h in range(0, 16, 2):
                    blocks.append(([moba[:, t, g * 64:(g + 1) * 64] for g in (h, h + 1) for t in range(LT)], flat(bT[:, h:h + 2, :]), None))
                for h in range(0, 8, 2):
                    blocks.append(([rqk[:, t, g * 64:(g + 1) * 64] for g in (h, h + 1) for t in range(LT)], flat(rT[:, h:h + 2, :]), None))
                turn(core, T + "t_", blocks)
            spare = x[:, LT:NT, :].rearrange("p t d -> p (t d)")
            causal = spare[:, 0:LT * SEQ].rearrange("p (t n) -> p t n", t=LT)
            gn = spare[:, 512:1536].rearrange("p (i n) -> p i n", i=2)
            decay = core.ga[:, 0:LT, :]
            tab_in = core.expect_tables(4)
            with core.phase() as block:
                @block.gpsimd
                def _(pool):
                    pool.dma_start(causal, a["causal"].rearrange("(t p) n -> p t n", p=P)).then_inc(core.tables_in, 16)
                    pool.dma_start(decay, a["ret_decay"].rearrange("(t p) n -> p t n", p=P)).then_inc(core.tables_in, 16)
                    pool.dma_start(gn[:, 0, :], row_bcast(a, f"gn_w{l}")).then_inc(core.tables_in, 16)
                    pool.dma_start(gn[:, 1, :], row_bcast(a, f"gn_b{l}")).then_inc(core.tables_in, 16)
                    pool.wait_ge(core.tables_in, tab_in)
            for name, qk, off, vsrc, scale in (("ma_", mT, 0, lambda b, h: ukv[:, b, h * 128 + 64:h * 128 + 128], 96 ** -0.5),
                                               ("mo_", bT, 512, lambda b, h: moba[:, b, 1024 + h * 64:1088 + h * 64], 64 ** -0.5)):
                jobs = [dict(q=qk[:, h, t * P:(t + 1) * P], k=qk[:, 8 + h, 0:(t + 1) * P], mask=causal[:, t, 0:(t + 1) * P],
                             feat=False, v=[vsrc(b, h) for b in range(t + 1)], out=oa[:, t, off + h * 64:off + (h + 1) * 64])
                        for h in range(8) for t in range(LT)]
                softmax_attention(core, T + name, jobs, scale)
            retention(core, T + "re_", rT, rv, decay, lambda t, h: oa[:, t, 1024 + h * P:1024 + (h + 1) * P])
            st = sb2("gst", [P, 4, LT * RET_H])
            sq = sb2("gsq", [P, 512])
            meaned, rooted = core.sem(T + "gn_meaned"), core.sem(T + "gn_rooted")
            with core.phase() as block:
                @block.scalar
                def _(act):
                    act.wait_ge(meaned, 1)
                    nc.scalar.activation(st[:, 2, :], st[:, 2, :], ACT.Sqrt).then_inc(rooted, 1)

                @block.vector
                def _(dve):
                    link = core.dve_chain
                    heads = lambda t: oa[:, t, 1024:1536].rearrange("p (h d) -> p h d", h=RET_H)
                    s4 = lambda n, t: st[:, n, t * RET_H:(t + 1) * RET_H]
                    wide = lambda z: z.unsqueeze(2).broadcast_to([P, RET_H, RET_V])
                    for t in range(LT):
                        link(dve, nc.vector.tensor_reduce(s4(0, t), heads(t), AX.X, ALU.add))
                        link(dve, nc.vector.tensor_scalar(s4(1, t), s4(0, t), 1.0 / RET_V, None, ALU.mult))
                        link(dve, nc.vector.tensor_tensor(heads(t), heads(t), wide(s4(1, t)), ALU.subtract))
                        link(dve, nc.vector.tensor_tensor(sq[:], oa[:, t, 1024:1536], oa[:, t, 1024:1536], ALU.mult))
                        link(dve, nc.vector.tensor_reduce(s4(0, t), sq[:].rearrange("p (h d) -> p h d", h=RET_H), AX.X, ALU.add))
                    nc.vector.tensor_scalar(st[:, 2, :], st[:, 0, :], 1.0 / RET_V, GN_EPS, ALU.mult, ALU.add).then_inc(meaned, 1)
                    dve.wait_ge(rooted, 1)
                    link(dve, nc.vector.reciprocal(st[:, 3, :], st[:, 2, :]))
                    for t in range(LT):
                        o = oa[:, t, 1024:1536]
                        link(dve, nc.vector.tensor_tensor(heads(t), heads(t), wide(s4(3, t)), ALU.mult))
                        link(dve, nc.vector.tensor_tensor(o, o, gn[:, 0, :], ALU.mult))
                        link(dve, nc.vector.tensor_tensor(o, o, gn[:, 1, :], ALU.add))
                        link(dve, nc.vector.tensor_tensor(o, o, rg[:, t, :], ALU.mult))
        oT = Split(nc, c, T + "oT", [P, 12, SEQ])
        mergedT = Split(nc, c, T + "mergedT", [P, KC, SEQ])
        weights = SplitWeights(core, c, T + "b", first[f"b_mla{l}"], 5)
        merged = x[:, LT:NT, :]
        part = core.hT[:, 0:2, :]
        turn_split(core, T + "ot_", [([oa[:, t, k * P:(k + 1) * P] for k in (2 * q, 2 * q + 1) for t in range(LT)],
                                      np.s_[:, 2 * q:2 * q + 2, :]) for q in range(6)], oT, weights)
        b_done, b_read, b_used = (core.sem(T + n) for n in ("branch_done", "branch_read", "branch_half_used"))
        with core.phase() as block:
            @block.sync
            def _(sp):
                weights.load_ahead(sp, 0, 6)

            @block.tensor
            def _(pe):
                for u in range(6):
                    w = weights.parts(pe, u)
                    for q in range(4):
                        t, j, n = q // 2, q % 2, 4 * (u // 2) + q
                        if n >= 8 and u % 2 == 0:
                            pe.wait_ge(b_read, n - 7)
                        for k in range(2):
                            mm = split_matmul(nc, ps[:, n % 8, :], oT.parts(np.s_[:, 2 * u + k, t * P:(t + 1) * P]),
                                              [z[:, k, j * BANK:(j + 1) * BANK] for z in w], u % 2 == 0 and k == 0, u % 2 == 1 and k == 1)
                        if u % 2:
                            mm.then_inc(b_done, 1)
                    if u % 2 == 0:
                        mm.then_inc(b_used, 1)

            @block.scalar
            def _(act):
                weights.take_lead(act, weights.B - 1)
                for u in range(5):
                    if u % 2:
                        act.wait_ge(b_done, 4 * (u // 2 + 1))
                    else:
                        act.wait_ge(b_used, u // 2 + 1)
                    weights.take_lead(act, weights.B + u)

            @block.vector
            def _(dve):
                weights.take_rest(dve, weights.B - 1)
                for b in range(3):
                    weights.take_rest(dve, weights.B + 2 * b)
                    if b < 2:
                        weights.take_rest(dve, weights.B + 2 * b + 1)
                    for n in range(4 * b, 4 * b + 4):
                        t, j = n // 2 % 2, n % 2
                        dve.wait_ge(b_done, n + 1)
                        g = gates[:, t, b * D + j * BANK:b * D + (j + 1) * BANK]
                        m = merged[:, t, j * BANK:(j + 1) * BANK]
                        if b == 0:
                            nc.vector.tensor_tensor(m, ps[:, n % 8, :], g, ALU.mult).then_inc(b_read, 1)
                        else:
                            nc.vector.tensor_tensor(part[:, n % 2, :], ps[:, n % 8, :], g, ALU.mult).then_inc(b_read, 1)
                            dve.wait_ge(b_read, n + 1)
                            core.dve_chain(dve, nc.vector.tensor_tensor(m, m, part[:, n % 2, :], ALU.add))
        turn_split(core, T + "mt_", [([merged[:, t, k * P:(k + 1) * P] for k in (2 * q, 2 * q + 1) for t in range(LT)],
                                      np.s_[:, 2 * q:2 * q + 2, :]) for q in range(4)], mergedT)
        down_split(core, T + "wo_", weights, 6, mergedT, LT, 2)
    add_banks(core, T + "r1_")
    with ExitStack() as c:
        upT = Split(nc, c, T + "upT", [P, D_FF // P, SEQ])
        weights = SplitWeights(core, c, T + "m", first[f"mup{l}"], 16)
        with ExitStack() as c2:
            h = Split(nc, c2, T + "h2", [P, KC, SEQ])
            normed(core, T + "n2_", range(LT), lambda k, s: col(f"mn{l}", k), into=h, weights=weights)
            way = core.hT[:, 0:4, 0:SEQ]

            def relu_squared(act, n, wi, g, src, dve_done):
                if n >= 4:
                    dve_done(n - 4)
                core.act_chain(act, nc.scalar.activation(way[:, n % 4, :], src, ACT.Relu))
                return nc.scalar.activation(way[:, n % 4, :], way[:, n % 4, :], ACT.Square)

            def split_up(dve, n, wi, g, src):
                at = np.s_[:, n, :]
                core.dve_chain(dve, upT.take_lead(dve, at, way[:, n % 4, :]))
                return upT.take_rest(dve, at, way[:, n % 4, :])
            project_split(core, T + "mu_", weights, 0, h, [[("features", m, 0, SEQ) for m in range(4)]] * 8, lambda n: "ad",
                          relu_squared, split_up)
        down_split(core, T + "md_", weights, 16, upT, LT, 8)
    add_banks(core, T + "r2_")


def add_banks(core, tag):
    nc = core.nc
    with core.phase() as block:
        @block.vector
        def _(dve):
            for t in range(LT):
                for j in range(2):
                    xs = core.x[:, t, j * BANK:(j + 1) * BANK]
                    last = nc.vector.tensor_tensor(xs, xs, core.ps[:, 2 * t + j, :], ALU.add)
            core.dve_chain(dve, last)


def final(core, out):
    nc, a, x = core.nc, core.a, core.x
    with ExitStack() as c:
        sq = c.enter_context(nc.sbuf_tensor("f_sq", [P, D], F32))
        gain = c.enter_context(nc.sbuf_tensor("f_gain", [P, D], F32))
        st = c.enter_context(nc.sbuf_tensor("f_st", [P, 3, LT], F32))
        gain_in = core.expect_tables(1)
        meaned, rooted, ready = (core.sem("f_" + n) for n in ("meaned", "rooted", "ready"))
        stored = core.stored
        with core.phase() as block:
            @block.gpsimd
            def _(pool):
                pool.dma_start(gain[:], row_bcast(a, "final")).then_inc(core.tables_in, 16)

            @block.scalar
            def _(act):
                act.wait_ge(meaned, 1)
                nc.scalar.activation(st[:, 1, :], st[:, 1, :], ACT.Sqrt).then_inc(rooted, 1)

            @block.vector
            def _(dve):
                link = core.dve_chain
                for t in range(LT):
                    link(dve, nc.vector.tensor_tensor_reduce(sq[:], x[:, t, :], x[:, t, :], 1.0 / D, EPS, ALU.mult, ALU.add, st[:, 1, t:t + 1]))
                nc.vector.tensor_copy(st[:, 0, 0:1], st[:, 1, 0:1]).then_inc(meaned, 1)
                dve.wait_ge(rooted, 1)
                link(dve, nc.vector.reciprocal(st[:, 2, :], st[:, 1, :]))
                dve.wait_ge(core.tables_in, gain_in)
                for t in range(LT):
                    nc.vector.scalar_tensor_tensor(out=x[:, t, :], in0=x[:, t, :], scalar=st[:, 2, t:t + 1], in1=gain[:],
                                                   op0=ALU.mult, op1=ALU.mult).then_inc(ready, 1)

            @block.sync
            def _(sp):
                for t in range(LT):
                    sp.wait_ge(ready, t + 1)
                    sp.dma_start(out[0, t * P:(t + 1) * P, :], x[:, t, :]).then_inc(stored, 16)
                sp.wait_ge(stored, 16 * LT)


INS = ['x', 'c', 'ctx', 'c_ctx', 'w_mod', 'b_mod', 'g_pre', 'g_post', 'e_w_in', 'e_conv_w', 'e_conv_b', 'e_filt_w1',
       'e_filt_b1', 'e_filt_freq', 'e_filt_w2', 'e_filt_b2', 'e_filt_w3', 'e_hy_bias', 'e_q_norm', 'e_k_norm',
       'e_w_out', 'o_w_in', 'o_conv_w', 'o_conv_b', 'o_gate_b', 'o_head_norm', 'o_w_out', 'attn_norm_2', 'w_in_2',
       'mla_q_norm_2', 'mla_kv_norm_2', 'mla_w_q_up_2', 'mla_w_kv_up_2', 'ret_gn_w_2', 'ret_gn_b_2',
       'w_branch_mla_2', 'w_branch_moba_2', 'w_branch_ret_2', 'w_out_2', 'mlp_norm_2', 'w_mlp_up_2',
       'w_mlp_down_2', 'final_norm_2']
DIRECT = ['x', 'ctx', 'w_mod', 'e_w_in', 'e_filt_w1', 'e_filt_w2', 'e_filt_w3', 'e_w_out', 'o_w_in', 'o_w_out',
          'w_in_2', 'mla_w_q_up_2', 'mla_w_kv_up_2', 'w_branch_mla_2', 'w_branch_moba_2', 'w_branch_ret_2', 'w_out_2',
          'w_mlp_up_2', 'w_mlp_down_2']


def feature_columns(p):
    out = np.zeros((P, NCOL), np.float32)

    def put(name, v):
        v = np.asarray(v).reshape(-1, P)
        at = COL_AT[name]
        out[:, at:at + v.shape[0]] = v.T

    def put_short(name, v, at_partition=0):
        out[at_partition:at_partition + len(v), COL_AT[name]] = v

    put("c", p["c"])
    put("c_ctx", p["c_ctx"])
    for l in range(DEPTH):
        put(f"b_sh{l}", p["b_mod"][l, 0:D])
        put(f"b_sc{l}", p["b_mod"][l, D:2 * D])
        put(f"g_pre{l}", p["g_pre"][l])
        put(f"an{l}", p["attn_norm_2"][l])
        put(f"mn{l}", p["mlp_norm_2"][l])
        put(f"qn{l}", p["mla_q_norm_2"][l])
        put(f"kvn{l}", p["mla_kv_norm_2"][l])
    for i in range(3):
        put(f"e_cw{i}", p["e_conv_w"][0, i])
        put(f"o_cw{i}", p["o_conv_w"][0, i])
    put("e_cb", p["e_conv_b"][0])
    put("o_cb", p["o_conv_b"][0])
    put("hy_bias", p["e_hy_bias"][0])
    put_short("f_b1", p["e_filt_b1"][0])
    put_short("f_b2", p["e_filt_b2"][0])
    put_short("f_fr", p["e_filt_freq"][0])
    gb = p["o_gate_b"][0]
    put_short("gb_i", gb[0:8])
    put_short("gb_f", gb[8:16])
    put_short("gb_i", gb[16:24], 32)
    put_short("gb_f", gb[24:32], 32)
    return out


def spread_rows(p):
    parts = {"b_ga0": p["b_mod"][0, 2 * D:], "b_ga1": p["b_mod"][1, 2 * D:], "g_post0": p["g_post"][0],
             "g_post1": p["g_post"][1], "q_norm": p["e_q_norm"][0], "k_norm": p["e_k_norm"][0],
             "head_norm": p["o_head_norm"][0], "gn_w0": p["ret_gn_w_2"][0], "gn_b0": p["ret_gn_b_2"][0],
             "gn_w1": p["ret_gn_w_2"][1], "gn_b1": p["ret_gn_b_2"][1], "final": p["final_norm_2"]}
    return np.concatenate([np.asarray(parts[k]).reshape(-1) for k in ROW_AT]).astype(np.float32)


def tables():
    out = {"ident": np.eye(P), "pick": np.kron(np.eye(2), np.ones((1, P)))}
    n = SEQ
    t = np.arange(2 * n)[:, None]
    f = np.arange(n)[None, :]
    cos = np.cos(2 * np.pi * ((t * f) % (2 * n)) / (2 * n))
    sin = -np.sin(2 * np.pi * ((t * f) % (2 * n)) / (2 * n))
    sin[:, 0] = (-1.0) ** t[:, 0]
    full = np.concatenate([cos, sin], 1)
    back_taps = full[(2 * n - np.arange(n)) % (2 * n)].copy()
    back_taps[0] = 0.0
    out["dft"] = np.concatenate([full[:n], back_taps], 0)
    inv = full[:n].T * (2.0 / (2 * n))
    inv[0] *= 0.5
    inv[n] *= 0.5
    out["idft"] = inv
    out["tap_ones"] = np.concatenate([np.ones(n), [0.0], np.ones(n - 1)]).reshape(4, P).T
    bands = np.linspace(1e-4, 15, 16, dtype=np.float32)
    ang = np.float32(2.0 * math.pi / n) * np.arange(n, dtype=np.float32)[:, None] * bands
    tt = np.linspace(0.0, 1.0, n, dtype=np.float32)[:, None]
    out["z_t"] = np.concatenate([tt, np.cos(ang), -np.sin(ang)], 1).T
    deltas = np.linspace(math.log(1e-2) / 1.5, math.log(1e-2) / 0.3, HY, dtype=np.float32)
    out["decay"] = np.exp(-tt * np.abs(deltas))

    def rot(pos, dim, inv_freq, reps):
        a = pos.astype(np.float32)[:, None] * inv_freq.astype(np.float32)
        return (np.tile(np.concatenate([np.cos(a), np.cos(a)], 1), (1, reps)),
                np.tile(np.concatenate([-np.sin(a), np.sin(a)], 1), (1, reps)))

    nf = DH // 4
    inv_freq = 10000.0 ** (-np.arange(nf) / nf)
    pos = np.arange(SEQ)
    c0, s0 = rot(pos // 64, 64, inv_freq, 1)
    c1, s1 = rot(pos % 64, 64, inv_freq, 1)
    out["rope_e"] = np.concatenate([c0, c1, s0, s1], 1)
    for name, dim, theta, reps in (("rope_mla", 32, 500000.0, 1), ("rope_moba", 16, 500000.0, 1), ("rope_ret", 64, 10000.0, 1)):
        cc, ss = rot(pos, dim, 1.0 / theta ** (np.arange(0, dim, 2) / dim), reps)
        out[name] = np.concatenate([cc, ss], 1)
    q, k = np.arange(SEQ)[:, None], np.arange(SEQ)[None, :]
    out["causal"] = np.where(k <= q, 0.0, NEG)
    out["anti"] = np.where(k >= q, 0.0, NEG)
    lg = np.log(1.0 - 2.0 ** (-5.0 - np.arange(RET_H)))
    out["ret_decay"] = np.concatenate([np.where(k <= q, np.exp(g * np.maximum(q - k, 0)), 0.0) for g in lg], 1) * RET_QK ** -0.5
    sel = np.zeros((40, 16, P))
    for d in range(2):
        for h in range(8):
            sel[32 * d + h, 8 * d + h] = 1.0
    out["select"] = sel.reshape(40, 16 * P)
    return {k2: np.ascontiguousarray(v, np.float32) for k2, v in out.items()}


def make(nc, arrays_shapes, n_phases=None, dump=None):
    a = {}
    for name, shape in arrays_shapes.items():
        a[name] = nc.dram_tensor(f"in_{name}", shape, F32, kind="ExternalInput").ap()
    out = nc.dram_tensor("out_0", (1, SEQ, D), F32, kind="ExternalOutput").ap()
    program(nc, a, out, n_phases, dump)
    return out


def host_arrays(p):
    arrays = {name: np.ascontiguousarray(p[name]) for name in DIRECT}
    arrays["cols"] = feature_columns(p)
    arrays["rows"] = spread_rows(p)
    g = p["o_w_in"][0][:, OD_G:].reshape(KC, P, 2, 2, 8)
    gate_w = np.zeros((P, KC, 2, 40), np.float32)
    gate_w[:, :, :, 0:8] = g[:, :, 0].transpose(1, 0, 2, 3)
    gate_w[:, :, :, 32:40] = g[:, :, 1].transpose(1, 0, 2, 3)
    arrays["gate_w"] = gate_w.reshape(P, KC * 80)
    arrays.update(tables())
    return arrays


def kernel(**inputs):
    import concourse.bacc as bacc
    from concourse.bass_utils import run_bass_kernel_spmd as run

    p = {k: np.asarray(v) for k, v in inputs.items()}
    arrays = host_arrays(p)
    nc = bacc.Bacc("TRN2", target_bir_lowering=False, num_devices=1)
    make(nc, {k: v.shape for k, v in arrays.items()})
    r = run(nc, [{f"in_{k}": v for k, v in arrays.items()}], core_ids=[0])
    return r.results[0]["out_0"]
```

```python
from contextlib import ExitStack, contextmanager
import math

import numpy as np
import concourse.bass as bass
from concourse import mybir

ALU = mybir.AluOpType
ACT = mybir.ActivationFunctionType
AX = mybir.AxisListType
F32 = mybir.dt.float32
F32R = mybir.dt.float32r

P = 128
D = 1024
KC = D // P
SEQ = 256
NT = 2 * SEQ // P
LT = SEQ // P
DEPTH = 2
EPS = 1e-6
GN_EPS = 1e-5
NEG = -1e30

HY = 1024
EV_XV, EV_GHY, EV_Q, EV_KV, EV_GATT = 0, 3072, 4096, 5120, 5632
HEADS, KVH, DH = 8, 2, 128
ML_H, ML_QK, ML_V = 8, 128, 256
OD_K, OD_V, OD_O, OD_Z, OD_G = 1024, 2048, 4096, 6144, 8192

MLA_Q, MLA_KV, MLA_R, MLA_N = 256, 128, 32, 64
IN2_FIRST = MLA_Q + MLA_KV + MLA_R
RET_H, RET_QK, RET_V = 4, 64, 128
D_FF = 4096

SLOTS = 2
BANK = 512

COL_AT = {}
_n = 0
for _name, _w in (("c", 8), ("c_ctx", 8), ("b_sh0", 8), ("b_sc0", 8), ("b_sh1", 8), ("b_sc1", 8),
                  ("g_pre0", 8), ("g_pre1", 8), ("e_cw0", 24), ("e_cw1", 24), ("e_cw2", 24), ("e_cb", 24),
                  ("hy_bias", 8), ("o_cw0", 16), ("o_cw1", 16), ("o_cw2", 16), ("o_cb", 16),
                  ("an0", 8), ("an1", 8), ("mn0", 8), ("mn1", 8), ("qn0", 2), ("qn1", 2), ("kvn0", 1), ("kvn1", 1),
                  ("f_b1", 1), ("f_b2", 1), ("f_fr", 1), ("gb_i", 1), ("gb_f", 1)):
    COL_AT[_name] = _n
    _n += _w
NCOL = _n

ROW_AT = {}
_n = 0
for _name, _w in (("b_ga0", D), ("b_ga1", D), ("g_post0", D), ("g_post1", D), ("q_norm", DH), ("k_norm", DH),
                  ("head_norm", 2048), ("gn_w0", 512), ("gn_b0", 512), ("gn_w1", 512), ("gn_b1", 512),
                  ("final", D)):
    ROW_AT[_name] = (_n, _w)
    _n += _w
NROW = _n


def weight_stream(a):
    items, first = [], {}

    def cols(name, w, starts, width=BANK):
        first[name] = len(items)
        for s in starts:
            items.append([(w[:, s:s + width].rearrange("(k p) n -> p k n", p=P), 0, KC, width)])

    def rows(name, w):
        first[name] = len(items)
        n = w.shape[0] // 512
        for i in range(n):
            items.append([(w[i * 512:(i + 1) * 512, :].rearrange("(k p) n -> p k n", p=P), 0, 4, D)])

    for l in range(DEPTH):
        cols(f"mod{l}", a["w_mod"][l], range(0, 3 * D, BANK))
    w = a["e_w_in"][0]
    cols("e_qkv", w, (EV_Q, EV_Q + 512, EV_KV))
    cols("e_gatt", w, (EV_GATT, EV_GATT + 512))
    cols("e_x1", w, (1024, 1536))
    cols("e_v", w, (2048, 2560))
    cols("e_x0", w, (0, 512))
    cols("e_ghy", w, (EV_GHY, EV_GHY + 512))
    rows("e_out", a["e_w_out"][0])
    w = a["o_w_in"][0]
    cols("o_q", w, (0, 512))
    cols("o_k", w, (OD_K, OD_K + 512))
    cols("o_v", w, range(OD_V, OD_O, BANK))
    cols("o_o", w, range(OD_O, OD_Z, BANK))
    cols("o_z", w, range(OD_Z, OD_G, BANK))
    rows("o_out", a["o_w_out"][0])
    for l in range(DEPTH):
        w = a["w_in_2"][l]
        cols(f"in{l}a", w, (0,), IN2_FIRST)
        cols(f"in{l}", w, range(IN2_FIRST, IN2_FIRST + 12 * BANK, BANK))
        first[f"up{l}"] = len(items)
        items.append([
            (a["mla_w_q_up_2"][l].rearrange("(k p) n -> p k n", p=P), 0, 2, 768),
            (a["mla_w_kv_up_2"][l].rearrange("(k p) n -> p k n", p=P), 1536, 1, 1024)])
        rows(f"b_mla{l}", a["w_branch_mla_2"][l])
        rows(f"b_moba{l}", a["w_branch_moba_2"][l])
        rows(f"b_ret{l}", a["w_branch_ret_2"][l])
        rows(f"out{l}", a["w_out_2"][l])
        cols(f"mup{l}", a["w_mlp_up_2"][l], range(0, D_FF, BANK))
        rows(f"mdn{l}", a["w_mlp_down_2"][l])
    return items, first


class Chain:

    def __init__(self, sem):
        self.sem, self.n = sem, 0

    def __call__(self, eng, ins):
        self.n += 1
        ins.then_inc(self.sem, 1)
        eng.wait_ge(self.sem, self.n)


class Core:

    def __init__(self, nc, a, ctx):
        self.nc, self.a, self.ctx = nc, a, ctx
        self.items, self.first = weight_stream(a)
        sb = lambda name, shape: ctx.enter_context(nc.sbuf_tensor(name, shape, F32))
        self.x = sb("x_res", [P, NT, D])
        self.hT = sb("hT", [P, KC, 2 * SEQ])
        self.ring = sb("weights", [P, SLOTS, 4096])
        self.cols = sb("cols", [P, NCOL])
        self.ident = sb("ident", [P, P])
        self.ga = sb("ga", [P, 3, D])
        self.mod = sb("mod", [P, 2, 2, KC, 2])
        self.small = sb("small", [P, 256])
        self.ps = ctx.enter_context(nc.psum_tensor("psum", [P, 8, BANK], F32))
        keep = lambda name: ctx.enter_context(nc.semaphore(name))
        self.tables_in, self.tables_n = keep("tables_in"), 0
        self.dense_in, self.filter_in = keep("hyena_dense_in"), keep("hyena_filter_in")
        self.stored = keep("result_stored")
        self.lead_ready, self.split_ready, self.n_split = keep("weight_lead_ready"), keep("weight_split_ready"), 0
        self.landed = [keep(f"weight_landed{s}") for s in range(SLOTS)]
        self.dve_chain = Chain(keep("dve_step"))
        self.act_chain = Chain(keep("act_step"))
        self.pool_chain = Chain(keep("pool_step"))
        self.landed_at, total = [], [0] * SLOTS
        for i, pieces in enumerate(self.items):
            total[i % SLOTS] += 16 * len(pieces)
            self.landed_at.append(total[i % SLOTS])
        self.fresh, self.old = ([], ExitStack()), ([], ExitStack())

    def expect_tables(self, n):
        self.tables_n += 16 * n
        return self.tables_n

    def sem(self, name):
        s = self.fresh[1].enter_context(self.nc.semaphore(name))
        self.fresh[0].append(s)
        return s

    @contextmanager
    def phase(self):
        old, self.old = self.old, self.fresh
        self.fresh = ([], ExitStack())
        with self.nc.Block() as block:
            if old[0]:
                @block.gpsimd
                def _(pool):
                    for s in old[0]:
                        pool.sem_clear(s)
            yield block
        old[1].close()

    def col(self, name, i=0, n=1):
        at = COL_AT[name] + i
        return self.cols[:, at:at + n]

    def load_weight(self, eng, i):
        for src, at, k, n in self.items[i]:
            dst = self.ring[:, i % SLOTS, at:at + k * n].rearrange("p (k n) -> p k n", k=k)
            eng.dma_start(dst, src).then_inc(self.landed[i % SLOTS], 16)

    def load_ahead(self, eng, lo, used, values):
        for i, value in enumerate(values):
            if lo + i + SLOTS < len(self.items):
                eng.wait_ge(used, value)
                self.load_weight(eng, lo + i + SLOTS)

    def weight(self, eng, i, piece=0):
        eng.wait_ge(self.landed[i % SLOTS], self.landed_at[i])
        _, at, k, n = self.items[i][piece]
        return self.ring[:, i % SLOTS, at:at + k * n].rearrange("p (k n) -> p k n", k=k)


class Split:

    def __init__(self, nc, c, name, shape):
        self.nc = nc
        self.lead = c.enter_context(nc.sbuf_tensor(name + "_lead", shape, F32R))
        self.rest = c.enter_context(nc.sbuf_tensor(name + "_rest", shape, F32R))

    def take_lead(self, eng, at, src):
        return eng.tensor_copy(self.lead[at], src)

    def take_rest(self, eng, at, src):
        return eng.tensor_tensor(self.rest[at], src, self.lead[at].bitcast(F32), ALU.subtract)

    def parts(self, at):
        return self.lead[at], self.rest[at]


def split_matmul(nc, out, lhs, rhs, start, stop):
    for i, (l, r) in enumerate(((lhs[0], rhs[0]), (lhs[0], rhs[1]), (lhs[1], rhs[0]))):
        mm = nc.tensor.matmul(out, l, r, start=start and i == 0, stop=stop and i == 2)
    return mm


class SplitWeights:

    def __init__(self, core, c, tag, first, n, buffers=2):
        self.core, self.B = core, buffers
        self.units = [(first + i, h) for i in range(n) for h in range(2)]
        self.base = core.n_split
        core.n_split += len(self.units)
        self.buf = Split(core.nc, c, tag + "w", [P, buffers, 2048])

    def size(self, u):
        _, _, k, n = self.core.items[self.units[u][0]][0]
        return k // 2, n

    def raw(self, u):
        i, h = self.units[u]
        k, n = self.size(u)
        return self.core.ring[:, i % SLOTS, h * k * n:(h + 1) * k * n]

    def at(self, u):
        k, n = self.size(u)
        return np.s_[:, u % self.B, 0:k * n]

    def take_lead(self, eng, u):
        if u < len(self.units):
            i = self.units[u][0]
            eng.wait_ge(self.core.landed[i % SLOTS], self.core.landed_at[i])
            self.core.nc.scalar.activation(self.buf.lead[self.at(u)], self.raw(u), ACT.Copy).then_inc(self.core.lead_ready, 1)

    def take_rest(self, eng, u):
        if u < len(self.units):
            eng.wait_ge(self.core.lead_ready, self.base + u + 1)
            self.buf.take_rest(eng, self.at(u), self.raw(u)).then_inc(self.core.split_ready, 1)

    def prime(self, dve):
        for u in range(self.B - 1):
            i = self.units[u][0]
            dve.wait_ge(self.core.landed[i % SLOTS], self.core.landed_at[i])
            self.buf.take_lead(dve, self.at(u), self.raw(u)).then_inc(self.core.lead_ready, 1)
            self.take_rest(dve, u)

    def parts(self, pe, u):
        pe.wait_ge(self.core.split_ready, self.base + u + 1)
        return [z.rearrange("p (k n) -> p k n", k=self.size(u)[0]) for z in self.buf.parts(self.at(u))]

    def load_ahead(self, sp, u0, n):
        for u in range(u0 + 1, u0 + n, 2):
            i = self.units[u][0]
            if i + SLOTS < len(self.core.items):
                sp.wait_ge(self.core.split_ready, self.base + u + 1)
                self.core.load_weight(sp, i + SLOTS)


def setup(core):
    nc, a = core.nc, core.a
    loaded = core.sem("setup_loaded")
    with core.phase() as block:
        @block.sync
        def _(sp):
            sp.dma_start(core.cols[:], a["cols"]).then_inc(loaded, 16)
            sp.dma_start(core.ident[:], a["ident"]).then_inc(loaded, 16)
            for i in range(SLOTS):
                core.load_weight(sp, i)
            sp.wait_ge(loaded, 32)


def row_bcast(a, name):
    at, n = ROW_AT[name]
    return a["rows"][at:at + n].partition_broadcast(P)


def adaln(core):
    nc, a, ps = core.nc, core.a, core.ps
    with ExitStack() as c:
        sb = lambda name, shape: c.enter_context(nc.sbuf_tensor(name, shape, F32))
        cond = sb("cond", [P, KC, 2])
        rows = sb("mod_rows", [2, DEPTH, 3 * D])
        pick = sb("row_pick", [2, 2, P])
        brow = sb("gate_rows", [P, 4, D])
        rows_in = core.expect_tables(5)
        cond_ready, mod_done, row_out = core.sem("cond_ready"), core.sem("mod_done"), core.sem("mod_row_out")
        turned, spread, x_in = (core.sem(n) for n in ("mod_turned", "gate_spread", "x_in"))
        lo = core.first["mod0"]
        gates = [(0, 0), (0, 1), (1, 0)]
        with core.phase() as block:
            @block.sync
            def _(sp):
                core.load_ahead(sp, lo, mod_done, range(1, 13))

            @block.gpsimd
            def _(pool):
                pool.dma_start(pick[:], a["pick"].rearrange("p (s n) -> p s n", s=2)).then_inc(core.tables_in, 16)
                for i, name in enumerate(("b_ga0", "b_ga1", "g_post0", "g_post1")):
                    pool.dma_start(brow[:, i, :], row_bcast(a, name)).then_inc(core.tables_in, 16)

            @block.scalar
            def _(act):
                for s, name in enumerate(("c", "c_ctx")):
                    nc.scalar.activation(cond[:, :, s], core.col(name, 0, KC), ACT.Silu).then_inc(cond_ready, 1)
                act.dma_start(core.x[:, 0:LT, :], a["x"][0].rearrange("(t p) d -> p t d", p=P)).then_inc(x_in, 16)
                act.dma_start(core.x[:, LT:NT, :], a["ctx"][0].rearrange("(t p) d -> p t d", p=P)).then_inc(x_in, 16)
                act.wait_ge(x_in, 32)

            @block.tensor
            def _(pe):
                pe.wait_ge(cond_ready, 2)
                for i in range(6 * DEPTH):
                    if i >= 2:
                        pe.wait_ge(row_out, i - 1)
                    w = core.weight(pe, lo + i)
                    for k in range(KC):
                        mm = nc.tensor.matmul(ps[0:2, i % 2, :], cond[:, k, :], w[:, k, :], start=(k == 0), stop=(k == KC - 1))
                    mm.then_inc(mod_done, 1)
                pe.wait_ge(row_out, 12)
                for l in range(DEPTH):
                    for k in range(2 * KC):
                        o = (l * 2 * KC + k) * 2
                        mm = nc.tensor.transpose(ps[:, 2, o:o + 2], rows[:, l, k * P:(k + 1) * P], core.ident[0:2, 0:2])
                mm.then_inc(turned, 1)
                pe.wait_ge(core.tables_in, rows_in)
                for n in range(6):
                    l, s = gates[n // 2]
                    b = 3 + n if n < 5 else 0
                    nc.tensor.matmul(ps[:, b, :], pick[:, s, :], rows[:, l, 2 * D + n % 2 * BANK:2 * D + (n % 2 + 1) * BANK],
                                     start=True, stop=True).then_inc(spread, 1)

            @block.vector
            def _(dve):
                link = core.dve_chain
                for i in range(6 * DEPTH):
                    dve.wait_ge(mod_done, i + 1)
                    nc.vector.tensor_copy(rows[:, i // 6, i % 6 * BANK:(i % 6 + 1) * BANK], ps[0:2, i % 2, :]).then_inc(row_out, 1)
                dve.wait_ge(turned, 1)
                for l in range(DEPTH):
                    m = ps[:, 2, l * 32:(l + 1) * 32].rearrange("p (h k s) -> p h k s", h=2, s=2)
                    for s in range(2):
                        nc.vector.tensor_tensor(core.mod[:, l, 0, :, s], m[:, 0, :, s], core.col(f"b_sh{l}", 0, KC), ALU.add)
                        link(dve, nc.vector.tensor_tensor(core.mod[:, l, 1, :, s], m[:, 1, :, s], core.col(f"b_sc{l}", 0, KC), ALU.add))
                        last = nc.vector.scalar_tensor_tensor(
                            out=core.mod[:, l, 1, :, s], in0=core.mod[:, l, 1, :, s], scalar=1.0,
                            in1=core.col(f"g_pre{l}", 0, KC), op0=ALU.add, op1=ALU.mult)
                link(dve, last)
                for n in range(6):
                    l, j = gates[n // 2][0], n % 2
                    dve.wait_ge(spread, n + 1)
                    o = core.ga[:, n // 2, j * BANK:(j + 1) * BANK]
                    link(dve, nc.vector.tensor_tensor(o, ps[:, 3 + n if n < 5 else 0, :], brow[:, l, j * BANK:(j + 1) * BANK], ALU.add))
                    last = nc.vector.tensor_tensor(o, o, brow[:, 2 + l, j * BANK:(j + 1) * BANK], ALU.mult)
                link(dve, last)


def normed(core, tag, tiles, scale, shift=None, into=None, weights=None, scratch=None):
    nc, ps, x, hT = core.nc, core.ps, core.x, core.hT
    with ExitStack() as c:
        T = len(tiles)
        if scratch is not None:
            xn, sq = (scratch[:, lo:lo + n * SEQ].rearrange("p (a b) -> p a b", a=a) for lo, n, a in ((0, 4 * T, T), (T * D, 4, 4)))
        else:
            xn, sq = core.ga[:, 0:T, :], hT[:, 0:4, SEQ:]
        st = c.enter_context(nc.sbuf_tensor(tag + "st", [P, 3, NT], F32))
        squares, meaned, rooted, scaled, turned, out_act, out_dve = (
            core.sem(tag + s) for s in ("squares", "meaned", "rooted", "scaled", "turned", "out_act", "out_dve"))
        T = len(tiles)
        lead_out = core.sem(tag + "lead_out")

        def split_lead(act, q):
            act.wait_ge(out_act, 2 * q + 2)
            if T == NT:
                act.wait_ge(out_dve, 2 * q + 2)
            at = np.s_[:, 2 * q:2 * q + 2, 0:T * P]
            nc.scalar.activation(into.lead[at], hT[at], ACT.Copy).then_inc(lead_out, 1)

        def split_rest(dve, q):
            dve.wait_ge(lead_out, q + 1)
            at = np.s_[:, 2 * q:2 * q + 2, 0:T * P]
            core.dve_chain(dve, into.take_rest(dve, at, hT[at]))

        with core.phase() as block:
            @block.scalar
            def _(act):
                for i, t in enumerate(tiles):
                    core.act_chain(act, nc.scalar.activation(sq, x[:, t, :].rearrange("p (a b) -> p a b", a=4), ACT.Square, accum_out=st[:, 0, i:i + 1]))
                nc.scalar.activation(sq[:, 0, 0:1], x[:, 0, 0:1], ACT.Copy).then_inc(squares, 1)
                act.wait_ge(meaned, 1)
                nc.scalar.activation(st[:, 1, 0:T], st[:, 1, 0:T], ACT.Sqrt).then_inc(rooted, 1)
                for k in range(KC):
                    act.wait_ge(turned, k + 1)
                    nc.scalar.activation(hT[:, k, 0:SEQ], ps[:, k % 4, 0:SEQ], ACT.Identity, scale=scale(k, 0),
                                         bias=shift(k, 0) if shift else 0.0).then_inc(out_act, 1)
                    if into and k % 2 and k > 1:
                        split_lead(act, k // 2 - 1)
                if into:
                    split_lead(act, KC // 2 - 1)

            @block.vector
            def _(dve):
                link = core.dve_chain
                if weights:
                    weights.prime(dve)
                dve.wait_ge(squares, 1)
                nc.vector.tensor_scalar(st[:, 1, 0:T], st[:, 0, 0:T], 1.0 / D, EPS, ALU.mult, ALU.add).then_inc(meaned, 1)
                dve.wait_ge(rooted, 1)
                link(dve, nc.vector.reciprocal(st[:, 2, 0:T], st[:, 1, 0:T]))
                for i, t in enumerate(tiles):
                    nc.vector.tensor_scalar(xn[:, i, :], x[:, t, :], st[:, 2, i:i + 1], None, ALU.mult).then_inc(scaled, 1)
                if T == NT:
                    for k in range(KC):
                        dve.wait_ge(turned, k + 1)
                        dve.wait_ge(out_act, k + 1)
                        nc.vector.tensor_scalar(hT[:, k, SEQ:2 * SEQ], ps[:, k % 4, SEQ:2 * SEQ], scale(k, 1),
                                                shift(k, 1), ALU.mult, ALU.add).then_inc(out_dve, 1)
                        if into and k % 2 and k > 1:
                            split_rest(dve, k // 2 - 1)
                if into:
                    for q in range(KC // 2 - 1 if T == NT else 0, KC // 2):
                        split_rest(dve, q)

            @block.tensor
            def _(pe):
                pe.wait_ge(scaled, T)
                for k in range(KC):
                    if k >= 4:
                        pe.wait_ge(out_dve if T == NT else out_act, k - 3)
                    for i in range(T):
                        mm = nc.tensor.transpose(ps[:, k % 4, i * P:(i + 1) * P], xn[:, i, k * P:(k + 1) * P], core.ident[:])
                    mm.then_inc(turned, 1)


def project_split(core, tag, weights, u0, h, groups, route, act_out, dve_out, banks=range(8), before=None, after=None,
                  on_gpsimd=0, act_between=None):
    nc, ps = core.nc, core.ps
    B = len(banks)
    product, act_read, dve_read = core.sem(tag + "product"), core.sem(tag + "act_read"), core.sem(tag + "dve_read")
    half_used = core.sem(tag + "half_used")
    W = len(groups)
    flat = [(w, g) for w, gs in enumerate(groups) for g in gs]
    start_at = [sum(len(gs) for gs in groups[:w]) for w in range(W + 1)]
    ways = [route(n) for n in range(len(flat))]
    acts = [sum("a" in w for w in ways[:n + 1]) for n in range(len(flat))]
    dves = [sum("d" in w for w in ways[:n + 1]) for n in range(len(flat))]

    def act_outs(act, w):
        for n in range(start_at[w], start_at[w + 1]):
            if "a" in ways[n]:
                act.wait_ge(product, n + 1)
                g = flat[n][1]
                act_out(act, n, w, g, ps[:, banks[n % B], 0:g[3] - g[2]], lambda m: act.wait_ge(dve_read, dves[m])).then_inc(act_read, 1)

    def dve_outs(dve, w):
        for n in range(start_at[w], start_at[w + 1]):
            if "d" in ways[n]:
                dve.wait_ge(product, n + 1)
                if "a" in ways[n]:
                    dve.wait_ge(act_read, acts[n])
                g = flat[n][1]
                dve_out(dve, n, w, g, ps[:, banks[n % B], 0:g[3] - g[2]]).then_inc(dve_read, 1)

    with core.phase() as block:
        if before:
            before(block)

        @block.sync
        def _(sp):
            weights.load_ahead(sp, u0, 2 * W)

        @block.tensor
        def _(pe):
            for u in range(2 * W):
                w = weights.parts(pe, u0 + u)
                for n in range(start_at[u // 2], start_at[u // 2 + 1]):
                    if n >= B and u % 2 == 0:
                        pe.wait_ge(dve_read if "d" in ways[n - B] else act_read, (dves if "d" in ways[n - B] else acts)[n - B])
                    kind, i, n0, n1 = flat[n][1]
                    for k in range(4):
                        kk = 4 * (u % 2) + k
                        if kind == "tokens":
                            lhs, rhs = h.parts(np.s_[:, kk, i * P:(i + 1) * P]), [z[:, k, n0:n1] for z in w]
                        else:
                            lhs, rhs = [z[:, k, i * P:(i + 1) * P] for z in w], h.parts(np.s_[:, kk, n0:n1])
                        mm = split_matmul(nc, ps[:, banks[n % B], 0:n1 - n0], lhs, rhs, kk == 0, kk == KC - 1)
                    if u % 2:
                        mm.then_inc(product, 1)
                if u % 2 == 0:
                    mm.then_inc(half_used, 1)

        @block.scalar
        def _(act):
            weights.take_lead(act, u0 + weights.B - 1)
            for u in range(2 * W):
                if u < 2 * W - 1:
                    if u % 2:
                        act.wait_ge(product, start_at[u // 2 + 1])
                    else:
                        act.wait_ge(half_used, u // 2 + 1)
                    weights.take_lead(act, u0 + weights.B + u)
                if u % 2:
                    act_outs(act, u // 2)
                if act_between and u == act_between[0]:
                    act_between[1](act)

        if on_gpsimd:
            @block.gpsimd
            def _(pool):
                for u in range(-1, min(on_gpsimd, 2 * W) - 1):
                    weights.take_rest(nc.gpsimd, u0 + weights.B + u)

        @block.vector
        def _(dve):
            for u in range(-1, 2 * W):
                if on_gpsimd - 1 <= u < 2 * W - 1:
                    if on_gpsimd and u == on_gpsimd - 1:
                        dve.wait_ge(core.split_ready, weights.base + u0 + weights.B + u)
                    weights.take_rest(dve, u0 + weights.B + u)
                if u >= 0 and u % 2:
                    dve_outs(dve, u // 2)

        if after:
            after(block)



def turn(core, tag, blocks, outs_per_bank=4):
    nc, ps = core.nc, core.ps
    turned, act_read, dve_read = core.sem(tag + "turned"), core.sem(tag + "act_read"), core.sem(tag + "dve_read")
    with core.phase() as block:
        @block.tensor
        def _(pe):
            for n, (ins, out, scale) in enumerate(blocks):
                if n >= 8:
                    pe.wait_ge(act_read if n % 2 == 0 else dve_read, (n - 8) // 2 + 1)
                at = 0
                for i in ins:
                    w, h = i.shape[0], i.shape[1]
                    mm = nc.tensor.transpose(ps[0:h, n % 8, at:at + w], i, core.ident[0:w, 0:w])
                    at += w
                mm.then_inc(turned, 1)

        @block.scalar
        def _(act):
            for n, (ins, out, scale) in enumerate(blocks):
                if n % 2 == 0:
                    act.wait_ge(turned, n + 1)
                    w = len(ins) * ins[0].shape[0]
                    nc.scalar.activation(out, ps[0:out.shape[0], n % 8, 0:w], ACT.Copy if scale is None else ACT.Identity,
                                         scale=1.0 if scale is None else scale).then_inc(act_read, 1)

        @block.vector
        def _(dve):
            for n, (ins, out, scale) in enumerate(blocks):
                if n % 2 == 1:
                    dve.wait_ge(turned, n + 1)
                    src = ps[0:out.shape[0], n % 8, 0:len(ins) * ins[0].shape[0]]
                    if scale is None:
                        nc.vector.tensor_copy(out, src).then_inc(dve_read, 1)
                    else:
                        nc.vector.tensor_scalar(out, src, scale, None, ALU.mult).then_inc(dve_read, 1)


def turn_split(core, tag, blocks, into, weights=None):
    nc, ps = core.nc, core.ps
    turned, lead_out, rest_out = core.sem(tag + "turned"), core.sem(tag + "lead_out"), core.sem(tag + "rest_out")
    with core.phase() as block:
        @block.tensor
        def _(pe):
            for n, (ins, at) in enumerate(blocks):
                if n >= 8:
                    pe.wait_ge(rest_out, n - 7)
                for q, i in enumerate(ins):
                    mm = nc.tensor.transpose(ps[:, n % 8, q * P:(q + 1) * P], i, core.ident[:])
                mm.then_inc(turned, 1)

        @block.scalar
        def _(act):
            for n, (ins, at) in enumerate(blocks):
                act.wait_ge(turned, n + 1)
                dst = into.lead[at]
                nc.scalar.activation(dst, bank(ps, n, dst), ACT.Copy).then_inc(lead_out, 1)

        @block.vector
        def _(dve):
            if weights:
                weights.prime(dve)
            for n, (ins, at) in enumerate(blocks):
                dve.wait_ge(lead_out, n + 1)
                into.take_rest(dve, at, bank(ps, n, into.rest[at])).then_inc(rest_out, 1)


def bank(ps, n, like):
    k, t = like.shape[1], like.shape[2]
    return ps[:, n % 8, 0:k * t].rearrange("p (k t) -> p k t", k=k)


def down_split(core, tag, weights, u0, source, tiles, n_weights, unsplit=None):
    nc, ps = core.nc, core.ps
    used, source_lead, source_ready = (core.sem(tag + n) for n in ("half_used", "source_lead", "source_ready"))
    N = 2 * n_weights
    at = lambda u: np.s_[:, 2 * u:2 * u + 2, :]
    with core.phase() as block:
        @block.sync
        def _(sp):
            weights.load_ahead(sp, u0, N)

        @block.tensor
        def _(pe):
            for u in range(N):
                if unsplit is not None:
                    pe.wait_ge(source_ready, u + 1)
                w = weights.parts(pe, u0 + u)
                for i in range(tiles):
                    for j in range(2):
                        for k in range(2):
                            mm = split_matmul(nc, ps[:, 2 * i + j, :], source.parts(np.s_[:, 2 * u + k, i * P:(i + 1) * P]),
                                              [z[:, k, j * BANK:(j + 1) * BANK] for z in w],
                                              u == 0 and k == 0, u == N - 1 and k == 1)
                mm.then_inc(used, 1)

        @block.scalar
        def _(act):
            for u in range(-1 if unsplit is None else -2, N - 1):
                if unsplit is not None:
                    for v in (0,) if u == -2 else () if u == -1 else (u + 1,):
                        nc.scalar.activation(source.lead[at(v)], unsplit[at(v)], ACT.Copy).then_inc(source_lead, 1)
                if u >= 0:
                    act.wait_ge(used, u + 1)
                weights.take_lead(act, u0 + weights.B + u)

        @block.vector
        def _(dve):
            for u in range(-1 if unsplit is None else -2, N - 1):
                if unsplit is not None:
                    for v in (0,) if u == -2 else () if u == -1 else (u + 1,):
                        dve.wait_ge(source_lead, v + 1)
                        source.take_rest(dve, at(v), unsplit[at(v)]).then_inc(source_ready, 1)
                weights.take_rest(dve, u0 + weights.B + u)


def gated_residual(core, tag, tiles, gate_of):
    nc, ps, x = core.nc, core.ps, core.x
    with ExitStack() as c:
        sq = c.enter_context(nc.sbuf_tensor(tag + "sq", [P, BANK], F32))
        st = c.enter_context(nc.sbuf_tensor(tag + "st", [P, 4, 2 * NT], F32))
        t = c.enter_context(nc.sbuf_tensor(tag + "t", [P, NT * 2, BANK], F32))
        squares, meaned, rooted = core.sem(tag + "squares"), core.sem(tag + "meaned"), core.sem(tag + "rooted")
        n = 2 * tiles
        with core.phase() as block:
            @block.scalar
            def _(act):
                for b in range(n):
                    core.act_chain(act, nc.scalar.activation(sq[:], ps[:, b, :], ACT.Square, accum_out=st[:, 0, b:b + 1]))
                nc.scalar.activation(sq[:, 0:1], st[:, 0, 0:1], ACT.Copy).then_inc(squares, 1)
                act.wait_ge(meaned, 1)
                nc.scalar.activation(st[:, 2, 0:tiles], st[:, 2, 0:tiles], ACT.Sqrt).then_inc(rooted, 1)

            @block.vector
            def _(dve):
                link = core.dve_chain
                dve.wait_ge(squares, 1)
                pairs = st[:, 0, 0:n].rearrange("p (t j) -> p t j", j=2)
                link(dve, nc.vector.tensor_tensor(st[:, 1, 0:tiles], pairs[:, :, 0], pairs[:, :, 1], ALU.add))
                nc.vector.tensor_scalar(st[:, 2, 0:tiles], st[:, 1, 0:tiles], 1.0 / D, EPS, ALU.mult, ALU.add).then_inc(meaned, 1)
                dve.wait_ge(rooted, 1)
                link(dve, nc.vector.reciprocal(st[:, 3, 0:tiles], st[:, 2, 0:tiles]))
                for i in range(tiles):
                    for j in range(2):
                        last = nc.vector.scalar_tensor_tensor(out=t[:, 2 * i + j, :], in0=ps[:, 2 * i + j, :],
                                                              scalar=st[:, 3, i:i + 1],
                                                              in1=core.ga[:, gate_of[i], j * BANK:(j + 1) * BANK],
                                                              op0=ALU.mult, op1=ALU.mult)
                link(dve, last)
                for i in range(tiles):
                    last = nc.vector.tensor_tensor(x[:, i, :], x[:, i, :],
                                                   t[:, 2 * i:2 * i + 2, :].rearrange("p j n -> p (j n)"), ALU.add)
                link(dve, last)


def side_taps(core, dve, dst, src, w0, w2):
    nc = core.nc
    S = dst.shape[1] // SEQ
    d, u = (z.rearrange("p (s t) -> p s t", s=S) for z in (dst, src))
    core.dve_chain(dve, nc.vector.scalar_tensor_tensor(out=d[:, :, 1:], in0=u[:, :, :SEQ - 1], scalar=w0,
                                                       in1=d[:, :, 1:], op0=ALU.mult, op1=ALU.add))
    return nc.vector.scalar_tensor_tensor(out=d[:, :, :SEQ - 1], in0=u[:, :, 1:], scalar=w2,
                                          in1=d[:, :, :SEQ - 1], op0=ALU.mult, op1=ALU.add)


def softmax_attention(core, tag, jobs, scale, room=None, before=None):
    nc, ps = core.nc, core.ps
    with ExitStack() as c:
        sb = lambda name, shape: c.enter_context(nc.sbuf_tensor(tag + name, shape, F32))
        nkm = max(j["k"].shape[1] for j in jobs)
        masked = sb("masked", [P, 3, nkm]) if jobs[0]["mask"] is not None else None
        if room is None:
            prob, probT = sb("prob", [P, 3, nkm]), sb("probT", [P, 2, nkm])
        else:
            prob, probT = (room[:, lo * nkm:(lo + n) * nkm].rearrange("p (a b) -> p a b", a=n) for lo, n in ((0, 3), (3, 2)))
        N = len(jobs)
        top, ntop, tot, rec = (sb(n, [P, N]) for n in ("top", "ntop", "tot", "rec"))
        scores, turned, values = core.sem(tag + "scores"), core.sem(tag + "turned"), core.sem(tag + "values")
        negmax, exped, prob_ready = core.sem(tag + "negmax"), core.sem(tag + "exped"), core.sem(tag + "prob_ready")
        probT_ready, out_done = core.sem(tag + "probT_ready"), core.sem(tag + "out_done")
        with core.phase() as block:
            if before:
                before(block)

            @block.tensor
            def _(pe):
                for j in range(N + 4):
                    if j < N:
                        if j >= 3:
                            pe.wait_ge(exped, j - 2)
                        k = jobs[j]["k"]
                        nc.tensor.matmul(ps[:, j % 3, 0:k.shape[1]], jobs[j]["q"], k, start=True, stop=True).then_inc(scores, 1)
                    if 2 <= j < N + 2:
                        i = j - 2
                        pe.wait_ge(prob_ready, i + 1)
                        if i >= 2:
                            pe.wait_ge(probT_ready, i - 1)
                        for b in range(jobs[i]["k"].shape[1] // P):
                            mm = nc.tensor.transpose(ps[:, 3 + i % 2, b * P:(b + 1) * P], prob[:, i % 3, b * P:(b + 1) * P], core.ident[:])
                        mm.then_inc(turned, 1)
                    if j >= 4:
                        i = j - 4
                        pe.wait_ge(probT_ready, i + 1)
                        if i >= 2:
                            pe.wait_ge(out_done, i - 1)
                        vs = jobs[i]["v"]
                        for b, v in enumerate(vs):
                            pt = probT[:, i % 2, b * P:(b + 1) * P]
                            dv = v.shape[1]
                            if jobs[i]["feat"]:
                                o, lhs, rhs = ps[0:dv, 5 + i % 2, 0:P], v, pt
                            else:
                                o, lhs, rhs = ps[:, 5 + i % 2, 0:dv], pt, v
                            mm = nc.tensor.matmul(o, lhs, rhs, start=(b == 0), stop=(b == len(vs) - 1))
                        mm.then_inc(values, 1)

            @block.scalar
            def _(act):
                for j in range(N + 2):
                    if j < N:
                        act.wait_ge(negmax, j + 1)
                        if j >= 3:
                            act.wait_ge(turned, j - 2)
                        nk = jobs[j]["k"].shape[1]
                        src = masked[:, j % 3, 0:nk] if jobs[j]["mask"] is not None else ps[:, j % 3, 0:nk]
                        nc.scalar.activation(prob[:, j % 3, 0:nk], src, ACT.Exp, bias=ntop[:, j:j + 1], scale=scale,
                                             accum_out=tot[:, j:j + 1]).then_inc(exped, 1)
                    if j >= 2:
                        i = j - 2
                        act.wait_ge(turned, i + 1)
                        if i >= 2:
                            act.wait_ge(values, i - 1)
                        nk = jobs[i]["k"].shape[1]
                        nc.scalar.activation(probT[:, i % 2, 0:nk], ps[:, 3 + i % 2, 0:nk], ACT.Copy).then_inc(probT_ready, 1)

            @block.vector
            def _(dve):
                link = core.dve_chain
                for j in range(N + 4):
                    if j < N:
                        dve.wait_ge(scores, j + 1)
                        nk = jobs[j]["k"].shape[1]
                        if jobs[j]["mask"] is not None:
                            if j >= 3:
                                dve.wait_ge(exped, j - 2)
                            link(dve, nc.vector.tensor_tensor_reduce(masked[:, j % 3, 0:nk], ps[:, j % 3, 0:nk], jobs[j]["mask"],
                                                                     1.0, NEG, ALU.add, ALU.max, top[:, j:j + 1]))
                        else:
                            link(dve, nc.vector.tensor_reduce(top[:, j:j + 1], ps[:, j % 3, 0:nk], AX.X, ALU.max))
                        nc.vector.tensor_scalar(ntop[:, j:j + 1], top[:, j:j + 1], -scale, None, ALU.mult).then_inc(negmax, 1)
                    if 1 <= j <= N:
                        i = j - 1
                        dve.wait_ge(exped, i + 1)
                        nk = jobs[i]["k"].shape[1]
                        link(dve, nc.vector.reciprocal(rec[:, i:i + 1], tot[:, i:i + 1]))
                        nc.vector.tensor_scalar(prob[:, i % 3, 0:nk], prob[:, i % 3, 0:nk], rec[:, i:i + 1], None, ALU.mult).then_inc(prob_ready, 1)
                    if j >= 4:
                        i = j - 4
                        dve.wait_ge(values, i + 1)
                        dv = jobs[i]["v"][0].shape[1]
                        if jobs[i]["feat"]:
                            nc.vector.tensor_tensor(jobs[i]["out"], ps[0:dv, 5 + i % 2, 0:P], jobs[i]["gate"], ALU.mult).then_inc(out_done, 1)
                        else:
                            nc.vector.tensor_copy(jobs[i]["out"], ps[:, 5 + i % 2, 0:dv]).then_inc(out_done, 1)


def rope(core, dve, x, tab, tmp, heads, width, halves=1):
    nc, link = core.nc, core.dve_chain
    w, h = halves * width, width // 2
    cos = tab[:, 0:w].unsqueeze(1).broadcast_to([P, heads, w])
    t1, t2 = tmp[:, 0, 0:heads * w].rearrange("p (a b) -> p a b", a=heads), tmp[:, 1, 0:heads * w].rearrange("p (a b) -> p a b", a=heads)
    nc.vector.tensor_tensor(t1, x, cos, ALU.mult)
    for a in range(halves):
        for first, second in ((0, h), (h, 0)):
            o = a * width
            s = tab[:, w + o + first:w + o + first + h].unsqueeze(1).broadcast_to([P, heads, h])
            last = nc.vector.tensor_tensor(t2[:, :, o + first:o + first + h], x[:, :, o + second:o + second + h], s, ALU.mult)
    link(dve, last)
    link(dve, nc.vector.tensor_tensor(x, t1, t2, ALU.add))


def even_layer(core):
    nc, a, ps = core.nc, core.a, core.ps
    mod, first = core.mod, core.first
    with ExitStack() as layer:
        mixT = layer.enter_context(nc.sbuf_tensor("mixT", [P, 16, 2 * SEQ], F32))
        with ExitStack() as c:
            room = c.enter_context(nc.sbuf_tensor("room", [P, 16, 2 * SEQ], F32))
            c_in = ExitStack()
            h = Split(nc, c_in, "eh", [P, KC, 2 * SEQ])
            weights = SplitWeights(core, c_in, "ei", first["e_qkv"], 13)
            normed(core, "en_", range(NT), lambda k, s: mod[:, 0, 1, k, s:s + 1], lambda k, s: mod[:, 0, 0, k, s:s + 1],
                   into=h, weights=weights, scratch=room[:].rearrange("p k t -> p (k t)"))
            even_attention(core, mixT, room, h, weights)
            hyena(core, mixT, room, h, weights, c_in)
        mix = Split(nc, layer, "mix", [P, 16, 2 * SEQ])
        weights = SplitWeights(core, layer, "eo", first["e_out"], 4)
        down_split(core, "eo_", weights, 0, mix, NT, 4, unsplit=mixT)
    gated_residual(core, "er_", NT, [0, 0, 1, 1])


def even_attention(core, mixT, room, h, weights):
    nc, a, ps = core.nc, core.a, core.ps
    first = core.first
    with ExitStack() as c:
        sb = lambda name, shape: c.enter_context(nc.sbuf_tensor(name, shape, F32))
        NH = HEADS + KVH
        flat, hflat = room[:].rearrange("p k t -> p (k t)"), core.hT[:].rearrange("p k t -> p (k t)")
        v = hflat[:, 0:NT * KVH * DH].rearrange("p (t n) -> p t n", t=NT)
        kT = core.hT[:, 2:2 + KVH, :]
        qT = mixT[:, 0:HEADS, :]
        turned = lambda h: qT[:, h, :] if h < HEADS else kT[:, h - HEADS, :]
        with ExitStack() as c2:
            W = NH * DH
            qk = flat[:, 0:NT * W].rearrange("p (t n) -> p t n", t=NT)

            def take(copy):
                def out(eng, n, wi, g, src, dve_out=None):
                    t = g[1]
                    if wi < 2:
                        return copy(qk[:, t, wi * 512:(wi + 1) * 512], src)
                    return copy(qk[:, t, 1024:1280] if g[2] == 0 else v[:, t, :], src)
                return out
            groups = [[("tokens", t, 0, 512) for t in range(NT)]] * 2 + \
                     [[("tokens", t, h * 256, h * 256 + 256) for t in range(NT) for h in range(2)]]
            project_split(core, "eqkv_", weights, 0, h, groups, lambda n: "ad"[n % 2],
                    take(lambda o, i: nc.scalar.activation(o, i, ACT.Copy)), take(nc.vector.tensor_copy))
            tmp = flat[:, NT * W:(NT + 2) * W].rearrange("p (t n) -> p t n", t=2)
            tab = flat[:, (NT + 2) * W:(NT + 2) * W + LT * 256].rearrange("p (t n) -> p t n", t=LT)
            gains = core.small[:].rearrange("p (i d) -> p i d", i=2)
            st = c2.enter_context(nc.sbuf_tensor("ea_st", [P, 3, NT * NH], F32))
            tabs_in, meaned, rooted = core.expect_tables(3), core.sem("ea_meaned"), core.sem("ea_rooted")

            def root(act):
                act.wait_ge(meaned, 1)
                nc.scalar.activation(st[:, 1, :], st[:, 1, :], ACT.Sqrt).then_inc(rooted, 1)

            def norm_and_rotate(block):
                @block.gpsimd
                def _(pool):
                    pool.dma_start(tab, a["rope_e"].rearrange("(t p) n -> p t n", p=P)).then_inc(core.tables_in, 16)
                    pool.dma_start(gains[:, 0, :], row_bcast(a, "q_norm")).then_inc(core.tables_in, 16)
                    pool.dma_start(gains[:, 1, :], row_bcast(a, "k_norm")).then_inc(core.tables_in, 16)

                @block.vector
                def _(dve):
                    link = core.dve_chain
                    for t in range(NT):
                        sq = tmp[:, t % 2, :]
                        link(dve, nc.vector.tensor_tensor(sq, qk[:, t, :], qk[:, t, :], ALU.mult))
                        link(dve, nc.vector.tensor_reduce(st[:, 0, t * NH:(t + 1) * NH], sq.rearrange("p (h d) -> p h d", h=NH),
                                                          AX.X, ALU.add))
                    nc.vector.tensor_scalar(st[:, 1, :], st[:, 0, :], 1.0 / DH, EPS, ALU.mult, ALU.add).then_inc(meaned, 1)
                    dve.wait_ge(rooted, 1)
                    link(dve, nc.vector.reciprocal(st[:, 2, :], st[:, 1, :]))
                    dve.wait_ge(core.tables_in, tabs_in)
                    for t in range(NT):
                        x = qk[:, t, :].rearrange("p (h d) -> p h d", h=NH)
                        r = st[:, 2, t * NH:(t + 1) * NH].unsqueeze(2).broadcast_to([P, NH, DH])
                        link(dve, nc.vector.tensor_tensor(x, x, r, ALU.mult))
                        nc.vector.tensor_tensor(x[:, 0:HEADS], x[:, 0:HEADS], gains[:, 0:1, :].broadcast_to([P, HEADS, DH]), ALU.mult)
                        link(dve, nc.vector.tensor_tensor(x[:, HEADS:], x[:, HEADS:], gains[:, 1:2, :].broadcast_to([P, KVH, DH]), ALU.mult))
                        if t < LT:
                            rope(core, dve, x, tab[:, t, :], tmp, NH, 64, 2)

            project_split(core, "ega_", weights, 6, h, [[("features", m, 0, 512) for m in range(4)]] * 2, lambda n: "a",
                    lambda act, n, wi, g, src, w: nc.scalar.activation(mixT[:, 8 + n, :], src, ACT.Silu), None,
                    before=norm_and_rotate, on_gpsimd=4, act_between=(0, root))
            turn(core, "ea_t_", [([qk[:, t, n * DH:(n + 1) * DH] for t in range(NT)], turned(n), None) for n in range(NH)])
        jobs = []
        for n in range(HEADS):
            g = n // (HEADS // KVH)
            for t in range(NT):
                k0 = 0 if t < LT else SEQ
                jobs.append(dict(q=qT[:, n, t * P:(t + 1) * P], k=kT[:, g, k0:2 * SEQ], mask=None, feat=True,
                                 v=[v[:, b, g * DH:(g + 1) * DH] for b in range(k0 // P, NT)],
                                 out=mixT[:, 8 + n, t * P:(t + 1) * P], gate=mixT[:, 8 + n, t * P:(t + 1) * P]))
        softmax_attention(core, "ea_", jobs, DH ** -0.5, flat)


def hyena(core, mixT, room, h, weights, c_in):
    nc, a, ps = core.nc, core.a, core.ps
    first, col = core.first, core.col
    NTT = 4
    with ExitStack() as c:
        sb = lambda name, shape, c=c: c.enter_context(nc.sbuf_tensor(name, shape, F32))
        gT, x0T = room[:, 0:KC, :], room[:, KC:2 * KC, :]
        with c_in:
            tmp = core.hT[:, 0:2, :]
            feats = [("features", m, 0, 512) for m in range(4)]

            def conv(tag, name, chan0, dst, after=None, own_tmp=False):
                def act_out(act, n, wi, g, src, dve_done):
                    if own_tmp and n >= 2:
                        dve_done(n - 2)
                    ch = chan0 + n
                    return nc.scalar.activation(dst(n), src, ACT.Identity, scale=col("e_cw1", ch), bias=col("e_cb", ch))

                def dve_out(dve, n, wi, g, src):
                    ch = chan0 + n
                    last = side_taps(core, dve, dst(n), src, col("e_cw0", ch), col("e_cw2", ch))
                    if after:
                        core.dve_chain(dve, last)
                        last = after(n)
                    return last
                project_split(core, tag, weights, 2 * (first[name] - first["e_qkv"]), h, [feats] * 2, lambda n: "ad", act_out, dve_out)

            conv("hx1_", "e_x1", 8, lambda n: gT[:, n, :])
            conv("hv_", "e_v", 16, lambda n: tmp[:, n % 2, :],
                 lambda n: nc.vector.tensor_tensor(gT[:, n, :], gT[:, n, :], tmp[:, n % 2, :], ALU.mult), own_tmp=True)
            conv("hx0_", "e_x0", 0, lambda n: x0T[:, n, :])

            def silu_tmp(act, n, wi, g, src, dve_done):
                if n >= 2:
                    dve_done(n - 2)
                return nc.scalar.activation(tmp[:, n % 2, :], src, ACT.Silu)
            project_split(core, "hgh_", weights, 22, h, [feats] * 2, lambda n: "ad", silu_tmp,
                    lambda dve, n, wi, g, src: nc.vector.tensor_tensor(x0T[:, n, :], x0T[:, n, :], tmp[:, n % 2, :], ALU.mult))

        F = sb("hy_F", [P, 5, HY])
        snorm = sb("hy_norm", [P, KC])
        dft = sb("hy_dft", [P, NTT, 2 * SEQ])
        tabs_in, dense_in, filter_in = core.expect_tables(2), core.dense_in, core.filter_in
        gtok = core.hT[:].rearrange("p k t -> p (k t)").rearrange("p (t d) -> p t d", t=NT)
        with ExitStack() as c2:
            sb2 = lambda name, shape: c2.enter_context(nc.sbuf_tensor(name, shape, F32))
            filt = mixT[:, 0:KC, :].rearrange("p k t -> p (k t)").rearrange("p (t d) -> p t d", t=NTT)
            scratch = core.hT[:].rearrange("p k t -> p (k t)")
            zt = sb2("hy_zt", [33, SEQ])
            w1, w2 = sb2("hy_w1", [33, 64]), sb2("hy_w2", [64, 64])
            w3 = scratch[0:64, 0:2 * HY]
            decay = scratch[:, 2 * HY:4 * HY].rearrange("p (t d) -> p t d", t=2)
            ones = sb2("hy_ones", [P, NTT])
            hd = sb2("hy_hd", [64, 4, SEQ])
            dense, sined, arg_ready = core.sem("hy_dense"), core.sem("hy_sined"), core.sem("hy_arg_ready")
            filt_out = core.sem("hy_filt_out")
            TWO_PI_HI = float(np.float32(6.28125))
            TWO_PI_LO = float(2 * math.pi - 6.28125)
            MAGIC = 12582912.0
            with core.phase() as block:
                @block.gpsimd
                def _(pool):
                    for dst, src, sem in ((zt[:], a["z_t"], dense_in), (w1[:], a["e_filt_w1"][0], dense_in),
                                          (w2[:], a["e_filt_w2"][0], dense_in), (w3, a["e_filt_w3"][0], filter_in),
                                          (decay, a["decay"].rearrange("(t p) n -> p t n", p=P), filter_in),
                                          (ones[:], a["tap_ones"], core.tables_in),
                                          (dft[:], a["dft"].rearrange("(t p) n -> p t n", p=P), core.tables_in)):
                        pool.dma_start(dst, src).then_inc(sem, 16)

                @block.tensor
                def _(pe):
                    pe.wait_ge(dense_in, 48)
                    nc.tensor.matmul(ps[0:64, 0, 0:SEQ], w1[:], zt[:], start=True, stop=True).then_inc(dense, 1)
                    pe.wait_ge(sined, 1)
                    nc.tensor.matmul(ps[0:64, 1, 0:SEQ], w2[:], hd[:, 3, :], start=True, stop=True).then_inc(dense, 1)
                    pe.wait_ge(sined, 2)
                    pe.wait_ge(filter_in, 32)
                    for n in range(8):
                        side, t, j = n // 4, n // 2 % 2, n % 2
                        if n >= 6:
                            pe.wait_ge(filt_out, n - 5)
                        nc.tensor.matmul(ps[:, 2 + n % 6, :], hd[:, 3, t * P:(t + 1) * P],
                                         w3[:, side * HY + j * BANK:side * HY + (j + 1) * BANK], start=True, stop=True).then_inc(dense, 1)

                @block.scalar
                def _(act):
                    for i in range(2):
                        act.wait_ge(arg_ready, i + 1)
                        nc.scalar.activation(hd[:, 3, :], hd[:, 2, :], ACT.Sin).then_inc(sined, 1)

                @block.vector
                def _(dve):
                    link = core.dve_chain
                    for i in range(2):
                        dve.wait_ge(dense, i + 1)
                        link(dve, nc.vector.tensor_scalar(hd[:, 0, :], ps[0:64, i, 0:SEQ], core.col(f"f_b{i + 1}")[0:64],
                                                          core.col("f_fr")[0:64], ALU.add, ALU.mult))
                        link(dve, nc.vector.tensor_scalar(hd[:, 1, :], hd[:, 0, :], float(1 / (2 * math.pi)), None, ALU.mult))
                        link(dve, nc.vector.tensor_scalar(hd[:, 1, :], hd[:, 1, :], MAGIC, None, ALU.add))
                        link(dve, nc.vector.tensor_scalar(hd[:, 1, :], hd[:, 1, :], MAGIC, None, ALU.subtract))
                        link(dve, nc.vector.scalar_tensor_tensor(out=hd[:, 0, :], in0=hd[:, 1, :], scalar=-TWO_PI_HI,
                                                                 in1=hd[:, 0, :], op0=ALU.mult, op1=ALU.add))
                        link(dve, nc.vector.scalar_tensor_tensor(out=hd[:, 0, :], in0=hd[:, 1, :], scalar=-TWO_PI_LO,
                                                                 in1=hd[:, 0, :], op0=ALU.mult, op1=ALU.add))
                        nc.vector.tensor_scalar(hd[:, 2, :], hd[:, 0, :], math.pi - 1e-6, -math.pi + 1e-6, ALU.min, ALU.max).then_inc(arg_ready, 1)
                    for n in range(8):
                        side, t, j = n // 4, n // 2 % 2, n % 2
                        dve.wait_ge(dense, n + 3)
                        nc.vector.tensor_tensor(filt[:, side * 2 + t, j * BANK:(j + 1) * BANK], ps[:, 2 + n % 6, :],
                                                decay[:, t, j * BANK:(j + 1) * BANK], ALU.mult).then_inc(filt_out, 1)
            absd, summed, F_done, F_out_dve = (core.sem(n) for n in ("hy_absd", "hy_summed", "hy_F_done", "hy_F_out_dve"))
            absf = c2.enter_context(nc.sbuf_tensor("hy_abs", [P, NTT, BANK], F32))
            with core.phase() as block:
                @block.scalar
                def _(act):
                    for j in range(2):
                        if j:
                            act.wait_ge(summed, 1)
                        for t in range(NTT):
                            core.act_chain(act, nc.scalar.activation(absf[:, t, :], filt[:, t, j * BANK:(j + 1) * BANK], ACT.Abs))
                        nc.scalar.activation(core.small[:, 1:2], core.ident[:, 0:1], ACT.Copy).then_inc(absd, 1)

                @block.tensor
                def _(pe):
                    pe.wait_ge(core.tables_in, tabs_in)
                    for n in range(8):
                        j, f = n // 4, n % 4
                        if n >= 7:
                            pe.wait_ge(F_out_dve, 1)
                        for t in range(NTT):
                            mm = nc.tensor.matmul(ps[:, 1 + n % 7, :], dft[:, t, f * P:(f + 1) * P],
                                                  filt[:, t, j * BANK:(j + 1) * BANK], start=(t == 0), stop=(t == NTT - 1))
                        mm.then_inc(F_done, 1)
                        if f == 3:
                            pe.wait_ge(absd, j + 1)
                            for ch in range(4):
                                for t in range(NTT):
                                    mm = nc.tensor.matmul(ps[:, 0, 4 * j + ch:4 * j + ch + 1], absf[:, t, ch * P:(ch + 1) * P],
                                                          ones[:, t:t + 1], start=(t == 0), stop=(t == NTT - 1))
                            mm.then_inc(summed, 1)

                @block.vector
                def _(dve):
                    link = core.dve_chain
                    for n in range(8):
                        j, f = n // 4, n % 4
                        dve.wait_ge(F_done, n + 1)
                        nc.vector.tensor_copy(F[:, f, j * BANK:(j + 1) * BANK], ps[:, 1 + n % 7, :]).then_inc(F_out_dve, 1)
                    dve.wait_ge(F_out_dve, 8)
                    link(dve, nc.vector.tensor_copy(F[:, 4, :], F[:, 0, :]))
                    link(dve, nc.vector.tensor_copy(F[0:1, 4, :], F[0:1, 2, :]))
                    link(dve, nc.vector.memset(F[0:1, 2, :], 0.0))
                    dve.wait_ge(summed, 2)
                    link(dve, nc.vector.reciprocal(snorm[:], ps[:, 0, 0:KC]))
        turn(core, "hy_t_", [([gT[:, 4 * q + i, t * P:(t + 1) * P] for i in range(4)],
                              gtok[:, t, q * BANK:(q + 1) * BANK], None) for t in range(NT) for q in range(2)])
        Y = sb("hy_Y", [P, 2, 4, BANK])
        T2 = sb("hy_T2", [P, 2, BANK])
        idft = dft[:, 2:4, :].rearrange("p a b -> p (a b)").rearrange("p (t n) -> p t n", t=NTT)
        y1 = core.small
        inv_in = core.expect_tables(1)
        spect, Y_ready, back, mixed = (core.sem(n) for n in ("hy_spect", "hy_Y_ready", "hy_back", "hy_mixed"))
        rounds = [(j, s) for j in range(2) for s in range(2)]
        with core.phase() as block:
            @block.gpsimd
            def _(pool):
                pool.dma_start(idft, a["idft"].rearrange("(t p) n -> p t n", p=P)).then_inc(core.tables_in, 16)

            @block.tensor
            def _(pe):
                pe.wait_ge(core.tables_in, inv_in)
                for r in range(len(rounds) + 1):
                    if r < len(rounds):
                        j, s = rounds[r]
                        if r:
                            pe.wait_ge(Y_ready, r)
                        for f in range(NTT):
                            for t in range(LT):
                                mm = nc.tensor.matmul(ps[:, f, :], dft[:, t, f * P:(f + 1) * P],
                                                      gtok[:, s * LT + t, j * BANK:(j + 1) * BANK], start=(t == 0), stop=(t == LT - 1))
                        mm.then_inc(spect, 1)
                    if r:
                        pe.wait_ge(Y_ready, r)
                        for ch in range(4):
                            if r >= 2:
                                pe.wait_ge(mixed, 4 * (r - 2) + ch + 1)
                            for f in range(NTT):
                                mm = nc.tensor.matmul(ps[:, 4 + ch, 0:SEQ], Y[:, (r - 1) % 2, f, ch * P:(ch + 1) * P], idft[:, f, :],
                                                      start=(f == 0), stop=(f == NTT - 1))
                            mm.then_inc(back, 1)

            @block.vector
            def _(dve):
                link = core.dve_chain
                for r in range(len(rounds) + 1):
                    if r < len(rounds):
                        j, s = rounds[r]
                        dve.wait_ge(spect, r + 1)
                        if r >= 2:
                            dve.wait_ge(back, 4 * (r - 1))
                        cs, Yr = slice(j * BANK, (j + 1) * BANK), Y[:, r % 2]
                        for f in range(2):
                            nc.vector.tensor_tensor(Yr[:, f, :], ps[:, f, :], F[:, f, cs], ALU.mult)
                            last = nc.vector.tensor_tensor(T2[:, f, :], ps[:, 2 + f, :], F[:, 2 + f, cs], ALU.mult)
                        link(dve, last)
                        link(dve, nc.vector.tensor_tensor(Yr[:, 0:2, :], Yr[:, 0:2, :], T2[:, 0:2, :], ALU.subtract))
                        for f in range(2):
                            nc.vector.tensor_tensor(Yr[:, 2 + f, :], ps[:, f, :], F[:, 2 + f, cs], ALU.mult)
                            last = nc.vector.tensor_tensor(T2[:, f, :], ps[:, 2 + f, :], F[:, 4 if f == 0 else 1, cs], ALU.mult)
                        link(dve, last)
                        nc.vector.tensor_tensor(Yr[:, 2:4, :], Yr[:, 2:4, :], T2[:, 0:2, :], ALU.add).then_inc(Y_ready, 1)
                    if r:
                        j, s = rounds[r - 1]
                        for ch in range(4):
                            k, ss = 4 * j + ch, slice(s * SEQ, (s + 1) * SEQ)
                            dve.wait_ge(back, 4 * (r - 1) + ch + 1)
                            if r > 1 or ch:
                                dve.wait_ge(mixed, 4 * (r - 1) + ch)
                            link(dve, nc.vector.tensor_scalar(y1[:], ps[:, 4 + ch, 0:SEQ], snorm[:, k:k + 1], None, ALU.mult))
                            link(dve, nc.vector.scalar_tensor_tensor(out=y1[:], in0=gT[:, k, ss], scalar=col("hy_bias", k),
                                                                     in1=y1[:], op0=ALU.mult, op1=ALU.add))
                            nc.vector.tensor_tensor(mixT[:, k, ss], y1[:], x0T[:, k, ss], ALU.mult).then_inc(mixed, 1)


def program(nc, a, out):
    with ExitStack() as ctx:
        core = Core(nc, a, ctx)
        setup(core)
        adaln(core)
        even_layer(core)
        odd_layer(core)
        for l in range(DEPTH):
            block2(core, l)
        final(core, out)


def mlstm_gates(core, c, fetched, wg, aT, cumT, g, taps):
    nc, a, ps = core.nc, core.a, core.ps
    R = 40
    sb = lambda name, shape: c.enter_context(nc.sbuf_tensor("mg_" + name, shape, F32))
    tot = sb("tot", [R, 2])
    products, logged, abs_ready, cum_ready, turned = (
        core.sem("mg_" + n) for n in ("products", "logged", "abs_ready", "cum_ready", "turned"))
    I, FG, LF, T, CUM, ONE = range(6)
    lat, ctx = slice(0, SEQ), slice(SEQ, 2 * SEQ)
    def before(block):
        @block.tensor
        def _(pe):
            pe.wait_ge(core.tables_in, fetched)
            for i in range(2):
                for k in range(KC):
                    mm = nc.tensor.matmul(ps[0:R, i, :], wg[:, k, i, :], core.hT[:, k, :], start=(k == 0), stop=(k == KC - 1))
                mm.then_inc(products, 1)

        @block.vector
        def _(dve):
            link = core.dve_chain
            link(dve, nc.vector.memset(g[:, ONE, :], 1.0))
            dve.wait_ge(products, 2)
            nc.vector.tensor_scalar(g[:, I, :], ps[0:R, 0, :], core.col("gb_i")[0:R], None, ALU.add)
            link(dve, nc.vector.tensor_scalar(g[:, FG, :], ps[0:R, 1, :], core.col("gb_f")[0:R], None, ALU.add))
            nc.vector.tensor_scalar(g[:, LF, :], g[:, FG, :], 0.0, None, ALU.min)
            nc.vector.scalar_tensor_tensor(out=g[:, T, :], in0=g[:, FG, :], scalar=-1.0, in1=g[:, FG, :],
                                           op0=ALU.mult, op1=ALU.max).then_inc(abs_ready, 1)
            dve.wait_ge(logged, 1)
            link(dve, nc.vector.tensor_tensor(g[:, LF, :], g[:, LF, :], g[:, T, :], ALU.subtract))
            nc.vector.tensor_tensor_scan(g[:, CUM, lat], g[:, ONE, lat], g[:, LF, lat], 0.0, ALU.mult, ALU.add)
            link(dve, nc.vector.tensor_tensor_scan(g[:, CUM, ctx], g[:, ONE, ctx], g[:, LF, ctx], 0.0, ALU.mult, ALU.add))
            end_lat, end_ctx = g[:, CUM, SEQ - 1:SEQ], g[:, CUM, 2 * SEQ - 1:2 * SEQ]
            nc.vector.tensor_copy(tot[:, 0:1], end_ctx)
            link(dve, nc.vector.tensor_tensor(tot[:, 1:2], end_ctx, end_lat, ALU.add))
            link(dve, nc.vector.tensor_scalar(g[0:8, CUM, lat], g[0:8, CUM, lat], tot[0:8, 0:1], None, ALU.add))
            B = slice(32, R)
            for n, part in ((1, lat), (0, ctx)):
                link(dve, nc.vector.tensor_scalar(g[B, CUM, part], g[B, CUM, part], -1.0, tot[B, n:n + 1], ALU.mult, ALU.add))
            link(dve, nc.vector.tensor_tensor(g[B, CUM, :], g[B, CUM, :], g[B, LF, :], ALU.add))
            nc.vector.tensor_tensor(aT, g[:, I, :], g[:, CUM, :], ALU.subtract).then_inc(cum_ready, 1)

    def after(block):
        @block.tensor
        def _(pe):
            pe.wait_ge(cum_ready, 1)
            for t in range(LT):
                mm = nc.tensor.transpose(ps[:, 2, t * R:(t + 1) * R], g[:, CUM, t * P:(t + 1) * P], core.ident[0:R, 0:R])
            mm.then_inc(turned, 1)

        @block.vector
        def _(dve):
            link = core.dve_chain
            dve.wait_ge(turned, 1)
            link(dve, nc.vector.tensor_copy(cumT, ps[:, 2, 0:LT * R].rearrange("p (t r) -> p t r", t=LT)))

    def between(act):
        act.wait_ge(abs_ready, 1)
        core.act_chain(act, nc.scalar.activation(g[:, T, :], g[:, T, :], ACT.Exp, scale=-1.0))
        nc.scalar.activation(g[:, T, :], g[:, T, :], ACT.Ln, bias=1.0).then_inc(logged, 1)
        for z in taps:
            for k in range(0, ML_H, 4):
                last = nc.scalar.activation(z[:, k:k + 4, :], z[:, k:k + 4, :], ACT.Silu)
        core.act_chain(act, last)

    return before, between, after


def mlstm(core, qT, kT, v, o_gate, aT, cumT, masks, hs, squares, z_gate):
    nc, ps = core.nc, core.ps
    scale = ML_QK ** -0.5
    with ExitStack() as c:
        sb = lambda name, shape: c.enter_context(nc.sbuf_tensor("ml_" + name, shape, F32))
        Dm = sb("decay", [P, 3, 2, 2 * SEQ])
        WT = sb("WT", [P, 2, 2 * SEQ])
        junk = sb("junk", [P, ML_V])
        gain = sb("gain", [P, ML_H * ML_V])
        gain_in = core.expect_tables(1)
        a_split = Split(nc, c, "ml_a", [40, 2 * SEQ])
        pick = c.enter_context(nc.sbuf_tensor("ml_pick", [40, 40], F32R))
        a_ready = core.sem("ml_a_ready")
        jobs = [(h, t) for h in range(ML_H) for t in range(LT)]
        N = len(jobs)
        mu, nmu, flr, den, rec = (sb(n, [P, 2 * N]) for n in ("mu", "nmu", "flr", "den", "rec"))
        sems = {n: core.sem("ml_" + n) for n in ("scores", "spread", "negmax", "decayed", "floored", "mixed",
                                                 "turned", "WT_ready", "values", "out_done")}
        sc, spread, negmax, decayed, floored, mixed, turned, WT_ready, values, out_done = sems.values()
        with core.phase() as block:
            @block.tensor
            def _(pe):
                pe.wait_ge(a_ready, 2)
                for j in range(N + 3):
                    if j < N:
                        h, t = jobs[j]
                        for d in range(2):
                            if j >= 1:
                                pe.wait_ge(negmax, 2 * (j - 1) + d + 1)
                            for i, a in enumerate(a_split.parts(np.s_[:, :])):
                                mm = nc.tensor.matmul(ps[:, 2 + d, :], pick[:, 32 * d + h:32 * d + h + 1].broadcast_to([40, P]), a,
                                                      start=(i == 0), stop=(i == 1))
                            mm.then_inc(spread, 1)
                    if 2 <= j < N + 2:
                        i = j - 2
                        pe.wait_ge(mixed, i + 1)
                        if i >= 2:
                            pe.wait_ge(WT_ready, i - 1)
                        for b in range(4):
                            mm = nc.tensor.transpose(ps[:, 4 + i % 2, b * P:(b + 1) * P], Dm[:, i % 3, 0, b * P:(b + 1) * P], core.ident[:])
                        mm.then_inc(turned, 1)
                    if j < N:
                        h, t = jobs[j]
                        nc.tensor.matmul(ps[:, j % 2, :], qT[:, h, t * P:(t + 1) * P], kT[:, h, :], start=True, stop=True).then_inc(sc, 1)
                    if j >= 3:
                        i = j - 3
                        h, t = jobs[i]
                        pe.wait_ge(WT_ready, i + 1)
                        if i >= 2:
                            pe.wait_ge(out_done, i - 1)
                        for b in range(4):
                            mm = nc.tensor.matmul(ps[:, 6 + i % 2, 0:ML_V], WT[:, i % 2, b * P:(b + 1) * P],
                                                  v[:, b, h * ML_V:(h + 1) * ML_V], start=(b == 0), stop=(b == 3))
                        mm.then_inc(values, 1)

            @block.gpsimd
            def _(pool):
                pool.dma_start(gain[:], row_bcast(core.a, "head_norm")).then_inc(core.tables_in, 16)
                pool.wait_ge(core.tables_in, gain_in)
                for t in range(LT):
                    last = nc.gpsimd.tensor_tensor(z_gate[:, t, :], z_gate[:, t, :], gain[:], ALU.mult)
                core.pool_chain(pool, last)

            @block.scalar
            def _(act):
                for j in range(N + 4):
                    if j >= 4:
                        h, t = jobs[j - 4]
                        act.wait_ge(out_done, j - 3)
                        core.act_chain(act, nc.scalar.activation(junk[:], hs[:, t, h * ML_V:(h + 1) * ML_V], ACT.Square,
                                                                 accum_out=squares[:, t * ML_H + h:t * ML_H + h + 1]))
                    if j < N:
                        h, t = jobs[j]
                        for d in range(2):
                            u = 2 * j + d
                            act.wait_ge(negmax, u + 1)
                            nc.scalar.activation(Dm[:, j % 3, d, :], Dm[:, j % 3, d, :], ACT.Exp, bias=nmu[:, u:u + 1]).then_inc(decayed, 1)
                            r = 32 * d + h
                            nc.scalar.activation(flr[:, u:u + 1], cumT[:, t, r:r + 1], ACT.Exp, bias=nmu[:, u:u + 1], scale=-1.0).then_inc(floored, 1)
                    if 2 <= j < N + 2:
                        i = j - 2
                        act.wait_ge(turned, i + 1)
                        if i >= 2:
                            act.wait_ge(values, i - 1)
                        nc.scalar.activation(WT[:, i % 2, :], ps[:, 4 + i % 2, :], ACT.Copy).then_inc(WT_ready, 1)

            @block.vector
            def _(dve):
                link = core.dve_chain
                nc.vector.tensor_copy(pick[:], core.ident[0:40, 0:40]).then_inc(a_ready, 1)
                link(dve, a_split.take_lead(dve, np.s_[:, :], aT))
                a_split.take_rest(dve, np.s_[:, :], aT).then_inc(a_ready, 1)
                for j in range(N + 3):
                    if j < N:
                        h, t = jobs[j]
                        if j >= 3:
                            dve.wait_ge(turned, j - 2)
                        for d in range(2):
                            u = 2 * j + d
                            dve.wait_ge(spread, u + 1)
                            m = LT * d + t
                            halves = lambda z: z.rearrange("p (s n) -> p s n", s=2)
                            link(dve, nc.vector.tensor_tensor_reduce(halves(Dm[:, j % 3, d, :]), halves(ps[:, 2 + d, :]), masks[:, m:2 * LT + 1:2 * LT - m, :],
                                                                     1.0, 0.0, ALU.add, ALU.max, mu[:, u:u + 1]))
                            nc.vector.tensor_scalar(nmu[:, u:u + 1], mu[:, u:u + 1], -1.0, None, ALU.mult).then_inc(negmax, 1)
                    if 1 <= j <= N:
                        i = j - 1
                        dve.wait_ge(sc, i + 1)
                        for d in range(2):
                            u = 2 * i + d
                            dve.wait_ge(decayed, u + 1)
                            link(dve, nc.vector.tensor_tensor_reduce(Dm[:, i % 3, d, :], ps[:, i % 2, :], Dm[:, i % 3, d, :],
                                                                     scale, 0.0, ALU.mult, ALU.add, den[:, u:u + 1]))
                            dve.wait_ge(floored, u + 1)
                            nd = den[:, u:u + 1]
                            link(dve, nc.vector.scalar_tensor_tensor(out=rec[:, u:u + 1], in0=nd, scalar=-1.0, in1=nd, op0=ALU.mult, op1=ALU.max))
                            link(dve, nc.vector.tensor_tensor(nd, rec[:, u:u + 1], flr[:, u:u + 1], ALU.max))
                            link(dve, nc.vector.reciprocal(rec[:, u:u + 1], den[:, u:u + 1]))
                        u = 2 * i
                        link(dve, nc.vector.tensor_scalar(Dm[:, i % 3, 0, :], Dm[:, i % 3, 0, :], rec[:, u:u + 1], None, ALU.mult))
                        nc.vector.scalar_tensor_tensor(out=Dm[:, i % 3, 0, :], in0=Dm[:, i % 3, 1, :], scalar=rec[:, u + 1:u + 2],
                                                       in1=Dm[:, i % 3, 0, :], op0=ALU.mult, op1=ALU.add).then_inc(mixed, 1)
                    if j >= 3:
                        i = j - 3
                        h, t = jobs[i]
                        dve.wait_ge(values, i + 1)
                        cs = slice(h * ML_V, (h + 1) * ML_V)
                        nc.vector.tensor_tensor(hs[:, t, cs], ps[:, 6 + i % 2, 0:ML_V], o_gate[:, t, cs], ALU.mult).then_inc(out_done, 1)


def odd_layer(core):
    nc, a, ps = core.nc, core.a, core.ps
    mod, first, col = core.mod, core.first, core.col
    with ExitStack() as c:
        sb = lambda name, shape: c.enter_context(nc.sbuf_tensor(name, shape, F32))
        v = sb("od_v", [P, NT, ML_H * ML_V])
        o_gate = sb("od_o", [P, LT, ML_H * ML_V])
        flat_v = v[:].rearrange("p t d -> p (t d)")
        z_gate = core.hT[:].rearrange("p k t -> p (k t)").rearrange("p (t d) -> p t d", t=LT)
        with ExitStack() as c2:
            kT = c2.enter_context(nc.sbuf_tensor("od_kT", [P, ML_H, 2 * SEQ], F32))
            qT = core.ga[:, 0:2, :].rearrange("p a (b t) -> p (a b) t", t=SEQ)
            c_in = ExitStack()
            h = Split(nc, c_in, "oh", [P, KC, 2 * SEQ])
            weights = SplitWeights(core, c_in, "oi", first["o_q"], 16)
            unit = lambda name: 2 * (first[name] - first["o_q"])
            normed(core, "on_", range(NT), lambda k, s: mod[:, 1, 1, k, s:s + 1], lambda k, s: mod[:, 1, 0, k, s:s + 1],
                   into=h, weights=weights, scratch=flat_v)

            def conv(tag, name, chan0, dst, tokens, before=None):
                def act_out(act, n, wi, g, src, dve_done):
                    ch = chan0 + n
                    return nc.scalar.activation(dst[:, n, :], src, ACT.Identity, scale=col("o_cw1", ch), bias=col("o_cb", ch))

                def dve_out(dve, n, wi, g, src):
                    ch = chan0 + n
                    return side_taps(core, dve, dst[:, n, :], src, col("o_cw0", ch), col("o_cw2", ch))
                project_split(core, tag, weights, unit(name), h, [[("features", m, 0, tokens) for m in range(4)]] * 2, lambda n: "ad", act_out, dve_out,
                              before=before)

            spare = core.x[:, LT:NT, :].rearrange("p t d -> p (t d)")
            masks = spare[:, 0:(2 * LT + 1) * SEQ].rearrange("p (n t) -> p n t", n=2 * LT + 1)
            aT = spare[0:40, 1280:1280 + 2 * SEQ]
            cumT = spare[:, 1792:1792 + LT * 40].rearrange("p (t r) -> p t r", t=LT)
            flat_o = o_gate[:].rearrange("p t d -> p (t d)")
            scratch = flat_o[0:40, 0:12 * SEQ].rearrange("p (n t) -> p n t", n=6)
            wg = flat_o[:, 12 * SEQ:12 * SEQ + KC * 80].rearrange("p (k i r) -> p k i r", k=KC, i=2)

            fetched = core.expect_tables(3)

            def fetch(block):
                @block.gpsimd
                def _(pool):
                    pool.dma_start(wg, a["gate_w"].rearrange("p (k i r) -> p k i r", k=KC, i=2)).then_inc(core.tables_in, 16)
                    for d, name in enumerate(("causal", "anti")):
                        pool.dma_start(masks[:, LT * d:LT * (d + 1), :], a[name].rearrange("(t p) n -> p t n", p=P)).then_inc(core.tables_in, 16)
                    core.pool_chain(pool, nc.gpsimd.memset(masks[:, 2 * LT, :], 0.0))

            conv("oq_", "o_q", 0, qT, SEQ)
            conv("ok_", "o_k", 8, kT, 2 * SEQ, before=fetch)

            def plain(dst):
                return (lambda act, n, wi, g, src, w: nc.scalar.activation(dst[:, g[1], wi * BANK:(wi + 1) * BANK], src, ACT.Copy),
                        lambda dve, n, wi, g, src: nc.vector.tensor_copy(dst[:, g[1], wi * BANK:(wi + 1) * BANK], src))

            def through(dst, func):
                return (lambda act, n, wi, g, src, w: nc.scalar.activation(dst[:, g[1], wi * BANK:(wi + 1) * BANK], src, func), None)
            with ExitStack() as c3:
                before, between, after = mlstm_gates(core, c3, fetched, wg, aT, cumT, scratch, (qT, kT[:]))

                project_split(core, "ov_", weights, unit("o_v"), h, [[("tokens", t, 0, BANK) for t in range(NT)]] * 4, lambda n: "a", *plain(v),
                              banks=range(3, 8), before=before, after=after, on_gpsimd=3, act_between=(1, between))
            project_split(core, "oo_", weights, unit("o_o"), h, [[("tokens", t, 0, BANK) for t in range(LT)]] * 4, lambda n: "a",
                          *through(o_gate, ACT.Sigmoid))
            project_split(core, "oz_", weights, unit("o_z"), h, [[("tokens", t, 0, BANK) for t in range(LT)]] * 4, lambda n: "a",
                          *through(z_gate, ACT.Silu))
            c_in.close()
            hs = o_gate
            squares = core.small[:, 0:LT * ML_H]
            mlstm(core, qT, kT, v, o_gate, aT, cumT, masks, hs, squares, z_gate)
        hsT = Split(nc, c, "hsT", [P, 16, SEQ])
        weights = SplitWeights(core, c, "oo", first["o_out"], 4)
        st = sb("od_st", [P, 2, LT * ML_H])
        meaned, rooted = core.sem("od_meaned"), core.sem("od_rooted")
        with core.phase() as block:
            @block.scalar
            def _(act):
                act.wait_ge(meaned, 1)
                nc.scalar.activation(st[:, 0, :], st[:, 0, :], ACT.Sqrt).then_inc(rooted, 1)

            @block.vector
            def _(dve):
                link = core.dve_chain
                nc.vector.tensor_scalar(st[:, 0, :], squares, 1.0 / ML_V, EPS, ALU.mult, ALU.add).then_inc(meaned, 1)
                weights.prime(dve)
                dve.wait_ge(rooted, 1)
                link(dve, nc.vector.reciprocal(st[:, 1, :], st[:, 0, :]))
                for t in range(LT):
                    for n in range(ML_H):
                        o, r = slice(n * ML_V, (n + 1) * ML_V), t * ML_H + n
                        last = nc.vector.scalar_tensor_tensor(out=hs[:, t, o], in0=hs[:, t, o], scalar=st[:, 1, r:r + 1],
                                                              in1=z_gate[:, t, o], op0=ALU.mult, op1=ALU.mult)
                link(dve, last)
        turn_split(core, "od_t_", [([hs[:, t, k * P:(k + 1) * P] for k in (2 * q, 2 * q + 1) for t in range(LT)],
                                    np.s_[:, 2 * q:2 * q + 2, :]) for q in range(8)], hsT)
        down_split(core, "od_d_", weights, 0, hsT, LT, 4)
    gated_residual(core, "or_", LT, [2, 2])


def retention(core, tag, rT, rv, decay, out):
    nc, ps = core.nc, core.ps
    with ExitStack() as c:
        sc = c.enter_context(nc.sbuf_tensor(tag + "sc", [P, 2, SEQ], F32))
        scT = c.enter_context(nc.sbuf_tensor(tag + "scT", [P, 2, SEQ], F32))
        scores, decayed, turned, back, values, out_done = (core.sem(tag + n) for n in ("scores", "decayed", "turned", "back", "values", "out_done"))
        jobs = [(h, t) for h in range(RET_H) for t in range(LT)]
        N = len(jobs)
        with core.phase() as block:
            @block.tensor
            def _(pe):
                for j in range(N + 2):
                    if j < N:
                        h, t = jobs[j]
                        nk = (t + 1) * P
                        if j >= 2:
                            pe.wait_ge(decayed, j - 1)
                        nc.tensor.matmul(ps[:, j % 2, 0:nk], rT[0:RET_QK, h, t * P:(t + 1) * P], rT[0:RET_QK, RET_H + h, 0:nk],
                                         start=True, stop=True).then_inc(scores, 1)
                    if 1 <= j <= N:
                        i = j - 1
                        pe.wait_ge(decayed, i + 1)
                        if i >= 2:
                            pe.wait_ge(back, i - 1)
                        for b in range(jobs[i][1] + 1):
                            mm = nc.tensor.transpose(ps[:, 2 + i % 2, b * P:(b + 1) * P], sc[:, i % 2, b * P:(b + 1) * P], core.ident[:])
                        mm.then_inc(turned, 1)
                    if j >= 2:
                        i = j - 2
                        h, t = jobs[i]
                        pe.wait_ge(back, i + 1)
                        if i >= 2:
                            pe.wait_ge(out_done, i - 1)
                        for b in range(t + 1):
                            mm = nc.tensor.matmul(ps[:, 4 + i % 2, 0:RET_V], scT[:, i % 2, b * P:(b + 1) * P],
                                                  rv[:, b, h * RET_V:(h + 1) * RET_V], start=(b == 0), stop=(b == t))
                        mm.then_inc(values, 1)

            @block.scalar
            def _(act):
                for i in range(N):
                    nk = (jobs[i][1] + 1) * P
                    act.wait_ge(turned, i + 1)
                    if i >= 2:
                        act.wait_ge(values, i - 1)
                    nc.scalar.activation(scT[:, i % 2, 0:nk], ps[:, 2 + i % 2, 0:nk], ACT.Copy).then_inc(back, 1)

            @block.vector
            def _(dve):
                for j in range(N + 2):
                    if j < N:
                        h, t = jobs[j]
                        nk = (t + 1) * P
                        dve.wait_ge(scores, j + 1)
                        if j >= 2:
                            dve.wait_ge(turned, j - 1)
                        nc.vector.tensor_tensor(sc[:, j % 2, 0:nk], ps[:, j % 2, 0:nk], decay[:, t, h * SEQ:h * SEQ + nk], ALU.mult).then_inc(decayed, 1)
                    if j >= 2:
                        h, t = jobs[j - 2]
                        dve.wait_ge(values, j - 1)
                        nc.vector.tensor_copy(out(t, h), ps[:, 4 + j % 2, 0:RET_V]).then_inc(out_done, 1)


def block2(core, l):
    nc, a, ps = core.nc, core.a, core.ps
    first, col, x = core.first, core.col, core.x
    T = f"b{l}_"
    with ExitStack() as c:
        sb = lambda name, shape, c=c: c.enter_context(nc.sbuf_tensor(T + name, shape, F32))
        gates = sb("gates", [P, LT, 3 * D])
        rg = sb("rg", [P, LT, 512])
        oa = sb("oa", [P, LT, 1536])
        with ExitStack() as c2:
            sb2 = lambda name, shape, c=c2: c.enter_context(nc.sbuf_tensor(T + name, shape, F32))
            lr = sb2("low", [P, LT, IN2_FIRST])
            moba = sb2("moba", [P, LT, 1536])
            rqk = sb2("rqk", [P, LT, 512])
            rv = sb2("rv", [P, LT, 512])
            tabs = x[:, LT:NT, 768:992]
            tmp = core.hT[:, 0:2, :]
            st = sb2("st", [P, 3, 4])
            c_in = ExitStack()
            h = Split(nc, c_in, T + "h", [P, KC, SEQ])
            weights = SplitWeights(core, c_in, T + "i", first[f"in{l}a"], 13)
            normed(core, T + "n_", range(LT), lambda k, s: col(f"an{l}", k), into=h, weights=weights)
            toks = lambda w: [("tokens", t, 0, w) for t in range(LT)]

            def copies(dst_of):
                return (lambda act, n, wi, g, src, w: nc.scalar.activation(dst_of(wi, g[1]), src, ACT.Copy),
                        lambda dve, n, wi, g, src: nc.vector.tensor_copy(dst_of(wi, g[1]), src))

            def where(wi, t):
                if wi == 0:
                    return lr[:, t, :]
                if wi <= 3:
                    return moba[:, t, (wi - 1) * BANK:wi * BANK]
                return rqk[:, t, :] if wi == 4 else rv[:, t, :]
            project_split(core, T + "p_", weights, 0, h, [toks(IN2_FIRST)] + [toks(BANK)] * 5, lambda n: "ad"[n % 2], *copies(where))
            project_split(core, T + "rg_", weights, 12, h, [toks(BANK)], lambda n: "a",
                    lambda act, n, wi, g, src, w: nc.scalar.activation(rg[:, g[1], :], src, ACT.Silu), None)
            with ExitStack() as c3:
                sb3 = lambda name, shape: sb2(name, shape, c3)
                uq = x[:, LT:NT, 0:768]
                tabs_in = core.expect_tables(5)
                decay = core.ga[:, 0:LT, :]
                causal = core.ga[:, 2, 0:LT * SEQ].rearrange("p (t n) -> p t n", t=LT)
                meaned, rooted = core.sem(T + "meaned"), core.sem(T + "rooted")
                o_moba, o_ret = 64, 96

                def root(act):
                    act.wait_ge(meaned, 1)
                    nc.scalar.activation(st[:, 1, :], st[:, 1, :], ACT.Sqrt).then_inc(rooted, 1)

                def norm_and_rotate(block):
                    @block.gpsimd
                    def _(pool):
                        at = 0
                        for name, w in (("rope_mla", 64), ("rope_moba", 32), ("rope_ret", 128)):
                            pool.dma_start(tabs[:, :, at:at + w], a[name].rearrange("(t p) n -> p t n", p=P)).then_inc(core.tables_in, 16)
                            at += w
                        pool.dma_start(causal, a["causal"].rearrange("(t p) n -> p t n", p=P)).then_inc(core.tables_in, 16)
                        pool.dma_start(decay, a["ret_decay"].rearrange("(t p) n -> p t n", p=P)).then_inc(core.tables_in, 16)

                    @block.vector
                    def _(dve):
                        link = core.dve_chain
                        parts = [(t, i, lo, w) for t in range(LT) for i, (lo, w) in enumerate(((0, MLA_Q), (MLA_Q, MLA_KV)))]
                        for t, i, lo, w in parts:
                            link(dve, nc.vector.tensor_tensor_reduce(tmp[:, 0, 0:w], lr[:, t, lo:lo + w], lr[:, t, lo:lo + w], 1.0 / w, EPS,
                                                                     ALU.mult, ALU.add, st[:, 1, 2 * t + i:2 * t + i + 1]))
                        nc.vector.tensor_copy(st[:, 0, 0:1], st[:, 1, 0:1]).then_inc(meaned, 1)
                        dve.wait_ge(core.tables_in, tabs_in)
                        for t in range(LT):
                            rope(core, dve, moba[:, t, 0:1024].rearrange("p (h d) -> p h d", h=16)[:, :, 0:16],
                                 tabs[:, t, o_moba:o_moba + 32], tmp, 16, 16)
                            rope(core, dve, rqk[:, t, :].rearrange("p (h d) -> p h d", h=8), tabs[:, t, o_ret:o_ret + 128], tmp, 8, 64)
                            rope(core, dve, lr[:, t, 384:416].unsqueeze(1), tabs[:, t, 0:64], tmp, 1, 32)
                        dve.wait_ge(rooted, 1)
                        link(dve, nc.vector.reciprocal(st[:, 2, :], st[:, 1, :]))
                        for t, i, lo, w in parts:
                            link(dve, nc.vector.tensor_scalar(lr[:, t, lo:lo + w], lr[:, t, lo:lo + w], st[:, 2, 2 * t + i:2 * t + i + 1], None, ALU.mult))
                project_split(core, T + "g_", weights, 14, h, [toks(BANK)] * 6, lambda n: "a",
                        lambda act, n, wi, g, src, w: nc.scalar.activation(gates[:, g[1], wi * BANK:(wi + 1) * BANK], src, ACT.Sigmoid), None,
                        before=norm_and_rotate, on_gpsimd=4, act_between=(0, root))
                c_in.close()
                ukv = sb2("ukv", [P, LT, 1024])
                mT = sb2("mT", [96, 2 * 8, SEQ])
                rT = sb2("rT", [64, 8, SEQ])
                lowT = sb3("lowT", [P, 3, SEQ])
                kk = sb3("kk", [P, LT, 8, 96])
                bT = core.hT[0:64].rearrange("p k t -> p (k t)").rearrange("p (h t) -> p h t", h=16)
                turn(core, T + "lt_", [([lr[:, t, k * P:(k + 1) * P] for t in range(LT)], lowT[:, k, :],
                                        col(f"qn{l}", k) if k < 2 else col(f"kvn{l}")) for k in range(3)])
                up_done, up_act, up_dve = core.sem(T + "up_done"), core.sem(T + "up_act"), core.sem(T + "up_dve")
                wi = first[f"up{l}"]
                with core.phase() as block:
                    @block.sync
                    def _(sp):
                        core.load_ahead(sp, wi, up_done, [8])

                    @block.tensor
                    def _(pe):
                        wq, wkv = core.weight(pe, wi, 0), core.weight(pe, wi, 1)
                        for t in range(LT):
                            for j in range(2):
                                for k in range(2):
                                    mm = nc.tensor.matmul(ps[:, 2 * t + j, 0:384], lowT[:, k, t * P:(t + 1) * P],
                                                          wq[:, k, j * 384:(j + 1) * 384], start=(k == 0), stop=(k == 1))
                                mm.then_inc(up_done, 1)
                        for t in range(LT):
                            for j in range(2):
                                nc.tensor.matmul(ps[:, 4 + 2 * t + j, :], lowT[:, 2, t * P:(t + 1) * P],
                                                 wkv[:, 0, j * BANK:(j + 1) * BANK], start=True, stop=True).then_inc(up_done, 1)

                    @block.scalar
                    def _(act):
                        for t in range(LT):
                            for j in range(2):
                                act.wait_ge(up_done, 4 + 2 * t + j + 1)
                                last = nc.scalar.activation(ukv[:, t, j * BANK:(j + 1) * BANK], ps[:, 4 + 2 * t + j, :], ACT.Copy)
                            core.act_chain(act, last)
                            nc.scalar.activation(kk[:, t, :, 0:64], ukv[:, t, :].rearrange("p (h d) -> p h d", h=8)[:, :, 0:64], ACT.Copy).then_inc(up_act, 1)
                            core.act_chain(act, nc.scalar.activation(kk[:, t, :, 64:96], lr[:, t, 384:416].unsqueeze(1).broadcast_to([P, 8, 32]), ACT.Copy))

                    @block.vector
                    def _(dve):
                        for t in range(LT):
                            for j in range(2):
                                dve.wait_ge(up_done, 2 * t + j + 1)
                                last = nc.vector.tensor_copy(uq[:, t, j * 384:(j + 1) * 384], ps[:, 2 * t + j, 0:384])
                            core.dve_chain(dve, last)
                            rope(core, dve, uq[:, t, :].rearrange("p (h d) -> p h d", h=8)[:, :, 64:96], tabs[:, t, 0:64], tmp, 8, 32)
                flat = lambda z: z.rearrange("p h t -> p (h t)")
                blocks = []
                for h in range(0, 8, 2):
                    blocks.append(([uq[:, t, g * 96:(g + 1) * 96] for g in (h, h + 1) for t in range(LT)], flat(mT[:, h:h + 2, :]), None))
                    blocks.append(([kk[:, t, g, :] for g in (h, h + 1) for t in range(LT)], flat(mT[:, 8 + h:10 + h, :]), None))
                for h in range(0, 16, 2):
                    blocks.append(([moba[:, t, g * 64:(g + 1) * 64] for g in (h, h + 1) for t in range(LT)], flat(bT[:, h:h + 2, :]), None))
                for h in range(0, 8, 2):
                    blocks.append(([rqk[:, t, g * 64:(g + 1) * 64] for g in (h, h + 1) for t in range(LT)], flat(rT[:, h:h + 2, :]), None))
                turn(core, T + "t_", blocks)
            spare = x[:, LT:NT, :].rearrange("p t d -> p (t d)")
            gn = spare[:, 0:1024].rearrange("p (i n) -> p i n", i=2)
            tables_in = core.tables_n
            gn_in = core.expect_tables(2)

            def fetch_gains(block):
                @block.gpsimd
                def _(pool):
                    pool.dma_start(gn[:, 0, :], row_bcast(a, f"gn_w{l}")).then_inc(core.tables_in, 16)
                    pool.dma_start(gn[:, 1, :], row_bcast(a, f"gn_b{l}")).then_inc(core.tables_in, 16)

                @block.vector
                def _(dve):
                    dve.wait_ge(core.tables_in, tables_in)
            for name, qk, off, vsrc, scale in (("ma_", mT, 0, lambda b, h: ukv[:, b, h * 128 + 64:h * 128 + 128], 96 ** -0.5),
                                               ("mo_", bT, 512, lambda b, h: moba[:, b, 1024 + h * 64:1088 + h * 64], 64 ** -0.5)):
                jobs = [dict(q=qk[:, h, t * P:(t + 1) * P], k=qk[:, 8 + h, 0:(t + 1) * P], mask=causal[:, t, 0:(t + 1) * P],
                             feat=False, v=[vsrc(b, h) for b in range(t + 1)], out=oa[:, t, off + h * 64:off + (h + 1) * 64])
                        for h in range(8) for t in range(LT)]
                softmax_attention(core, T + name, jobs, scale, before=fetch_gains if name == "ma_" else None)
            retention(core, T + "re_", rT, rv, decay, lambda t, h: oa[:, t, 1024 + h * P:1024 + (h + 1) * P])
            st = sb2("gst", [P, 4, LT * RET_H])
            sq = sb2("gsq", [P, 512])
            meaned, rooted = core.sem(T + "gn_meaned"), core.sem(T + "gn_rooted")
            with core.phase() as block:
                @block.scalar
                def _(act):
                    act.wait_ge(meaned, 1)
                    nc.scalar.activation(st[:, 2, :], st[:, 2, :], ACT.Sqrt).then_inc(rooted, 1)

                @block.vector
                def _(dve):
                    link = core.dve_chain
                    heads = lambda t: oa[:, t, 1024:1536].rearrange("p (h d) -> p h d", h=RET_H)
                    dve.wait_ge(core.tables_in, gn_in)
                    s4 = lambda n, t: st[:, n, t * RET_H:(t + 1) * RET_H]
                    wide = lambda z: z.unsqueeze(2).broadcast_to([P, RET_H, RET_V])
                    for t in range(LT):
                        link(dve, nc.vector.tensor_reduce(s4(0, t), heads(t), AX.X, ALU.add))
                        link(dve, nc.vector.tensor_scalar(s4(1, t), s4(0, t), 1.0 / RET_V, None, ALU.mult))
                        link(dve, nc.vector.tensor_tensor(heads(t), heads(t), wide(s4(1, t)), ALU.subtract))
                        link(dve, nc.vector.tensor_tensor(sq[:], oa[:, t, 1024:1536], oa[:, t, 1024:1536], ALU.mult))
                        link(dve, nc.vector.tensor_reduce(s4(0, t), sq[:].rearrange("p (h d) -> p h d", h=RET_H), AX.X, ALU.add))
                    nc.vector.tensor_scalar(st[:, 2, :], st[:, 0, :], 1.0 / RET_V, GN_EPS, ALU.mult, ALU.add).then_inc(meaned, 1)
                    dve.wait_ge(rooted, 1)
                    link(dve, nc.vector.reciprocal(st[:, 3, :], st[:, 2, :]))
                    for t in range(LT):
                        o = oa[:, t, 1024:1536]
                        link(dve, nc.vector.tensor_tensor(heads(t), heads(t), wide(s4(3, t)), ALU.mult))
                        link(dve, nc.vector.tensor_tensor(o, o, gn[:, 0, :], ALU.mult))
                        link(dve, nc.vector.tensor_tensor(o, o, gn[:, 1, :], ALU.add))
                        link(dve, nc.vector.tensor_tensor(o, o, rg[:, t, :], ALU.mult))
        oT = Split(nc, c, T + "oT", [P, 12, SEQ])
        mergedT = Split(nc, c, T + "mergedT", [P, KC, SEQ])
        weights = SplitWeights(core, c, T + "b", first[f"b_mla{l}"], 5)
        merged = x[:, LT:NT, :]
        part = core.hT[:, 0:2, :]
        turn_split(core, T + "ot_", [([oa[:, t, k * P:(k + 1) * P] for k in (2 * q, 2 * q + 1) for t in range(LT)],
                                      np.s_[:, 2 * q:2 * q + 2, :]) for q in range(6)], oT, weights)
        b_done, b_read, b_used = (core.sem(T + n) for n in ("branch_done", "branch_read", "branch_half_used"))
        with core.phase() as block:
            @block.sync
            def _(sp):
                weights.load_ahead(sp, 0, 6)

            @block.tensor
            def _(pe):
                for u in range(6):
                    w = weights.parts(pe, u)
                    for q in range(4):
                        t, j, n = q // 2, q % 2, 4 * (u // 2) + q
                        if n >= 8 and u % 2 == 0:
                            pe.wait_ge(b_read, n - 7)
                        for k in range(2):
                            mm = split_matmul(nc, ps[:, n % 8, :], oT.parts(np.s_[:, 2 * u + k, t * P:(t + 1) * P]),
                                              [z[:, k, j * BANK:(j + 1) * BANK] for z in w], u % 2 == 0 and k == 0, u % 2 == 1 and k == 1)
                        if u % 2:
                            mm.then_inc(b_done, 1)
                    if u % 2 == 0:
                        mm.then_inc(b_used, 1)

            @block.scalar
            def _(act):
                weights.take_lead(act, weights.B - 1)
                for u in range(5):
                    if u % 2:
                        act.wait_ge(b_done, 4 * (u // 2 + 1))
                    else:
                        act.wait_ge(b_used, u // 2 + 1)
                    weights.take_lead(act, weights.B + u)

            @block.vector
            def _(dve):
                weights.take_rest(dve, weights.B - 1)
                for b in range(3):
                    weights.take_rest(dve, weights.B + 2 * b)
                    if b < 2:
                        weights.take_rest(dve, weights.B + 2 * b + 1)
                    for n in range(4 * b, 4 * b + 4):
                        t, j = n // 2 % 2, n % 2
                        dve.wait_ge(b_done, n + 1)
                        g = gates[:, t, b * D + j * BANK:b * D + (j + 1) * BANK]
                        m = merged[:, t, j * BANK:(j + 1) * BANK]
                        if b == 0:
                            nc.vector.tensor_tensor(m, ps[:, n % 8, :], g, ALU.mult).then_inc(b_read, 1)
                        else:
                            nc.vector.tensor_tensor(part[:, n % 2, :], ps[:, n % 8, :], g, ALU.mult).then_inc(b_read, 1)
                            dve.wait_ge(b_read, n + 1)
                            core.dve_chain(dve, nc.vector.tensor_tensor(m, m, part[:, n % 2, :], ALU.add))
        turn_split(core, T + "mt_", [([merged[:, t, k * P:(k + 1) * P] for k in (2 * q, 2 * q + 1) for t in range(LT)],
                                      np.s_[:, 2 * q:2 * q + 2, :]) for q in range(4)], mergedT)
        down_split(core, T + "wo_", weights, 6, mergedT, LT, 2)
    add_banks(core, T + "r1_")
    with ExitStack() as c:
        upT = Split(nc, c, T + "upT", [P, D_FF // P, SEQ])
        weights = SplitWeights(core, c, T + "m", first[f"mup{l}"], 16)
        with ExitStack() as c2:
            h = Split(nc, c2, T + "h2", [P, KC, SEQ])
            normed(core, T + "n2_", range(LT), lambda k, s: col(f"mn{l}", k), into=h, weights=weights)
            way = core.hT[:, 0:4, 0:SEQ]

            def relu_squared(act, n, wi, g, src, dve_done):
                if n >= 4:
                    dve_done(n - 4)
                core.act_chain(act, nc.scalar.activation(way[:, n % 4, :], src, ACT.Relu))
                return nc.scalar.activation(way[:, n % 4, :], way[:, n % 4, :], ACT.Square)

            def split_up(dve, n, wi, g, src):
                at = np.s_[:, n, :]
                core.dve_chain(dve, upT.take_lead(dve, at, way[:, n % 4, :]))
                return upT.take_rest(dve, at, way[:, n % 4, :])
            project_split(core, T + "mu_", weights, 0, h, [[("features", m, 0, SEQ) for m in range(4)]] * 8, lambda n: "ad",
                          relu_squared, split_up)
        down_split(core, T + "md_", weights, 16, upT, LT, 8)
    add_banks(core, T + "r2_")


def add_banks(core, tag):
    nc = core.nc
    with core.phase() as block:
        @block.vector
        def _(dve):
            for t in range(LT):
                for j in range(2):
                    xs = core.x[:, t, j * BANK:(j + 1) * BANK]
                    last = nc.vector.tensor_tensor(xs, xs, core.ps[:, 2 * t + j, :], ALU.add)
            core.dve_chain(dve, last)


def final(core, out):
    nc, a, x = core.nc, core.a, core.x
    with ExitStack() as c:
        sq = c.enter_context(nc.sbuf_tensor("f_sq", [P, D], F32))
        gain = c.enter_context(nc.sbuf_tensor("f_gain", [P, D], F32))
        st = c.enter_context(nc.sbuf_tensor("f_st", [P, 3, LT], F32))
        gain_in = core.expect_tables(1)
        meaned, rooted, ready = (core.sem("f_" + n) for n in ("meaned", "rooted", "ready"))
        stored = core.stored
        with core.phase() as block:
            @block.gpsimd
            def _(pool):
                pool.dma_start(gain[:], row_bcast(a, "final")).then_inc(core.tables_in, 16)

            @block.scalar
            def _(act):
                act.wait_ge(meaned, 1)
                nc.scalar.activation(st[:, 1, :], st[:, 1, :], ACT.Sqrt).then_inc(rooted, 1)

            @block.vector
            def _(dve):
                link = core.dve_chain
                for t in range(LT):
                    link(dve, nc.vector.tensor_tensor_reduce(sq[:], x[:, t, :], x[:, t, :], 1.0 / D, EPS, ALU.mult, ALU.add, st[:, 1, t:t + 1]))
                nc.vector.tensor_copy(st[:, 0, 0:1], st[:, 1, 0:1]).then_inc(meaned, 1)
                dve.wait_ge(rooted, 1)
                link(dve, nc.vector.reciprocal(st[:, 2, :], st[:, 1, :]))
                dve.wait_ge(core.tables_in, gain_in)
                for t in range(LT):
                    nc.vector.scalar_tensor_tensor(out=x[:, t, :], in0=x[:, t, :], scalar=st[:, 2, t:t + 1], in1=gain[:],
                                                   op0=ALU.mult, op1=ALU.mult).then_inc(ready, 1)

            @block.sync
            def _(sp):
                for t in range(LT):
                    sp.wait_ge(ready, t + 1)
                    sp.dma_start(out[0, t * P:(t + 1) * P, :], x[:, t, :]).then_inc(stored, 16)
                sp.wait_ge(stored, 16 * LT)


INS = ['x', 'c', 'ctx', 'c_ctx', 'w_mod', 'b_mod', 'g_pre', 'g_post', 'e_w_in', 'e_conv_w', 'e_conv_b', 'e_filt_w1',
       'e_filt_b1', 'e_filt_freq', 'e_filt_w2', 'e_filt_b2', 'e_filt_w3', 'e_hy_bias', 'e_q_norm', 'e_k_norm',
       'e_w_out', 'o_w_in', 'o_conv_w', 'o_conv_b', 'o_gate_b', 'o_head_norm', 'o_w_out', 'attn_norm_2', 'w_in_2',
       'mla_q_norm_2', 'mla_kv_norm_2', 'mla_w_q_up_2', 'mla_w_kv_up_2', 'ret_gn_w_2', 'ret_gn_b_2',
       'w_branch_mla_2', 'w_branch_moba_2', 'w_branch_ret_2', 'w_out_2', 'mlp_norm_2', 'w_mlp_up_2',
       'w_mlp_down_2', 'final_norm_2']
DIRECT = ['x', 'ctx', 'w_mod', 'e_w_in', 'e_filt_w1', 'e_filt_w2', 'e_filt_w3', 'e_w_out', 'o_w_in', 'o_w_out',
          'w_in_2', 'mla_w_q_up_2', 'mla_w_kv_up_2', 'w_branch_mla_2', 'w_branch_moba_2', 'w_branch_ret_2', 'w_out_2',
          'w_mlp_up_2', 'w_mlp_down_2']


def feature_columns(p):
    out = np.zeros((P, NCOL), np.float32)

    def put(name, v):
        v = np.asarray(v).reshape(-1, P)
        at = COL_AT[name]
        out[:, at:at + v.shape[0]] = v.T

    def put_short(name, v, at_partition=0):
        out[at_partition:at_partition + len(v), COL_AT[name]] = v

    put("c", p["c"])
    put("c_ctx", p["c_ctx"])
    for l in range(DEPTH):
        put(f"b_sh{l}", p["b_mod"][l, 0:D])
        put(f"b_sc{l}", p["b_mod"][l, D:2 * D])
        put(f"g_pre{l}", p["g_pre"][l])
        put(f"an{l}", p["attn_norm_2"][l])
        put(f"mn{l}", p["mlp_norm_2"][l])
        put(f"qn{l}", p["mla_q_norm_2"][l])
        put(f"kvn{l}", p["mla_kv_norm_2"][l])
    for i in range(3):
        put(f"e_cw{i}", p["e_conv_w"][0, i])
        put(f"o_cw{i}", p["o_conv_w"][0, i])
    put("e_cb", p["e_conv_b"][0])
    put("o_cb", p["o_conv_b"][0])
    put("hy_bias", p["e_hy_bias"][0])
    put_short("f_b1", p["e_filt_b1"][0])
    put_short("f_b2", p["e_filt_b2"][0])
    put_short("f_fr", p["e_filt_freq"][0])
    gb = p["o_gate_b"][0]
    put_short("gb_i", gb[0:8])
    put_short("gb_f", gb[8:16])
    put_short("gb_i", gb[16:24], 32)
    put_short("gb_f", gb[24:32], 32)
    return out


def spread_rows(p):
    parts = {"b_ga0": p["b_mod"][0, 2 * D:], "b_ga1": p["b_mod"][1, 2 * D:], "g_post0": p["g_post"][0],
             "g_post1": p["g_post"][1], "q_norm": p["e_q_norm"][0], "k_norm": p["e_k_norm"][0],
             "head_norm": p["o_head_norm"][0], "gn_w0": p["ret_gn_w_2"][0], "gn_b0": p["ret_gn_b_2"][0],
             "gn_w1": p["ret_gn_w_2"][1], "gn_b1": p["ret_gn_b_2"][1], "final": p["final_norm_2"]}
    return np.concatenate([np.asarray(parts[k]).reshape(-1) for k in ROW_AT]).astype(np.float32)


def tables():
    out = {"ident": np.eye(P), "pick": np.kron(np.eye(2), np.ones((1, P)))}
    n = SEQ
    t = np.arange(2 * n)[:, None]
    f = np.arange(n)[None, :]
    cos = np.cos(2 * np.pi * ((t * f) % (2 * n)) / (2 * n))
    sin = -np.sin(2 * np.pi * ((t * f) % (2 * n)) / (2 * n))
    sin[:, 0] = (-1.0) ** t[:, 0]
    full = np.concatenate([cos, sin], 1)
    back_taps = full[(2 * n - np.arange(n)) % (2 * n)].copy()
    back_taps[0] = 0.0
    out["dft"] = np.concatenate([full[:n], back_taps], 0)
    inv = full[:n].T * (2.0 / (2 * n))
    inv[0] *= 0.5
    inv[n] *= 0.5
    out["idft"] = inv
    out["tap_ones"] = np.concatenate([np.ones(n), [0.0], np.ones(n - 1)]).reshape(4, P).T
    bands = np.linspace(1e-4, 15, 16, dtype=np.float32)
    ang = np.float32(2.0 * math.pi / n) * np.arange(n, dtype=np.float32)[:, None] * bands
    tt = np.linspace(0.0, 1.0, n, dtype=np.float32)[:, None]
    out["z_t"] = np.concatenate([tt, np.cos(ang), -np.sin(ang)], 1).T
    deltas = np.linspace(math.log(1e-2) / 1.5, math.log(1e-2) / 0.3, HY, dtype=np.float32)
    out["decay"] = np.exp(-tt * np.abs(deltas))

    def rot(pos, dim, inv_freq, reps):
        a = pos.astype(np.float32)[:, None] * inv_freq.astype(np.float32)
        return (np.tile(np.concatenate([np.cos(a), np.cos(a)], 1), (1, reps)),
                np.tile(np.concatenate([-np.sin(a), np.sin(a)], 1), (1, reps)))

    nf = DH // 4
    inv_freq = 10000.0 ** (-np.arange(nf) / nf)
    pos = np.arange(SEQ)
    c0, s0 = rot(pos // 64, 64, inv_freq, 1)
    c1, s1 = rot(pos % 64, 64, inv_freq, 1)
    out["rope_e"] = np.concatenate([c0, c1, s0, s1], 1)
    for name, dim, theta, reps in (("rope_mla", 32, 500000.0, 1), ("rope_moba", 16, 500000.0, 1), ("rope_ret", 64, 10000.0, 1)):
        cc, ss = rot(pos, dim, 1.0 / theta ** (np.arange(0, dim, 2) / dim), reps)
        out[name] = np.concatenate([cc, ss], 1)
    q, k = np.arange(SEQ)[:, None], np.arange(SEQ)[None, :]
    out["causal"] = np.where(k <= q, 0.0, NEG)
    out["anti"] = np.where(k >= q, 0.0, NEG)
    lg = np.log(1.0 - 2.0 ** (-5.0 - np.arange(RET_H)))
    out["ret_decay"] = np.concatenate([np.where(k <= q, np.exp(g * np.maximum(q - k, 0)), 0.0) for g in lg], 1) * RET_QK ** -0.5
    return {k2: np.ascontiguousarray(v, np.float32) for k2, v in out.items()}


def make(nc, arrays_shapes):
    a = {}
    for name, shape in arrays_shapes.items():
        a[name] = nc.dram_tensor(f"in_{name}", shape, F32, kind="ExternalInput").ap()
    out = nc.dram_tensor("out_0", (1, SEQ, D), F32, kind="ExternalOutput").ap()
    program(nc, a, out)
    return out


def host_arrays(p):
    arrays = {name: np.ascontiguousarray(p[name]) for name in DIRECT}
    arrays["cols"] = feature_columns(p)
    arrays["rows"] = spread_rows(p)
    g = p["o_w_in"][0][:, OD_G:].reshape(KC, P, 2, 2, 8)
    gate_w = np.zeros((P, KC, 2, 40), np.float32)
    gate_w[:, :, :, 0:8] = g[:, :, 0].transpose(1, 0, 2, 3)
    gate_w[:, :, :, 32:40] = g[:, :, 1].transpose(1, 0, 2, 3)
    arrays["gate_w"] = gate_w.reshape(P, KC * 80)
    arrays.update(tables())
    return arrays


def kernel(**inputs):
    import concourse.bacc as bacc
    from concourse.bass_utils import run_bass_kernel_spmd as run

    p = {k: np.asarray(v) for k, v in inputs.items()}
    arrays = host_arrays(p)
    nc = bacc.Bacc("TRN2", target_bir_lowering=False, num_devices=1)
    make(nc, {k: v.shape for k, v in arrays.items()})
    r = run(nc, [{f"in_{k}": v for k, v in arrays.items()}], core_ids=[0])
    return r.results[0]["out_0"]
```
